# Optimizing a Trainium2 kernel written in Bass

```python
import math
import jax, jax.numpy as jnp
from jax import lax
import numpy as np

D_MODEL = 2048
BATCH = 1
SEQ = 256
DEPTH = 1

NUM_MIXERS = 2
N_GLA_LAYERS = (DEPTH + NUM_MIXERS - 1) // NUM_MIXERS
N_GDN_LAYERS = DEPTH // NUM_MIXERS

EPS = 1e-6
CHUNK = 64
PLE_DIM = 256
D_FF = ((8 * D_MODEL + 3 * 256 - 1) // (3 * 256)) * 256

GLA_HEADS = 4
GLA_DK = D_MODEL // (2 * GLA_HEADS)
GLA_DV = D_MODEL // GLA_HEADS
GLA_KEY_DIM = GLA_HEADS * GLA_DK
GLA_VAL_DIM = GLA_HEADS * GLA_DV
GLA_GATE_RANK = 16
GLA_GATE_NORM = 16.0
GLA_PROJ = 2 * GLA_KEY_DIM + 2 * GLA_VAL_DIM + 2 * GLA_GATE_RANK

GDN_QK_HEADS = D_MODEL // 128
GDN_V_HEADS = 2 * GDN_QK_HEADS
GDN_DK = 128
GDN_DV = 128
GDN_KEY_DIM = GDN_QK_HEADS * GDN_DK
GDN_VAL_DIM = GDN_V_HEADS * GDN_DV
GDN_CONV_DIM = 2 * GDN_KEY_DIM + GDN_VAL_DIM
CONV_W = 5
GDN_PROJ = GDN_CONV_DIM + GDN_VAL_DIM + 4 * GDN_V_HEADS


def rmsnorm(x, w):
    xf = x.astype(jnp.float32)
    y = xf * lax.rsqrt(jnp.mean(xf * xf, axis=-1, keepdims=True) + EPS)
    return (y * w.astype(jnp.float32)).astype(x.dtype)

def l2norm(x):
    xf = x.astype(jnp.float32)
    return xf * lax.rsqrt(jnp.sum(xf * xf, axis=-1, keepdims=True) + EPS)

def to_heads(x, n):
    b, t, _ = x.shape
    return x.reshape(b, t, n, -1).transpose(0, 2, 1, 3)

def from_heads(x):
    b, n, t, d = x.shape
    return x.transpose(0, 2, 1, 3).reshape(b, t, n * d)

def flip_t(x):
    return jnp.flip(x, axis=2)

def gla_chunked(q, k, v, g):
    b, h, t, dk = q.shape
    dv = v.shape[-1]
    nc = t // CHUNK
    q, k, g = (a.reshape(b, h, nc, CHUNK, dk) for a in (q, k, g))
    v = v.reshape(b, h, nc, CHUNK, dv)
    cum = jnp.cumsum(g, axis=-2)
    last = cum[..., -1:, :]
    q_dec = q * jnp.exp(cum)
    k_dec = k * jnp.exp(last - cum)
    chunk_decay = jnp.exp(last[..., 0, :])
    lower = jnp.tril(jnp.ones((CHUNK, CHUNK), dtype=bool))
    xs = tuple(jnp.moveaxis(a, 2, 0) for a in (q, k, v, cum, q_dec, k_dec, chunk_decay))

    def step(S, inp):
        q_i, k_i, v_i, c_i, qd_i, kd_i, cd_i = inp
        pair = jnp.where(lower[..., None],
                         jnp.exp(jnp.minimum(c_i[..., :, None, :] - c_i[..., None, :, :], 0.0)), 0.0)
        a_i = jnp.einsum('bhid,bhjd,bhijd->bhij', q_i, k_i, pair)
        o_i = jnp.einsum('bhij,bhjv->bhiv', a_i, v_i) + jnp.einsum('bhid,bhdv->bhiv', qd_i, S)
        S = S * cd_i[..., None] + jnp.einsum('bhcd,bhcv->bhdv', kd_i, v_i)
        return S, o_i

    S0 = jnp.zeros((b, h, dk, dv), jnp.float32)
    _, o = lax.scan(step, S0, xs)
    return jnp.moveaxis(o, 0, 2).reshape(b, h, t, dv)

def gated_delta_chunked(q, k, v, g, beta):
    b, h, t, dk = q.shape
    dv = v.shape[-1]
    nc = t // CHUNK
    q = q.reshape(b, h, nc, CHUNK, dk)
    k = k.reshape(b, h, nc, CHUNK, dk)
    v = v.reshape(b, h, nc, CHUNK, dv)
    cum = jnp.cumsum(g.reshape(b, h, nc, CHUNK), axis=-1)
    beta = beta.reshape(b, h, nc, CHUNK, 1)
    idx = jnp.arange(CHUNK)
    lower = idx[:, None] >= idx[None, :]
    strict = idx[:, None] > idx[None, :]
    decay = jnp.where(lower, jnp.exp(jnp.minimum(cum[..., :, None] - cum[..., None, :], 0.0)), 0.0)
    k_beta = k * beta
    tri = jnp.where(strict, jnp.einsum('bhnid,bhnjd->bhnij', k_beta, k) * decay, 0.0) \
        + jnp.eye(CHUNK, dtype=jnp.float32)
    rhs = jnp.concatenate([v * beta, k_beta * jnp.exp(cum)[..., None]], axis=-1)
    sol = lax.linalg.triangular_solve(tri, rhs, left_side=True, lower=True, unit_diagonal=True)
    u, w = sol[..., :dv], sol[..., dv:]
    attn = jnp.einsum('bhnid,bhnjd->bhnij', q, k) * decay
    last = cum[..., -1:]
    q_dec = q * jnp.exp(cum)[..., None]
    k_dec = k * jnp.exp(last - cum)[..., None]
    chunk_decay = jnp.exp(last)
    xs = tuple(jnp.moveaxis(a, 2, 0) for a in (u, w, attn, q_dec, k_dec, chunk_decay))

    def step(S, inp):
        u_i, w_i, a_i, qd_i, kd_i, cd_i = inp
        v_new = u_i - jnp.einsum('bhcd,bhdv->bhcv', w_i, S)
        o_i = jnp.einsum('bhcd,bhdv->bhcv', qd_i, S) + jnp.einsum('bhij,bhjv->bhiv', a_i, v_new)
        S = S * cd_i[..., None] + jnp.einsum('bhcd,bhcv->bhdv', kd_i, v_new)
        return S, o_i

    S0 = jnp.zeros((b, h, dk, dv), jnp.float32)
    _, o = lax.scan(step, S0, xs)
    return jnp.moveaxis(o, 0, 2).reshape(b, h, t, dv)

def centred_short_conv(x, w):
    c = x.shape[-1]
    return lax.conv_general_dilated(
        x, w[:, None, :].astype(x.dtype), window_strides=(1,),
        padding=[(CONV_W // 2, CONV_W // 2)],
        dimension_numbers=('NWC', 'WIO', 'NWC'), feature_group_count=c)

def gla_mixer(hn, w_in, w_gate_up, b_gate, out_norm, w_out):
    b, t, _ = hn.shape
    proj = jnp.einsum('btd,de->bte', hn, w_in)
    q, k, v, og, lr = jnp.split(
        proj, [GLA_KEY_DIM, 2 * GLA_KEY_DIM, 2 * GLA_KEY_DIM + GLA_VAL_DIM,
               2 * GLA_KEY_DIM + 2 * GLA_VAL_DIM], axis=-1)
    lr = lr.reshape(b, t, 2, GLA_GATE_RANK)
    gk = jnp.einsum('btzr,zrd->zbtd', lr, w_gate_up) + b_gate[:, None, None, :]
    logdec = jax.nn.log_sigmoid(gk.astype(jnp.float32)) / GLA_GATE_NORM
    qh = to_heads(q, GLA_HEADS).astype(jnp.float32) * (GLA_DK ** -0.5)
    kh = to_heads(k, GLA_HEADS).astype(jnp.float32)
    vh = to_heads(v, GLA_HEADS).astype(jnp.float32)
    g_fwd = to_heads(logdec[0], GLA_HEADS)
    g_bwd = to_heads(logdec[1], GLA_HEADS)
    o = gla_chunked(qh, kh, vh, g_fwd) \
        + flip_t(gla_chunked(flip_t(qh), flip_t(kh), flip_t(vh), flip_t(g_bwd)))
    o = rmsnorm(o, out_norm)
    o = from_heads(o).astype(hn.dtype) * jax.nn.silu(og)
    return jnp.einsum('bte,ed->btd', o, w_out)

def gdn_mixer(hn, w_in, conv_w, a_log, dt_bias, out_norm, w_out):
    b, t, _ = hn.shape
    proj = jnp.einsum('btd,de->bte', hn, w_in)
    qkv, z, ba = jnp.split(proj, [GDN_CONV_DIM, GDN_CONV_DIM + GDN_VAL_DIM], axis=-1)
    qkv = jax.nn.silu(centred_short_conv(qkv, conv_w))
    q, k, v = jnp.split(qkv, [GDN_KEY_DIM, 2 * GDN_KEY_DIM], axis=-1)
    rep = GDN_V_HEADS // GDN_QK_HEADS
    qh = jnp.repeat(l2norm(to_heads(q, GDN_QK_HEADS)), rep, axis=1) * (GDN_DK ** -0.5)
    kh = jnp.repeat(l2norm(to_heads(k, GDN_QK_HEADS)), rep, axis=1)
    vh = to_heads(v, GDN_V_HEADS).astype(jnp.float32)
    ba = ba.reshape(b, t, 2, 2, GDN_V_HEADS).astype(jnp.float32)
    beta = jax.nn.sigmoid(ba[:, :, 0]).transpose(2, 0, 3, 1)
    a_in = ba[:, :, 1].transpose(2, 0, 3, 1)
    g = -jnp.exp(a_log.astype(jnp.float32))[:, None, :, None] \
        * jax.nn.softplus(a_in + dt_bias.astype(jnp.float32)[:, None, :, None])
    o = gated_delta_chunked(qh, kh, vh, g[0], beta[0]) \
        + flip_t(gated_delta_chunked(flip_t(qh), flip_t(kh), flip_t(vh), flip_t(g[1]), flip_t(beta[1])))
    o = rmsnorm(o, out_norm)
    o = from_heads(o).astype(hn.dtype) * jax.nn.silu(z)
    return jnp.einsum('bte,ed->btd', o, w_out)

def swiglu(hn, w_in, w_out):
    gate, up = jnp.split(jnp.einsum('btd,de->bte', hn, w_in), 2, axis=-1)
    return jnp.einsum('btf,fd->btd', jax.nn.silu(gate) * up, w_out)

def first_inputs(seed: int = 0) -> dict:
    key = jax.random.key(seed)
    ks = jax.random.split(key, 21)
    f32 = jnp.float32

    def nrm(k, shape, scale):
        return jax.random.normal(k, shape, f32) * scale

    def gain(k, shape):
        return 1.0 + 0.05 * jax.random.normal(k, shape, f32)

    x = nrm(ks[0], (BATCH, SEQ, D_MODEL), 1.0)
    p = nrm(ks[1], (DEPTH, BATCH, SEQ, PLE_DIM), 1.0)
    mixer_norm = gain(ks[2], (DEPTH, D_MODEL))
    gla_w_in = nrm(ks[3], (N_GLA_LAYERS, D_MODEL, GLA_PROJ), D_MODEL ** -0.5)
    gla_w_gate_up = nrm(ks[4], (N_GLA_LAYERS, 2, GLA_GATE_RANK, GLA_KEY_DIM), GLA_GATE_RANK ** -0.5)
    gla_b_gate = nrm(ks[5], (N_GLA_LAYERS, 2, GLA_KEY_DIM), 0.5)
    gla_out_norm = gain(ks[6], (N_GLA_LAYERS, GLA_DV))
    gla_w_out = nrm(ks[7], (N_GLA_LAYERS, GLA_VAL_DIM, D_MODEL), GLA_VAL_DIM ** -0.5)
    gdn_w_in = nrm(ks[8], (N_GDN_LAYERS, D_MODEL, GDN_PROJ), D_MODEL ** -0.5)
    gdn_conv = nrm(ks[9], (N_GDN_LAYERS, CONV_W, GDN_CONV_DIM), CONV_W ** -0.5)
    gdn_a_log = jnp.log(jax.random.uniform(ks[10], (N_GDN_LAYERS, 2, GDN_V_HEADS), f32, 1.0, 16.0))
    dt = jnp.exp(jax.random.uniform(ks[11], (N_GDN_LAYERS, 2, GDN_V_HEADS), f32,
                                    math.log(1e-3), math.log(1e-1)))
    gdn_dt_bias = dt + jnp.log(-jnp.expm1(-dt))
    gdn_out_norm = gain(ks[12], (N_GDN_LAYERS, GDN_DV))
    gdn_w_out = nrm(ks[13], (N_GDN_LAYERS, GDN_VAL_DIM, D_MODEL), GDN_VAL_DIM ** -0.5)
    ffn_norm = gain(ks[14], (DEPTH, D_MODEL))
    ffn_w_in = nrm(ks[15], (DEPTH, D_MODEL, 2 * D_FF), D_MODEL ** -0.5)
    ffn_w_out = nrm(ks[16], (DEPTH, D_FF, D_MODEL), D_FF ** -0.5)
    ple_norm = gain(ks[17], (DEPTH, D_MODEL))
    ple_w_gate = nrm(ks[18], (DEPTH, D_MODEL, D_MODEL), D_MODEL ** -0.5)
    ple_w_proj = nrm(ks[19], (DEPTH, PLE_DIM, D_MODEL), PLE_DIM ** -0.5)
    final_norm = gain(ks[20], (D_MODEL,))
    return {"x": x, "p": p, "mixer_norm": mixer_norm,
            "gla_w_in": gla_w_in, "gla_w_gate_up": gla_w_gate_up, "gla_b_gate": gla_b_gate,
            "gla_out_norm": gla_out_norm, "gla_w_out": gla_w_out,
            "gdn_w_in": gdn_w_in, "gdn_conv": gdn_conv, "gdn_a_log": gdn_a_log,
            "gdn_dt_bias": gdn_dt_bias, "gdn_out_norm": gdn_out_norm, "gdn_w_out": gdn_w_out,
            "ffn_norm": ffn_norm, "ffn_w_in": ffn_w_in, "ffn_w_out": ffn_w_out,
            "ple_norm": ple_norm, "ple_w_gate": ple_w_gate, "ple_w_proj": ple_w_proj,
            "final_norm": final_norm}

def first_block(x, p, mixer_norm, gla_w_in, gla_w_gate_up, gla_b_gate, gla_out_norm, gla_w_out,
              gdn_w_in, gdn_conv, gdn_a_log, gdn_dt_bias, gdn_out_norm, gdn_w_out,
              ffn_norm, ffn_w_in, ffn_w_out, ple_norm, ple_w_gate, ple_w_proj, final_norm):
    h = x
    for i in range(DEPTH):
        j = i // NUM_MIXERS
        hn = rmsnorm(h, mixer_norm[i])
        if i % NUM_MIXERS == 0:
            mix = gla_mixer(hn, gla_w_in[j], gla_w_gate_up[j], gla_b_gate[j],
                            gla_out_norm[j], gla_w_out[j])
        else:
            mix = gdn_mixer(hn, gdn_w_in[j], gdn_conv[j], gdn_a_log[j], gdn_dt_bias[j],
                            gdn_out_norm[j], gdn_w_out[j])
        h = h + mix
        h = h + swiglu(rmsnorm(h, ffn_norm[i]), ffn_w_in[i], ffn_w_out[i])
        gate = jax.nn.sigmoid(jnp.einsum('btd,de->bte', rmsnorm(h, ple_norm[i]), ple_w_gate[i]))
        h = h + gate * jnp.einsum('btk,kd->btd', p[i], ple_w_proj[i])
    return rmsnorm(h, final_norm)


HEAD_DIM = 64
A_HEADS = 8
A_WIDTH = A_HEADS * HEAD_DIM
CHUNK_2 = 128
B_WIDTH = 768
CONV_WIDTH = 3
DILATION_PATTERNS = ((128, 1), (512, 4), (2048, 16))
C_HEADS_PER_PATTERN = 4
C_HEADS = C_HEADS_PER_PATTERN * len(DILATION_PATTERNS)
C_WIDTH = C_HEADS * HEAD_DIM
D_MIX = A_WIDTH + B_WIDTH + C_WIDTH
PROJ_SIZES = (A_WIDTH, A_WIDTH, B_WIDTH, B_WIDTH, B_WIDTH, C_WIDTH, C_WIDTH, C_WIDTH)
PROJ_SPLITS = tuple(int(s) for s in np.cumsum(PROJ_SIZES)[:-1])
D_IN_PROJ = sum(PROJ_SIZES)
D_FF_2 = 4 * D_MODEL


def rms_norm(x, g):
    x32 = x.astype(jnp.float32)
    y = x32 * lax.rsqrt(jnp.mean(x32 * x32, axis=-1, keepdims=True) + EPS)
    return (y * g.astype(jnp.float32)).astype(x.dtype)

def spatial_gating(u, v, w_s, b_s):
    bsz, s = u.shape[:2]
    n_chunks = s // CHUNK_2
    vc = v.reshape(bsz, n_chunks, CHUNK_2, A_HEADS, HEAD_DIM)
    w_causal = jnp.tril(w_s)
    mixed = jnp.einsum('hij,bcjhd->bcihd', w_causal, vc) + b_s.T[None, None, :, :, None]
    return u * mixed.reshape(bsz, s, A_WIDTH)

def short_gated_conv(b_gate, c_gate, xb, w_conv):
    z = c_gate * xb
    zp = jnp.pad(z, ((0, 0), (CONV_WIDTH - 1, 0), (0, 0)))
    s = z.shape[1]
    conv = sum(w_conv[i] * zp[:, i:i + s] for i in range(CONV_WIDTH))
    return b_gate * conv

def head_rms_norm(x, g):
    x32 = x.astype(jnp.float32)
    return x32 * lax.rsqrt(jnp.mean(x32 * x32, axis=-1, keepdims=True) + EPS) * g.astype(jnp.float32)

def dilated_window_attention(q, k, v, window, dilation):
    bsz, s, h, d = q.shape
    length = s // dilation
    blk = window // dilation
    nb = -(-length // blk)
    lp = nb * blk

    def to_sub(t):
        t = t.reshape(bsz, length, dilation, h, d).transpose(0, 2, 1, 3, 4)
        t = jnp.pad(t, ((0, 0), (0, 0), (0, lp - length), (0, 0), (0, 0)))
        return t.reshape(bsz, dilation, nb, blk, h, d)

    qb = to_sub(q)
    kb = to_sub(k)
    vb = to_sub(v.astype(jnp.float32))
    pad_prev = ((0, 0), (0, 0), (1, 0), (0, 0), (0, 0), (0, 0))
    kcat = jnp.concatenate([jnp.pad(kb, pad_prev)[:, :, :-1], kb], axis=3)
    vcat = jnp.concatenate([jnp.pad(vb, pad_prev)[:, :, :-1], vb], axis=3)

    scores = jnp.einsum('brnqhd,brnkhd->brnhqk', qb, kcat) * (HEAD_DIM ** -0.5)
    qi = jnp.arange(blk)[:, None]
    kj = jnp.arange(2 * blk)[None, :]
    band = (kj >= qi) & (kj <= qi + blk)
    has_prev = jnp.arange(nb)[:, None, None] > 0
    mask = band[None] & (has_prev | (kj >= blk)[None])
    scores = jnp.where(mask[None, None, :, None], scores, -jnp.inf)
    m = jnp.max(scores, axis=-1, keepdims=True)
    e = jnp.exp(scores - m)
    den = jnp.sum(e, axis=-1, keepdims=True)
    o = jnp.einsum('brnhqk,brnkhd->brnhqd', e, vcat) / den
    lse = (m + jnp.log(den))[..., 0]

    o = o.transpose(0, 1, 2, 4, 3, 5).reshape(bsz, dilation, lp, h, d)[:, :, :length]
    o = o.transpose(0, 2, 1, 3, 4).reshape(bsz, s, h, d)
    lse = lse.transpose(0, 1, 2, 4, 3).reshape(bsz, dilation, lp, h)[:, :, :length]
    lse = lse.transpose(0, 2, 1, 3).reshape(bsz, s, h)
    return o, lse

def dilated_mixture(q, k, v, q_g, k_g):
    bsz, s = q.shape[:2]
    q = head_rms_norm(q.reshape(bsz, s, C_HEADS, HEAD_DIM), q_g)
    k = head_rms_norm(k.reshape(bsz, s, C_HEADS, HEAD_DIM), k_g)
    v = v.reshape(bsz, s, C_HEADS, HEAD_DIM)
    outs, lses = [], []
    for g, (window, dilation) in enumerate(DILATION_PATTERNS):
        sl = slice(g * C_HEADS_PER_PATTERN, (g + 1) * C_HEADS_PER_PATTERN)
        o, lse = dilated_window_attention(q[:, :, sl], k[:, :, sl], v[:, :, sl], window, dilation)
        outs.append(o)
        lses.append(lse)
    alpha = jax.nn.softmax(jnp.stack(lses, axis=0), axis=0)
    y = jnp.stack(outs, axis=0) * alpha[..., None]
    return y.transpose(1, 2, 0, 3, 4).reshape(bsz, s, C_WIDTH).astype(v.dtype)

def second_inputs(seed: int = 0) -> dict:
    key = jax.random.key(seed)
    ks = jax.random.split(key, 12)
    n = jax.random.normal
    f32 = jnp.float32
    return {
        'x': n(ks[0], (BATCH, SEQ, D_MODEL), f32),
        'attn_norm': 1.0 + 0.02 * n(ks[1], (DEPTH, D_MODEL), f32),
        'w_in': n(ks[2], (DEPTH, D_MODEL, D_IN_PROJ), f32) * D_MODEL ** -0.5,
        'sgu_w': n(ks[3], (DEPTH, A_HEADS, CHUNK_2, CHUNK_2), f32) * CHUNK_2 ** -0.5,
        'sgu_b': 1.0 + 0.1 * n(ks[4], (DEPTH, A_HEADS, CHUNK_2), f32),
        'conv_w': n(ks[5], (DEPTH, CONV_WIDTH, B_WIDTH), f32) * CONV_WIDTH ** -0.5,
        'q_norm': 1.0 + 0.02 * n(ks[6], (DEPTH, HEAD_DIM), f32),
        'k_norm': 1.0 + 0.02 * n(ks[7], (DEPTH, HEAD_DIM), f32),
        'w_out': n(ks[8], (DEPTH, D_MIX, D_MODEL), f32) * D_MIX ** -0.5,
        'mlp_norm': 1.0 + 0.02 * n(ks[9], (DEPTH, D_MODEL), f32),
        'w_mlp_in': n(ks[10], (DEPTH, D_MODEL, D_FF_2), f32) * D_MODEL ** -0.5,
        'w_mlp_out': n(ks[11], (DEPTH, D_FF_2, D_MODEL), f32) * D_FF_2 ** -0.5,
    }

def second_block(x, attn_norm, w_in, sgu_w, sgu_b, conv_w, q_norm, k_norm, w_out,
              mlp_norm, w_mlp_in, w_mlp_out):
    for l in range(DEPTH):
        h = rms_norm(x, attn_norm[l])
        p = h @ w_in[l]
        a_u, a_v, b_b, b_c, b_x, q, k, v = jnp.split(p, PROJ_SPLITS, axis=-1)
        y_a = spatial_gating(a_u, a_v, sgu_w[l], sgu_b[l])
        y_b = short_gated_conv(b_b, b_c, b_x, conv_w[l])
        y_c = dilated_mixture(q, k, v, q_norm[l], k_norm[l])
        x = x + jnp.concatenate([y_a, y_b, y_c], axis=-1) @ w_out[l]
        h = rms_norm(x, mlp_norm[l])
        x = x + jnp.square(jax.nn.relu(h @ w_mlp_in[l])) @ w_mlp_out[l]
    return x


def setup_inputs(seed=0):
    out = dict(first_inputs(seed))
    for name, value in second_inputs(seed + 1).items():
        if name != "x":
            out[name + "_2"] = value
    return out


def reference(
    x, p, mixer_norm, gla_w_in, gla_w_gate_up, gla_b_gate, gla_out_norm, gla_w_out, gdn_w_in,
    gdn_conv, gdn_a_log, gdn_dt_bias, gdn_out_norm, gdn_w_out, ffn_norm, ffn_w_in, ffn_w_out,
    ple_norm, ple_w_gate, ple_w_proj, final_norm, attn_norm_2, w_in_2, sgu_w_2, sgu_b_2,
    conv_w_2, q_norm_2, k_norm_2, w_out_2, mlp_norm_2, w_mlp_in_2, w_mlp_out_2,
):
    x = first_block(
        x, p, mixer_norm, gla_w_in, gla_w_gate_up, gla_b_gate, gla_out_norm, gla_w_out,
        gdn_w_in, gdn_conv, gdn_a_log, gdn_dt_bias, gdn_out_norm, gdn_w_out, ffn_norm, ffn_w_in,
        ffn_w_out, ple_norm, ple_w_gate, ple_w_proj, final_norm,
    )
    return second_block(
        x, attn_norm_2, w_in_2, sgu_w_2, sgu_b_2, conv_w_2, q_norm_2, k_norm_2, w_out_2,
        mlp_norm_2, w_mlp_in_2, w_mlp_out_2,
    )


_drawn_inputs = setup_inputs


def setup_inputs(seed=0):
    import zlib

    import numpy as np

    out = dict(_drawn_inputs(seed))
    spreads = {}
    factors = {'ple_norm': 5.79,
     'attn_norm_2': 2.733,
     'q_norm_2': 44.828,
     'k_norm_2': 42.734,
     'mlp_norm_2': 11.393,
     'sgu_b_2': 4.743}
    for name, (base, spread) in spreads.items():
        noise = np.random.default_rng([zlib.crc32(name.encode()), seed]).standard_normal(out[name].shape)
        drawn = base * np.exp(spread * noise) if base else spread * noise
        out[name] = __import__('jax').numpy.asarray(drawn.astype(out[name].dtype))
    for name, factor in factors.items():
        out[name] = (out[name] * factor).astype(out[name].dtype)
    return out
```

```python
import numpy as np
import concourse.bass as bass
from concourse import mybir
from contextlib import ExitStack

F32 = mybir.dt.float32
F32R = mybir.dt.float32r
U32 = mybir.dt.uint32
ALU = mybir.AluOpType
ACT = mybir.ActivationFunctionType
AX = mybir.AxisListType

P = 128
T = 256
D = 2048
DT = D // P
EPS = 1e-6
RING = 8
KP = DT // 2
GLA_H = 4
GLA_U = 8
DV_T = 4
LEVELS = [1, 2, 4, 8, 16, 32, 64, 128]
FFN_HALVES = [24, 20]
MLP_HALF = 32
HD = 64
C_H = 12
N_IN2 = 44
Q0, K0, V0, AV0, AU0, BC0, BX0, BB0 = 0, 6, 12, 18, 22, 26, 32, 38
NEG = -1.0e38
GAINS = ["mixer", "ffn", "ple", "final", "attn2", "mlp2"]


class Stage:

    def __init__(self, name, k, groups, u, slot0, group0):
        self.name, self.k, self.groups, self.u = name, k, groups, u
        self.kp = k // 2
        self.slot0, self.group0 = slot0, group0
        self.iters = groups // u
        self.body_slots = u * self.kp


def plan():
    order = [("qk", 16, 8, 2), ("v", 16, 8, 2), ("og", 16, 8, 2), ("gla_out", 16, 8, 2)]
    for n, k in enumerate(FFN_HALVES):
        order += [(f"ffn_in{n}", 16, k, 2), (f"ffn_out{n}", k, 8, 2 if k % 8 == 0 else 4)]
    order += [("ple_proj", 2, 8, 8), ("ple_gate", 16, 8, 2), ("in2", 16, N_IN2 // 2, 2), ("out2", 16, 8, 2)]
    for n in range(2):
        order += [(f"mlp_in{n}", 16, MLP_HALF // 2, 2), (f"mlp_out{n}", MLP_HALF, 8, 2)]
    stages, slot, group = {}, RING, 0
    for name, k, groups, u in order:
        stages[name] = s = Stage(name, k, groups, u, slot, group)
        assert s.body_slots % RING == 0
        slot += groups * s.kp
        group += groups
    return stages, slot


STAGES, N_SLOTS = plan()



def build(nc, A, out):
    st = STAGES
    with ExitStack() as ctx:
        def sb(name, shape, dt=F32, where=ctx):
            return where.enter_context(nc.sbuf_tensor(name, shape, dt))

        def sem(name):
            return ctx.enter_context(nc.semaphore(name))

        raw = sb("raw", [P, RING, 2, T])
        w_hi = sb("w_hi", [P, RING, 2, T], F32R)
        w_lo = sb("w_lo", [P, RING, 2, T], F32R)
        h = sb("h", [P, DT, T])
        xs = sb("xs", [P, DT, 2, T], F32R)
        ones = sb("ones", [P, P])
        ident = sb("ident", [P, P])
        gains = sb("gains", [P, len(GAINS), DT, 1])
        gain_fa = sb("gain_fa", [P, DT, 1])
        half = sb("half", [P, 2, T])
        total = sb("total", [P, 2, T])
        scaled = sb("scaled", [P, 2, T])
        sq_sum = sb("sq_sum", [P, 2, T])
        ms = sb("ms", [P, T])
        root = sb("root", [P, T])
        newt = sb("newt", [P, T])
        rs = sb("rs", [P, T])
        rs_final = sb("rs_final", [P, T])
        causal = sb("causal", [P, P])
        head_pair = sb("head_pair", [P, 2])
        qk_gain = sb("qk_gain", [P, 2])
        conv_w = sb("conv_w", [P, 6, 3])
        small = sb("small", [P, 6, 48])

        with ExitStack() as gla:
            cum = sb("cum", [P, 2, GLA_U, T], where=gla)
            dec = sb("dec", [P, 2, GLA_U, T], where=gla)
            qk_dec = sb("qk_dec", [P, 2, GLA_U, T], where=gla)
            qk = sb("qk", [P, 2, GLA_U, T], where=gla)
            v_nat = sb("v_nat", [P, 2, D], where=gla)
            a_t = sb("a_t", [P, GLA_H, 4, P], where=gla)
            masks = sb("masks", [P, len(LEVELS) - 1, P], where=gla)
            b_gate = sb("b_gate", [P, 2, GLA_U], where=gla)
            out_gain = sb("out_gain", [P, DV_T], where=gla)
        with ExitStack() as main:
            acts = sb("acts", [P, MLP_HALF, 2, T], F32R, where=main)
            gate = sb("gate", [P, 2, T], where=main)
            act_gate = sb("act_gate", [P, 2, T], where=main)
            prod = sb("prod", [P, 2, T], where=main)
            sq = sb("sq", [P, 2, 2, T], where=main)
        with ExitStack() as early:
            sb("pad_early", [P, 64 * T], where=early)
            w_up = sb("w_up", [32, 2, GLA_U, P], where=early)
            lr_w_hi = sb("lr_w_hi", [P, DT, P], F32R, where=early)
            lr_t = sb("lr_t", [P, T], where=early)
        with ExitStack() as ple:
            sb("pad_ple", [P, 40 * T], where=ple)
            ple_val = sb("ple_val", [P, DT, T], where=ple)
            p_split = sb("p_split", [P, 2, 2, T], F32R, where=ple)
            p_raw = sb("p_raw", [P, 2, T], where=ple)
        with ExitStack() as att:
            prob = sb("prob", [P, C_H, 2, T], where=att)
            amask = sb("amask", [P, 3, 2, T], where=att)
            bias_a = sb("bias_a", [P, 4, P], where=att)
            proj = sb("proj", [P, N_IN2, T], where=att)
            v2_nat = sb("v2_nat", [P, 2, 1280], where=att)
            prob_t = sb("prob_t", [P, 2, 2, T], where=att)
            sgu_wt = sb("sgu_wt", [P, 8, P], where=att)
        with ExitStack() as over:
            sq_qk = sb("sq_qk", [P, 12, T], where=over)
        with ExitStack() as over:
            r_wide = sb("r_wide", [P, 2, 24, HD], where=over)
        ps = ctx.enter_context(nc.psum_tensor("ps", [P, 8, 512], F32))

        raw_loaded = [sem(f"raw_loaded{i}") for i in range(RING // 2)]
        hi_ready = sem("hi_ready")
        lo_ready = sem("lo_ready")
        slots_used = sem("slots_used")
        half_ready = sem("half_ready")
        sum_done = sem("sum_done")
        evict_done = sem("evict_done")
        x_hi_ready = sem("x_hi_ready")
        tile_ready = sem("tile_ready")
        silu_done = sem("silu_done")
        prod_done = sem("prod_done")
        h_done = sem("h_done")
        sq_ready = sem("sq_ready")
        sq_added = sem("sq_added")
        norm_sum = sem("norm_sum")
        norm_ms = sem("norm_ms")
        norm_root = sem("norm_root")
        norm_done = sem("norm_done")
        sq_step = sem("sq_step")
        x_loaded = sem("x_loaded")
        x_again = sem("x_again")
        consts = sem("consts")
        late_consts = sem("late_consts")
        out_stored = sem("out_stored")
        act_step = sem("act_step")
        dve_step = sem("dve_step")
        x_sq = sem("x_sq")
        lr_done = sem("lr_done")
        lr_half = sem("lr_half")
        lr_ready = sem("lr_ready")
        gk_done = sem("gk_done")
        gk_read = sem("gk_read")
        ls_step = sem("ls_step")
        ls_ready = sem("ls_ready")
        vt_done = sem("vt_done")
        vt_read = sem("vt_read")
        s_done = sem("s_done")
        s_read = sem("s_read")
        dec_arg = sem("dec_arg")
        dec_exp = sem("dec_exp")
        dec_ready = sem("dec_ready")
        o_done = sem("o_done")
        o_read = sem("o_read")
        o_sq = sem("o_sq")
        og_silu = sem("og_silu")
        og_used = sem("og_used")
        y_ready = sem("y_ready")
        p_hi = sem("p_hi")
        p_ready = sem("p_ready")
        qk_sq = sem("qk_sq")
        hs_done = sem("hs_done")
        hs_ready = sem("hs_ready")
        rb_done = sem("rb_done")
        qn_ready = sem("qn_ready")
        sc_done = sem("sc_done")
        sc_read = sem("sc_read")
        nm_ready = sem("nm_ready")
        e_ready = sem("e_ready")
        ln_ready = sem("ln_ready")
        lm_ready = sem("lm_ready")
        wexp = sem("wexp")
        pw_ready = sem("pw_ready")
        pt_done = sem("pt_done")
        pt_read = sem("pt_read")
        yc_done = sem("yc_done")
        v2_done = sem("v2_done")
        v2_read = sem("v2_read")
        wm_ready = sem("wm_ready")
        ya_done = sem("ya_done")
        ya_ready = sem("ya_ready")
        yb_ready = sem("yb_ready")

        N_CONST = 11
        block = ctx.enter_context(nc.Block())

        def wait(eng, s, n):
            if not isinstance(n, int) or n > 0:
                eng.wait_ge(s, n)

        def first_time(it):
            return isinstance(it, int) and it == 0

        def iterate(eng, n, body):
            body(0)
            if n > 1:
                with eng.Fori(1, n) as it:
                    body(it)

        tiles_before = {"qk": 16}
        n = 16
        for name in ("v", "og"):
            tiles_before[name] = n
        for name, made_before in (("gla_out", 16), ("ffn_in0", 16), ("ffn_out0", 24), ("ffn_in1", 0), ("ffn_out1", 20),
                                  ("ple_proj", 0), ("ple_gate", 16), ("in2", 16), ("out2", 16), ("mlp_in0", 16),
                                  ("mlp_out0", 32), ("mlp_in1", 0), ("mlp_out1", 32)):
            n += made_before
            tiles_before[name] = n
        prods = {"ffn_in0": 0, "ffn_in1": 24, "mlp_in0": 60, "mlp_in1": 92}
        norm_no = {"ffn_in0": 1, "ple_gate": 2, "in2": 3, "mlp_in0": 4}
        norm_at = {"qk": 0}

        @block.sync
        def _(sp):
            def turn(t):
                for c in range(RING // 2):
                    wait(sp, lo_ready, RING * (t - 1) + 2 * c + 2)
                    sp.dma_start(raw[:, 2 * c:2 * c + 2], A["stream"][RING // 2 * t + c]).then_inc(raw_loaded[c], 16)

            for dst, src in ((gains, "gains"), (ones, "ones"), (ident, "ident")):
                sp.dma_start(dst[:], A[src]).then_inc(consts, 16)
            sp.dma_start(h[:], A["x"]).then_inc(x_loaded, 16)
            iterate(sp, N_SLOTS // RING, turn)
            e0 = 2 * st["mlp_out1"].group0
            for j in range(DT):
                sp.wait_ge(evict_done, e0 + j + 1)
                sp.dma_start(out[:, j], h[:, j]).then_inc(out_stored, 16)
            sp.wait_ge(out_stored, 16 * DT)

        def y_tile(k):
            return 22 + k if k < 10 else 6 + k

        def causal3():
            return causal[:].rearrange("p (a i) -> p a i", a=1).broadcast_to([P, 8, P])

        @block.tensor
        def _(pe):
            def slot(n, r, kp, moving, banks, first, last):
                pe.wait_ge(lo_ready, n + 1)
                for a in range(2):
                    x = moving(2 * kp + a)
                    for b, bank in enumerate(banks):
                        w = slice(b * P, (b + 1) * P)
                        pe.matmul(ps[:, bank, :], w_hi[:, r, a, w], x.rearrange("p a t -> p (a t)"),
                                  start=first and a == 0, stop=last and a == 1, skip_group_check=True)
                        mm = pe.matmul(ps[:, bank, 0:T], w_lo[:, r, a, w], x[:, 0],
                                       start=False, stop=last and a == 1, skip_group_check=True)
                mm.then_inc(slots_used, 1)

            def groups(s, it, moving, needs=(), after_first=None):
                for u in range(s.u):
                    wait(pe, sum_done, 2 * (s.group0 + it * s.u + u - 1))
                    for kp in range(s.kp):
                        if first_time(it) and u == 0:
                            for at, s_, count in needs:
                                if at == kp:
                                    pe.wait_ge(s_, count)
                        local = u * s.kp + kp
                        slot(s.slot0 + it * s.body_slots + local, local % RING, kp, moving,
                             [2 * (u % 2), 2 * (u % 2) + 1], kp == 0, kp == s.kp - 1)
                    if first_time(it) and u == 0 and after_first is not None:
                        after_first()

            def stage(name, moving, needs=(), after_first=None):
                iterate(pe, st[name].iters, lambda it: groups(st[name], it, moving, needs, after_first))

            def norm(k, cols):
                def go():
                    pe.wait_ge(sq_added, k)
                    for c in range(cols):
                        mm = pe.matmul(ps[:, 4, c * T:(c + 1) * T], ones[:], sq_sum[:, c], start=True, stop=True,
                                       skip_group_check=True)
                    mm.then_inc(norm_sum, 1)
                return go

            pe.wait_ge(consts, 16 * N_CONST)
            pe.wait_ge(x_sq, 1)
            for j in range(DT):
                mm = pe.matmul(ps[:, 4, 0:T], ones[:], cum[:, j // 8, j % 8], start=j == 0, stop=j == DT - 1,
                               skip_group_check=True)
            mm.then_inc(norm_sum, 1)
            pe.wait_ge(tile_ready, 16)
            for kp in range(KP):
                slot(kp, kp, kp, lambda k: xs[:, k], [5], kp == 0, kp == KP - 1)
            stage("qk", lambda k: xs[:, k])
            stage("v", lambda k: xs[:, k])
            pe.wait_ge(lr_ready, 1)
            for n in range(8):
                wait(pe, gk_read, n - 3)
                for c in range(2):
                    z, u = (2 * n + c) // GLA_U, (2 * n + c) % GLA_U
                    mm = pe.matmul(ps[:, 4 + n % 4, c * T:(c + 1) * T], w_up[:, z, u], lr_t[0:32], start=True,
                                   stop=True, skip_group_check=True)
                mm.then_inc(gk_done, 1)
            pe.wait_ge(evict_done, 2 * st["og"].group0)
            for n in range(8):
                if n < 4:
                    pe.wait_ge(gk_read, 5 + n)
                else:
                    pe.wait_ge(vt_read, n - 3)
                for c in range(4):
                    j, tt = (4 * n + c) % DT, n // 4
                    mm = pe.transpose(ps[:, 4 + n % 4, c * P:(c + 1) * P], dec[:, j // 8, j % 8, tt * P:(tt + 1) * P],
                                      ident[:])
                mm.then_inc(vt_done, 1)
            stage("og", lambda k: xs[:, k])
            for lv in range(len(LEVELS) + 1):
                src = qk if lv == 0 else qk_dec
                cross = lv == len(LEVELS)
                pe.wait_ge(dec_ready, lv + 1)
                for hp in range(2):
                    m = 2 * lv + hp
                    if m < 4:
                        pe.wait_ge(vt_read, 8)
                    wait(pe, s_read, m - 3)
                    for hh in range(2):
                        for jt in range(2):
                            it_ = 1 - jt if cross else jt
                            for d in range(2):
                                u = 2 * (2 * hp + hh) + d
                                mm = pe.matmul(ps[:, 4 + m % 4, (2 * hh + jt) * P:(2 * hh + jt + 1) * P],
                                               src[:, 1, u, jt * P:(jt + 1) * P], src[:, 0, u, it_ * P:(it_ + 1) * P],
                                               start=d == 0, stop=d == 1, skip_group_check=True)
                    mm.then_inc(s_done, 1)
            for n in range(8):
                wait(pe, s_read, 18 if n == 0 else 0)
                wait(pe, o_read, n - 3)
                for c in range(2):
                    dv = 2 * n + c
                    for jt in range(2):
                        mm = pe.matmul(ps[:, 4 + n % 4, c * T:(c + 1) * T], v_nat[:, jt, dv * P:(dv + 1) * P],
                                       a_t[:, dv // DV_T, 2 * jt:2 * jt + 2].rearrange("p a i -> p (a i)"),
                                       start=jt == 0, stop=jt == 1, skip_group_check=True)
                mm.then_inc(o_done, 1)
            pe.wait_ge(o_read, 8)
            pe.wait_ge(o_sq, 8)
            for hd in range(GLA_H):
                for d in range(DV_T):
                    mm = pe.matmul(ps[:, 4 + hd // 2, (hd % 2) * T:(hd % 2 + 1) * T], ones[:],
                                   qk[:, (hd * DV_T + d) // 8, (hd * DV_T + d) % 8], start=d == 0, stop=d == DV_T - 1,
                                   skip_group_check=True)
            mm.then_inc(norm_sum, 1)
            tb = tiles_before
            stage("gla_out", lambda k: acts[:, k], [(0, tile_ready, tb["gla_out"])])
            stage("ffn_in0", lambda k: xs[:, k],
                  [(0, tile_ready, tb["ffn_in0"] - 2), (KP - 1, tile_ready, tb["ffn_in0"])], norm(16, 1))
            for n in range(2):
                s = st[f"ffn_out{n}"]
                if n:
                    stage("ffn_in1", lambda k: xs[:, k])
                stage(s.name, lambda k: acts[:, k],
                      [(0, tile_ready, tb[s.name] - 2), (s.kp - 1, tile_ready, tb[s.name])])
            s = st["ple_proj"]
            pe.wait_ge(p_ready, 1)
            for g in range(8):
                pe.wait_ge(sum_done, 2 * (s.group0 + g - 1))
                slot(s.slot0 + g, g, 0, lambda k: p_split[:, k], [2 * (g % 2), 2 * (g % 2) + 1], True, True)
            stage("ple_gate", lambda k: xs[:, k], [(0, tile_ready, tb["ple_gate"])], norm(32, 1))
            stage("in2", lambda k: acts[:, k],
                  [(0, tile_ready, tb["in2"] - 2), (KP - 1, tile_ready, tb["in2"])], norm(48, 2))

            pe.wait_ge(qk_sq, 1)
            for tt in range(2):
                for j in range(12):
                    mm = pe.matmul(ps[:, 4, tt * 24 + 2 * j:tt * 24 + 2 * j + 2], sq_qk[:, j, tt * P:(tt + 1) * P],
                                   head_pair[:], start=True, stop=True, skip_group_check=True)
            mm.then_inc(hs_done, 1)
            for n in range(5):
                wait(pe, v2_read, n - 2)
                for c in range(4):
                    j, tt = (4 * n + c) % 10, (4 * n + c) // 10
                    mm = pe.transpose(ps[:, 5 + n % 3, c * P:(c + 1) * P], proj[:, V0 + j, tt * P:(tt + 1) * P], ident[:])
                mm.then_inc(v2_done, 1)
            pe.wait_ge(hs_ready, 1)
            pe.wait_ge(v2_read, 5)
            for n in range(6):
                wait(pe, qn_ready, 2 * (n - 3))
                for c in range(2):
                    j = 2 * n + c
                    for tt in range(2):
                        r = r_wide[:, tt, 2 * j:2 * j + 2].rearrange("p a b -> p (a b)")
                        mm = pe.matmul(ps[:, 4 + n % 4, c * T + tt * P:c * T + (tt + 1) * P],
                                       r, ident[:],
                                       start=True, stop=True, skip_group_check=True)
                mm.then_inc(rb_done, 1)
            pe.wait_ge(qn_ready, 12)
            for hd in range(C_H):
                wait(pe, sc_read, 2 * (hd - 3))
                j, rows = hd // 2, slice(HD * (hd % 2), HD * (hd % 2) + HD)
                for tt in range(2):
                    mm = pe.matmul(ps[:, 4 + hd % 4, tt * T:(tt + 1) * T], proj[rows, Q0 + j, tt * P:(tt + 1) * P],
                                   proj[rows, K0 + j], start=True, stop=True, skip_group_check=True)
                mm.then_inc(sc_done, 1)
            pe.wait_ge(wm_ready, 1)
            pe.wait_ge(sum_done, 2 * st["out2"].group0)
            for n in range(4):
                for c in range(2):
                    mm = pe.matmul(ps[:, n, c * T:(c + 1) * T], v2_nat[:, c, 768 + n * P:768 + (n + 1) * P],
                                   sgu_wt[:, 2 * n:2 * n + 2].rearrange("p a i -> p (a i)"), start=True, stop=True,
                                   skip_group_check=True)
                mm.then_inc(ya_done, 1)
            pe.wait_ge(sc_read, 24)
            for hd in range(C_H + 1):
                if hd < C_H:
                    pe.wait_ge(pw_ready, 2 * (hd + 1))
                    wait(pe, pt_read, hd - 1)
                    for s_ in range(2):
                        for tt in range(2):
                            mm = pe.transpose(ps[:, 4 + hd % 2, s_ * T + tt * P:s_ * T + (tt + 1) * P],
                                              prob[:, hd, tt, s_ * P:(s_ + 1) * P], ident[:])
                    mm.then_inc(pt_done, 1)
                if hd:
                    g = hd - 1
                    pe.wait_ge(pt_read, g + 1)
                    wait(pe, tile_ready, (tb["in2"] + g // 2 - 1) if g // 2 >= 2 else 0)
                    for s_ in range(2):
                        mm = pe.matmul(ps[HD * (g % 2):HD * (g % 2) + HD, 6 + (g // 2) % 2, 0:T],
                                       v2_nat[:, s_, g * HD:(g + 1) * HD], prob_t[:, g % 2, s_], start=s_ == 0,
                                       stop=s_ == 1, skip_group_check=True)
                    mm.then_inc(yc_done, 1)

            stage("out2", lambda k: acts[:, y_tile(k)], [(0, tile_ready, tb["out2"])])
            stage("mlp_in0", lambda k: xs[:, k],
                  [(0, tile_ready, tb["mlp_in0"] - 2), (KP - 1, tile_ready, tb["mlp_in0"])], norm(64, 1))
            for n in range(2):
                s = st[f"mlp_out{n}"]
                if n:
                    stage("mlp_in1", lambda k: xs[:, k])
                stage(s.name, lambda k: acts[:, k],
                      [(0, tile_ready, tb[s.name] - 2), (s.kp - 1, tile_ready, tb[s.name])])

        hidden = {"ffn_in0": "swiglu", "ffn_in1": "swiglu", "mlp_in0": "relu2", "mlp_in1": "relu2"}
        residual = {"gla_out": (0, 1), "ffn_out1": (16, 2), "out2": (48, 5)}

        def tile_no(s, it, u, b):
            return 2 * (s.group0 + it * s.u + u) + b

        def tile_of(s, it, u, b):
            if hidden.get(s.name) == "swiglu":
                return 2 * (it * (s.u // 2) + u // 2) + b
            return 2 * (it * s.u + u) + b

        def slots_loop(eng, s, split, finish, before, extra=None):
            def body(it):
                for u in range(s.u):
                    for kp in range(s.kp):
                        local = u * s.kp + kp
                        split(s.slot0 + it * s.body_slots + local, local % RING,
                              s.slot0 // RING + it * (s.body_slots // RING) + local // RING)
                        if 4 <= kp < 8:
                            if u > 0:
                                finish(s, it, u - 1, kp - 4)
                            elif not first_time(it):
                                finish(s, it - 1, s.u - 1, kp - 4)
                            elif before is not None:
                                finish(before, before.iters - 1, before.u - 1, kp - 4)
                        if extra is not None and first_time(it) and u == 1:
                            extra(kp)
            iterate(eng, s.iters, body)

        @block.scalar
        def _(act):
            def split(n, r, turn):
                if r % 2 == 0:
                    act.wait_ge(raw_loaded[r // 2], 16 * (turn + 1))
                wait(act, slots_used, n - RING + 1)
                act.activation(w_hi[:, r], raw[:, r], ACT.Copy).then_inc(hi_ready, 1)

            def second(s, it, u, b):
                e, j = tile_no(s, it, u, b), tile_of(s, it, u, b)
                kind = hidden.get(s.name)
                if kind == "swiglu" and u % 2 == 0:
                    act.wait_ge(evict_done, e + 1)
                    act.activation(act_gate[:, b], scaled[:, b], ACT.Silu).then_inc(silu_done, 1)
                elif kind:
                    act.wait_ge(prod_done, prods[s.name] + j + 1)
                    act.wait_ge(consts, 16 * N_CONST)
                    act.activation(acts[:, j, 0], prod[:, b], ACT.Copy).then_inc(x_hi_ready, 1)
                elif s.name in residual:
                    added, gain = residual[s.name]
                    act.wait_ge(evict_done, e + 1)
                    wait(act, sq_added, added + j - 1)
                    act.wait_ge(consts, 16 * N_CONST)
                    act.activation(sq[:, b, 0], h[:, j], ACT.Square).then_inc(sq_ready, 1)
                    act.activation(xs[:, j, 0], h[:, j], ACT.Copy, scale=gains[:, gain, j]).then_inc(x_hi_ready, 1)
                elif s.name == "ple_gate":
                    act.wait_ge(evict_done, e + 1)
                    act.activation(act_gate[:, b], scaled[:, b], ACT.Sigmoid).then_inc(silu_done, 1)

            def third(s, it, u, b):
                if s.name == "ple_gate":
                    j = tile_of(s, it, u, b)
                    act.wait_ge(h_done, j + 1)
                    wait(act, sq_added, 32 + j - 1)
                    act.wait_ge(consts, 16 * N_CONST)
                    act.activation(sq[:, b, 0], h[:, j], ACT.Square)
                    act.activation(sq[:, b, 1], h[:, j], ACT.Square, scale=gains[:, 3, j]).then_inc(sq_ready, 1)
                    act.activation(acts[:, j, 0], h[:, j], ACT.Copy, scale=gain_fa[:, j]).then_inc(x_hi_ready, 1)

            def halves(s, it, u, b):
                act.wait_ge(slots_used, s.slot0 + (it * s.u + u + 1) * s.kp)
                wait(act, sum_done, tile_no(s, it, u, b) - 1)
                act.activation(half[:, b], ps[:, 2 * (u % 2) + b, T:2 * T], ACT.Copy).then_inc(half_ready, 1)

            def finish(s, it, u, step):
                if step < 2:
                    halves(s, it, u, step)
                if 1 <= step < 3:
                    second(s, it, u, step - 1)
                if step >= 2:
                    third(s, it, u, step - 2)

            def square_root(n):
                act.wait_ge(norm_ms, n)
                act.activation(root[:], ms[:], ACT.Sqrt).then_inc(norm_root, 1)

            def stage(name, before, extra=None):
                slots_loop(act, st[name], split, finish, st[before] if before else None, extra)

            def yc_split(j):
                act.wait_ge(yc_done, 2 * j + 2)
                act.activation(acts[:, 16 + j, 0], ps[:, 6 + j % 2, 0:T], ACT.Copy).then_inc(x_hi_ready, 1)

            for dst, src in ((b_gate, "b_gate"), (out_gain, "out_gain"), (masks, "masks"), (w_up, "w_up"),
                             (causal, "causal"), (head_pair, "head_pair"), (qk_gain, "qk_gain"), (conv_w, "conv_w")):
                act.dma_start(dst[:], A[src]).then_inc(consts, 16)
            act.wait_ge(x_loaded, 16)
            act.wait_ge(consts, 16 * N_CONST)
            act.activation(cum[:], h[:].rearrange("p (a b) t -> p a b t", a=2), ACT.Square).then_inc(x_sq, 1)
            for j in range(DT):
                act.activation(xs[:, j, 0], h[:, j], ACT.Copy, scale=gains[:, 0, j]).then_inc(x_hi_ready, 1)
            square_root(1)
            for r in range(RING):
                split(r, r, 0)
            act.wait_ge(slots_used, RING)
            act.activation(half[:, 0], ps[:, 5, T:2 * T], ACT.Copy).then_inc(lr_half, 1)
            stage("qk", None)
            stage("v", "qk")
            for step in range(4):
                finish(st["v"], st["v"].iters - 1, 1, step)
            stage("og", None)
            for step in range(4):
                finish(st["og"], st["og"].iters - 1, 1, step)
            act.wait_ge(ls_step, 1)
            act.activation(dec[:], dec[:], ACT.Exp, scale=-1.0).then_inc(act_step, 1)
            act.wait_ge(act_step, 1)
            act.activation(dec[:], dec[:], ACT.Ln, bias=1.0).then_inc(ls_ready, 1)
            for lv in range(len(LEVELS)):
                act.wait_ge(dec_arg, lv + 1)
                act.activation(dec[:], dec[:], ACT.Exp, scale=1.0 / 16).then_inc(dec_exp, 1)
            for n in range(8):
                act.wait_ge(o_read, n + 1)
                o2 = qk_dec[:].rearrange("p a b t -> p (a b) t")[:, 2 * n:2 * n + 2]
                act.activation(qk[:].rearrange("p a b t -> p (a b) t")[:, 2 * n:2 * n + 2], o2, ACT.Square).then_inc(o_sq, 1)
            act.wait_ge(norm_ms, 2)
            act.activation(dec[:, 0, 4:8], dec[:, 0, 0:4], ACT.Sqrt).then_inc(norm_root, 1)
            act.activation(h[:], h[:], ACT.Silu).then_inc(og_silu, 1)
            y = qk_dec[:].rearrange("p a b t -> p (a b) t")
            act.wait_ge(y_ready, 1)
            act.activation(acts[:, 0:DT, 0], y, ACT.Copy).then_inc(x_hi_ready, 16)
            act.wait_ge(og_used, 4)
            act.dma_start(h[:], A["x"]).then_inc(x_again, 16)
            stage("gla_out", None)
            stage("ffn_in0", "gla_out", lambda kp: square_root(3) if kp == 1 else None)
            act.dma_start(p_raw[:], A["p"]).then_inc(late_consts, 16)
            stage("ffn_out0", "ffn_in0")
            act.wait_ge(late_consts, 16)
            act.activation(p_split[:, :, 0], p_raw[:], ACT.Copy).then_inc(p_hi, 1)
            stage("ffn_in1", "ffn_out0")
            stage("ffn_out1", "ffn_in1")
            s, before = st["ple_proj"], st["ffn_out1"]
            for g in range(8):
                split(s.slot0 + g, g, s.slot0 // RING)
                if g == 1:
                    for step in range(4):
                        finish(before, before.iters - 1, before.u - 1, step)
                if g >= 2:
                    halves(s, 0, g - 2, 0)
                    halves(s, 0, g - 2, 1)
            for g in (6, 7):
                halves(s, 0, g, 0)
                halves(s, 0, g, 1)
            stage("ple_gate", None, lambda kp: square_root(4) if kp == 1 else None)
            stage("in2", "ple_gate", lambda kp: square_root(4 + kp) if kp in (1, 2) else None)
            for step in range(4):
                finish(st["in2"], st["in2"].iters - 1, 0 + st["in2"].u - 1, step)

            act.wait_ge(slots_used, st["out2"].slot0)
            for dst, src in ((amask, "amask"), (bias_a, "bias_a"), (sgu_wt, "sgu_wt")):
                act.dma_start(dst[:], A[src]).then_inc(late_consts, 16)
            act.wait_ge(evict_done, 2 * (st["in2"].group0 + 6))
            act.activation(sq_qk[:], proj[:, Q0:V0], ACT.Square).then_inc(qk_sq, 1)
            act.wait_ge(norm_ms, 7)
            act.activation(small[:, 2], small[:, 1], ACT.Sqrt).then_inc(norm_root, 1)
            for hd in range(C_H):
                for tt in range(2):
                    i = 2 * hd + tt
                    act.wait_ge(nm_ready, i + 1)
                    act.activation(prob[:, hd, tt], prob[:, hd, tt], ACT.Exp, bias=small[:, 1, i:i + 1],
                                   accum_out=small[:, 2, i:i + 1]).then_inc(e_ready, 1)
            act.wait_ge(e_ready, 24)
            act.activation(small[:, 3, 0:24], small[:, 2, 0:24], ACT.Ln).then_inc(ln_ready, 1)
            act.wait_ge(lm_ready, 1)
            act.activation(small[:, 4, 0:24], small[:, 4, 0:24], ACT.Exp).then_inc(wexp, 1)
            for hd in range(C_H):
                act.wait_ge(pt_done, hd + 1)
                wait(act, yc_done, hd - 1)
                act.activation(prob_t[:, hd % 2], ps[:, 4 + hd % 2].rearrange("p (a t) -> p a t", a=2), ACT.Copy)\
                    .then_inc(pt_read, 1)
                if hd % 2 == 1 and hd >= 3:
                    yc_split(hd // 2 - 1)
            yc_split(5)
            act.wait_ge(ya_ready, 1)
            act.activation(acts[:, 22:26, 0], proj[:, AU0:AU0 + 4], ACT.Copy).then_inc(x_hi_ready, 4)
            act.wait_ge(yb_ready, 1)
            act.wait_ge(tile_ready, tiles_before["in2"] + 10)
            act.activation(acts[:, 26:32, 0], proj[:, BB0:BB0 + 6], ACT.Copy).then_inc(x_hi_ready, 6)
            stage("out2", None)
            stage("mlp_in0", "out2", lambda kp: square_root(8) if kp == 1 else None)
            stage("mlp_out0", "mlp_in0")
            stage("mlp_in1", "mlp_out0")
            stage("mlp_out1", "mlp_in1")
            for step in range(2):
                finish(st["mlp_out1"], st["mlp_out1"].iters - 1, 1, step)

        @block.gpsimd
        def _(pool):
            def add_up(done, cols, norms):
                if norms:
                    pool.wait_ge(norm_sum, norms)
                pool.memset(sq_sum[:, 0:cols], 0.0).then_inc(sq_step, 1)
                pool.wait_ge(sq_step, len(done_norms) + 1)
                done_norms.append(done)

                def two(i):
                    for b in range(2):
                        k = done + i * 2 + b
                        pool.wait_ge(sq_ready, k + 1)
                        wait(pool, sq_added, k)
                        pool.tensor_tensor(sq_sum[:, 0:cols], sq_sum[:, 0:cols], sq[:, b, 0:cols], ALU.add)\
                            .then_inc(sq_added, 1)
                iterate(pool, DT // 2, two)

            done_norms = []
            add_up(0, 1, 2)
            add_up(16, 1, 3)
            add_up(32, 2, 4)
            add_up(48, 1, 5)

        @block.vector
        def _(dve):
            steps = [0]

            def link(ins):
                steps[0] += 1
                ins.then_inc(dve_step, 1)
                dve.wait_ge(dve_step, steps[0])

            def split(n, r, turn):
                dve.wait_ge(hi_ready, n + 1)
                dve.tensor_tensor(w_lo[:, r], raw[:, r], w_hi[:, r].bitcast(F32), ALU.subtract).then_inc(lo_ready, 1)

            def add_halves(s, it, u, b):
                e = tile_no(s, it, u, b)
                dve.wait_ge(half_ready, e + 1)
                wait(dve, evict_done, e - 1)
                dve.tensor_tensor(total[:, b], ps[:, 2 * (u % 2) + b, 0:T], half[:, b], ALU.add).then_inc(sum_done, 1)
                dve.wait_ge(sum_done, e + 1)
                return e

            targets = {"qk": qk, "v": dec, "og": h}

            def first(s, it, u, b):
                e, j, name = add_halves(s, it, u, b), tile_of(s, it, u, b), s.name
                if name in targets:
                    t = targets[name]
                    flat = t[:] if name == "og" else t[:].rearrange("p a b t -> p (a b) t")
                    dve.tensor_tensor(flat[:, j], total[:, b], rs[:], ALU.mult).then_inc(evict_done, 1)
                elif name == "in2":
                    dve.tensor_tensor(proj[:, j], total[:, b], rs[:], ALU.mult).then_inc(evict_done, 1)
                elif name == "ple_proj":
                    dve.tensor_copy(ple_val[:, j], total[:, b]).then_inc(evict_done, 1)
                elif hidden.get(name) == "swiglu" and u % 2 == 0:
                    dve.tensor_tensor(scaled[:, b], total[:, b], rs[:], ALU.mult).then_inc(evict_done, 1)
                elif hidden.get(name) == "swiglu":
                    dve.tensor_tensor(gate[:, b], total[:, b], rs[:], ALU.mult).then_inc(evict_done, 1)
                    dve.wait_ge(evict_done, e + 1)
                    dve.wait_ge(silu_done, prods[name] + j + 1)
                    wait(dve, tile_ready, tiles_in(name) + j - 1)
                    dve.tensor_tensor(prod[:, b], gate[:, b], act_gate[:, b], ALU.mult).then_inc(prod_done, 1)
                elif hidden.get(name) == "relu2":
                    dve.tensor_tensor(scaled[:, b], total[:, b], rs[:], ALU.mult).then_inc(evict_done, 1)
                    dve.wait_ge(evict_done, e + 1)
                    wait(dve, tile_ready, tiles_in(name) + j - 1)
                    dve.scalar_tensor_tensor(out=prod[:, b], in0=scaled[:, b], scalar=0.0, in1=scaled[:, b],
                                             op0=ALU.max, op1=ALU.mult).then_inc(prod_done, 1)
                elif name == "ple_gate":
                    dve.tensor_tensor(scaled[:, b], total[:, b], rs[:], ALU.mult).then_inc(evict_done, 1)
                elif name == "out2":
                    dve.scalar_tensor_tensor(out=scaled[:, b], in0=h[:, j], scalar=gains[:, 3, j],
                                             in1=rs_final[:], op0=ALU.mult, op1=ALU.mult).then_inc(h_done, 1)
                    dve.wait_ge(h_done, 16 + j + 1)
                    dve.tensor_tensor(h[:, j], scaled[:, b], total[:, b], ALU.add).then_inc(evict_done, 1)
                else:
                    dve.tensor_tensor(h[:, j], h[:, j], total[:, b], ALU.add).then_inc(evict_done, 1)

            def tiles_in(name):
                return tiles_before[name]

            def then(s, it, u, b):
                e, j = tile_no(s, it, u, b), tile_of(s, it, u, b)
                kind = hidden.get(s.name)
                if kind == "swiglu" and u % 2 == 0:
                    return
                if kind:
                    dve.wait_ge(x_hi_ready, tiles_in(s.name) + j + 1)
                    dve.tensor_tensor(acts[:, j, 1], prod[:, b], acts[:, j, 0].bitcast(F32), ALU.subtract)\
                        .then_inc(tile_ready, 1)
                elif s.name in residual:
                    dve.wait_ge(x_hi_ready, tiles_in(s.name) + j + 1)
                    dve.scalar_tensor_tensor(out=xs[:, j, 1], in0=h[:, j], scalar=gains[:, residual[s.name][1], j],
                                             in1=xs[:, j, 0].bitcast(F32), op0=ALU.mult, op1=ALU.subtract)\
                        .then_inc(tile_ready, 1)
                elif s.name == "ple_gate":
                    dve.wait_ge(silu_done, 44 + j + 1)
                    dve.tensor_tensor(prod[:, b], act_gate[:, b], ple_val[:, j], ALU.mult).then_inc(prod_done, 1)
                    dve.wait_ge(prod_done, 44 + j + 1)
                    dve.tensor_tensor(h[:, j], h[:, j], prod[:, b], ALU.add).then_inc(h_done, 1)

            def last(s, it, u, b):
                if s.name == "ple_gate":
                    j = tile_of(s, it, u, b)
                    dve.wait_ge(x_hi_ready, tiles_in(s.name) + j + 1)
                    dve.scalar_tensor_tensor(out=acts[:, j, 1], in0=h[:, j], scalar=gain_fa[:, j],
                                             in1=acts[:, j, 0].bitcast(F32), op0=ALU.mult, op1=ALU.subtract)\
                        .then_inc(tile_ready, 1)

            def finish(s, it, u, step):
                if step < 2:
                    first(s, it, u, step)
                else:
                    then(s, it, u, step - 2)
                if step == 3:
                    last(s, it, u, 0)
                    last(s, it, u, 1)

            def stage(name, before, extra=None):
                slots_loop(dve, st[name], split, finish, st[before] if before else None, extra)

            def newton(out_, r, x, tmp):
                link(dve.reciprocal(out_, r))
                link(dve.tensor_tensor(tmp, out_, out_, ALU.mult))
                link(dve.tensor_tensor(tmp, tmp, x, ALU.mult))
                link(dve.tensor_scalar(tmp, tmp, -0.5, 1.5, ALU.mult, ALU.add))
                link(dve.tensor_tensor(out_, out_, tmp, ALU.mult))

            def norm_begin(k):
                dve.wait_ge(norm_sum, k)
                dve.tensor_scalar(ms[:], ps[:, 4, 0:T], 1.0 / D, EPS, ALU.mult, ALU.add).then_inc(norm_ms, 1)

            def norm_end(k, dst):
                dve.wait_ge(norm_root, k)
                newton(dst, root[:], ms[:], newt[:])

            def norm_hook(k, sums=None):
                def go(kp):
                    if kp == 0:
                        norm_begin(sums or k)
                    if kp == 2:
                        norm_end(k, rs[:])
                return go

            dve.wait_ge(consts, 16 * N_CONST)
            link(dve.tensor_tensor(gain_fa[:], gains[:, 3], gains[:, 4], ALU.mult))
            for j in range(DT):
                dve.wait_ge(x_hi_ready, j + 1)
                dve.scalar_tensor_tensor(out=xs[:, j, 1], in0=h[:, j], scalar=gains[:, 0, j],
                                         in1=xs[:, j, 0].bitcast(F32), op0=ALU.mult, op1=ALU.subtract)\
                    .then_inc(tile_ready, 1)
            norm_begin(1)
            norm_end(1, rs[:])
            for r in range(RING):
                split(r, r, 0)
            dve.wait_ge(lr_half, 1)
            link(dve.tensor_tensor(total[:, 0], ps[:, 5, 0:T], half[:, 0], ALU.add))
            dve.tensor_tensor(lr_t[:], total[:, 0], rs[:], ALU.mult).then_inc(lr_ready, 1)
            dve.wait_ge(lr_ready, 1)
            stage("qk", None)
            stage("v", "qk")
            for step in range(4):
                finish(st["v"], st["v"].iters - 1, 1, step)
            cumf = cum[:].rearrange("p a b t -> p (a b) t")
            bgf = b_gate[:].rearrange("p a b -> p (a b)")
            for n in range(8):
                dve.wait_ge(gk_done, n + 1)
                for c in range(2):
                    ins = dve.tensor_scalar(cumf[:, 2 * n + c], ps[:, 4 + n % 4, c * T:(c + 1) * T],
                                            bgf[:, 2 * n + c:2 * n + c + 1], None, ALU.add)
                ins.then_inc(gk_read, 1)
            dve.wait_ge(gk_read, 8)
            for n in range(8):
                dve.wait_ge(vt_done, n + 1)
                dve.tensor_copy(v_nat[:, n // 4, (n % 4) * 512:(n % 4 + 1) * 512], ps[:, 4 + n % 4]).then_inc(vt_read, 1)
            stage("og", None)
            for step in range(4):
                finish(st["og"], st["og"].iters - 1, 1, step)
            dve.wait_ge(vt_read, 8)
            dve.scalar_tensor_tensor(out=dec[:], in0=cum[:], scalar=-1.0, in1=cum[:], op0=ALU.mult, op1=ALU.max)\
                .then_inc(ls_step, 1)
            dve.wait_ge(ls_ready, 1)
            link(dve.scalar_tensor_tensor(out=dec[:], in0=cum[:], scalar=0.0, in1=dec[:], op0=ALU.min, op1=ALU.subtract))
            link(dve.memset(qk_dec[:, 0, 0], 1.0))
            link(dve.memset(cum[:, 1, :, 0:1], 0.0))
            for u in range(GLA_U):
                dve.tensor_tensor_scan(cum[:, 0, u], qk_dec[:, 0, 0], dec[:, 0, u], 0.0, ALU.mult, ALU.add)
                ins = dve.tensor_tensor_scan(cum[:, 1, u, 1:T], qk_dec[:, 0, 0, 1:T], dec[:, 1, u, 0:T - 1], 0.0,
                                             ALU.mult, ALU.add)
            ins.then_inc(dec_ready, 1)
            dve.wait_ge(dec_ready, 1)

            def scores_out(lv):
                for hp in range(2):
                    m = 2 * lv + hp
                    dve.wait_ge(s_done, m + 1)
                    for hh in range(2):
                        hd = 2 * hp + hh
                        src = ps[:, 4 + m % 4, hh * T:(hh + 1) * T].rearrange("p (a i) -> p a i", a=2)
                        if lv == 0:
                            ins = dve.tensor_scalar(a_t[:, hd, 0:4:3], src, 2.0, None, ALU.mult)
                        elif lv < len(LEVELS):
                            dst = a_t[:, hd, 0:4:3]
                            mask = masks[:, lv - 1:lv].bitcast(U32).broadcast_to([P, 2, P])
                            if hd == 0 and hp == 0:
                                dve.wait_ge(s_read, 2 * lv)
                            ins = dve.copy_predicated(dst, mask, src)
                        else:
                            ins = dve.tensor_copy(a_t[:, hd, 1:3], src)
                    ins.then_inc(s_read, 1)

            for lv, s in enumerate(LEVELS):
                def cut(x):
                    return x.rearrange("p u (n b s) -> p (u n) b s", b=2, s=s)
                n = GLA_U * T // (2 * s)
                f, b, dq, dk = cut(cum[:, 0]), cut(cum[:, 1]), cut(dec[:, 0]), cut(dec[:, 1])
                ref_f = f[:, :, 0, s - 1:s].broadcast_to([P, n, s])
                ref_b = b[:, :, 1, 0:1].broadcast_to([P, n, s])
                if lv:
                    dve.wait_ge(dec_ready, lv + 1)
                dve.tensor_tensor(dq[:, :, 1], f[:, :, 1], ref_f, ALU.subtract)
                dve.tensor_tensor(dk[:, :, 0], ref_f, f[:, :, 0], ALU.subtract)
                dve.tensor_tensor(dq[:, :, 0], ref_b, b[:, :, 0], ALU.subtract)
                dve.tensor_tensor(dk[:, :, 1], b[:, :, 1], ref_b, ALU.subtract).then_inc(dec_arg, 1)
                scores_out(lv)
                dve.wait_ge(dec_exp, lv + 1)
                dve.tensor_tensor(qk_dec[:], qk[:], dec[:], ALU.mult).then_inc(dec_ready, 1)
            scores_out(len(LEVELS))
            o = qk_dec[:].rearrange("p a b t -> p (a b) t")
            for n in range(8):
                dve.wait_ge(o_done, n + 1)
                dve.tensor_scalar(o[:, 2 * n:2 * n + 2], ps[:, 4 + n % 4].rearrange("p (a t) -> p a t", a=2),
                                  1.0 / 16, None, ALU.mult).then_inc(o_read, 1)
            m4, r4, t4, d4 = dec[:, 0, 0:4], dec[:, 0, 4:8], dec[:, 1, 0:4], dec[:, 1, 4:8]
            dve.wait_ge(norm_sum, 2)
            dve.tensor_scalar(m4, ps[:, 4:6].rearrange("p a (b t) -> p (a b) t", b=2), 1.0 / 512, EPS, ALU.mult, ALU.add)\
                .then_inc(norm_ms, 1)
            dve.wait_ge(norm_root, 2)
            newton(d4, r4, m4, t4)
            dve.wait_ge(og_silu, 1)
            o4 = o.rearrange("p (a b) t -> p a b t", b=DV_T)
            og4 = h[:].rearrange("p (a b) t -> p a b t", b=DV_T)
            for d in range(DV_T):
                dve.scalar_tensor_tensor(out=o4[:, :, d], in0=o4[:, :, d], scalar=out_gain[:, d:d + 1],
                                         in1=og4[:, :, d], op0=ALU.mult, op1=ALU.mult).then_inc(og_used, 1)
            dve.wait_ge(og_used, 4)
            for d in range(DV_T):
                ins = dve.tensor_tensor(o4[:, :, d], o4[:, :, d], d4, ALU.mult)
            ins.then_inc(y_ready, 1)
            dve.wait_ge(x_hi_ready, 32)
            dve.wait_ge(y_ready, 1)
            dve.tensor_tensor(acts[:, 0:DT, 1], o, acts[:, 0:DT, 0].bitcast(F32), ALU.subtract).then_inc(tile_ready, 16)
            dve.wait_ge(x_again, 16)
            stage("gla_out", None)
            stage("ffn_in0", "gla_out", norm_hook(3))
            stage("ffn_out0", "ffn_in0")
            dve.wait_ge(p_hi, 1)
            dve.tensor_tensor(p_split[:, :, 1], p_raw[:], p_split[:, :, 0].bitcast(F32), ALU.subtract).then_inc(p_ready, 1)
            stage("ffn_in1", "ffn_out0")
            stage("ffn_out1", "ffn_in1")
            s, before = st["ple_proj"], st["ffn_out1"]
            for g in range(8):
                split(s.slot0 + g, g, s.slot0 // RING)
                if g == 1:
                    for step in range(4):
                        finish(before, before.iters - 1, before.u - 1, step)
                if g >= 2:
                    first(s, 0, g - 2, 0)
                    first(s, 0, g - 2, 1)
            for g in (6, 7):
                first(s, 0, g, 0)
                first(s, 0, g, 1)
            stage("ple_gate", None, norm_hook(4))

            def two_norms(kp):
                if kp == 0:
                    norm_begin(5)
                if kp == 2:
                    norm_end(5, rs_final[:])
                    link(dve.tensor_tensor(ms[:], rs_final[:], rs_final[:], ALU.mult))
                    link(dve.tensor_tensor(ms[:], ms[:], ps[:, 4, T:2 * T], ALU.mult))
                    dve.tensor_scalar(ms[:], ms[:], 1.0 / D, EPS, ALU.mult, ALU.add).then_inc(norm_ms, 1)
                if kp == 3:
                    norm_end(6, rs[:])
                    link(dve.tensor_tensor(rs[:], rs[:], rs_final[:], ALU.mult))

            stage("in2", "ple_gate", two_norms)
            for step in range(4):
                finish(st["in2"], st["in2"].iters - 1, st["in2"].u - 1, step)

            dve.wait_ge(evict_done, 2 * st["out2"].group0)
            dve.wait_ge(hs_done, 1)
            dve.tensor_scalar(small[:, 1], ps[:, 4, 0:48], 1.0 / HD, EPS, ALU.mult, ALU.add).then_inc(norm_ms, 1)
            for n in range(5):
                dve.wait_ge(v2_done, n + 1)
                for c in range(4):
                    j, tt = (4 * n + c) % 10, (4 * n + c) // 10
                    ins = dve.tensor_copy(v2_nat[:, tt, j * P:(j + 1) * P], ps[:, 5 + n % 3, c * P:(c + 1) * P])
                ins.then_inc(v2_read, 1)
            dve.wait_ge(norm_root, 7)
            newton(small[:, 0], small[:, 2], small[:, 1], small[:, 3])
            link(dve.tensor_scalar(qk_gain[:, 0:1], qk_gain[:, 0:1], HD ** -0.5, None, ALU.mult))
            wide = small[:, 0:1].rearrange("p o (a h) -> p (o a) h", a=2).rearrange("p a (h o) -> p a h o", o=1)
            dve.tensor_copy(r_wide[:], wide.broadcast_to([P, 2, 24, HD])).then_inc(hs_ready, 1)
            for j in range(12):
                dve.wait_ge(rb_done, j // 2 + 1)
                dve.scalar_tensor_tensor(out=proj[:, Q0 + j], in0=proj[:, Q0 + j], scalar=qk_gain[:, j // 6:j // 6 + 1],
                                         in1=ps[:, 4 + (j // 2) % 4, (j % 2) * T:(j % 2 + 1) * T], op0=ALU.mult,
                                         op1=ALU.mult).then_inc(qn_ready, 1)
            dve.wait_ge(late_consts, 64)
            dve.tensor_tensor(sgu_wt[:], sgu_wt[:], causal3(), ALU.mult).then_inc(wm_ready, 1)
            dve.wait_ge(qk_sq, 1)
            for hd in range(C_H):
                dve.wait_ge(sc_done, hd + 1)
                for tt in range(2):
                    i = 2 * hd + tt
                    dve.tensor_tensor_reduce(prob[:, hd, tt], ps[:, 4 + hd % 4, tt * T:(tt + 1) * T],
                                             amask[:, hd // 4, tt], 1.0, 2 * NEG, ALU.add, ALU.max,
                                             small[:, 0, i:i + 1]).then_inc(sc_read, 1)
                    dve.wait_ge(sc_read, i + 1)
                    dve.tensor_scalar(small[:, 1, i:i + 1], small[:, 0, i:i + 1], -1.0, None, ALU.mult).then_inc(nm_ready, 1)
            dve.wait_ge(late_consts, 64)
            for n in range(4):
                dve.wait_ge(ya_done, n + 1)
                for hf in range(2):
                    rows = slice(HD * hf, HD * hf + HD)
                    src = ps[rows, n].rearrange("p (c a i) -> p c a i", c=2, a=2)[:, :, hf]
                    ins = dve.tensor_tensor(proj[rows, AV0 + n].rearrange("p (c i) -> p c i", c=2), src,
                                            bias_a[rows, n:n + 1].broadcast_to([HD, 2, P]), ALU.add)
            link(ins)
            dve.tensor_tensor(proj[:, AU0:AU0 + 4], proj[:, AU0:AU0 + 4], proj[:, AV0:AV0 + 4], ALU.mult).then_inc(ya_ready, 1)
            bx, bc, bb = proj[:, BX0:BX0 + 6], proj[:, BC0:BC0 + 6], proj[:, BB0:BB0 + 6]
            link(dve.tensor_tensor(bx, bx, bc, ALU.mult))
            for j in range(6):
                ins = dve.tensor_scalar(bc[:, j], bx[:, j], conv_w[:, j, 2:3], None, ALU.mult)
            link(ins)
            for lag in (1, 2):
                for j in range(6):
                    ins = dve.scalar_tensor_tensor(out=bc[:, j, lag:T], in0=bx[:, j, 0:T - lag],
                                                   scalar=conv_w[:, j, 2 - lag:3 - lag], in1=bc[:, j, lag:T],
                                                   op0=ALU.mult, op1=ALU.add)
                link(ins)
            dve.tensor_tensor(bb, bb, bc, ALU.mult).then_inc(yb_ready, 1)
            dve.wait_ge(ln_ready, 1)
            mx, den, lse, wt, s5 = (small[:, k, 0:24] for k in (0, 2, 3, 4, 5))
            link(dve.tensor_tensor(lse, lse, mx, ALU.add))
            g3 = lse.rearrange("p (g x) -> p g x", g=3)
            w3 = wt.rearrange("p (g x) -> p g x", g=3)
            link(dve.tensor_tensor(s5[:, 0:8], g3[:, 0], g3[:, 1], ALU.max))
            link(dve.tensor_tensor(s5[:, 0:8], s5[:, 0:8], g3[:, 2], ALU.max))
            for g in range(3):
                ins = dve.tensor_tensor(w3[:, g], g3[:, g], s5[:, 0:8], ALU.subtract)
            ins.then_inc(lm_ready, 1)
            dve.wait_ge(wexp, 1)
            link(dve.tensor_tensor(s5[:, 8:16], w3[:, 0], w3[:, 1], ALU.add))
            link(dve.tensor_tensor(s5[:, 8:16], s5[:, 8:16], w3[:, 2], ALU.add))
            for g in range(3):
                ins = dve.tensor_tensor(den.rearrange("p (g x) -> p g x", g=3)[:, g],
                                        den.rearrange("p (g x) -> p g x", g=3)[:, g], s5[:, 8:16], ALU.mult)
            link(ins)
            link(dve.reciprocal(den, den))
            link(dve.tensor_tensor(wt, wt, den, ALU.mult))
            for i in range(24):
                dve.tensor_scalar(prob[:, i // 2, i % 2], prob[:, i // 2, i % 2], wt[:, i:i + 1], None, ALU.mult)\
                    .then_inc(pw_ready, 1)
            for j in range(6):
                dve.wait_ge(x_hi_ready, tiles_before["in2"] + j + 1)
                dve.tensor_tensor(acts[:, 16 + j, 1], ps[:, 6 + j % 2, 0:T], acts[:, 16 + j, 0].bitcast(F32), ALU.subtract)\
                    .then_inc(tile_ready, 1)
            dve.wait_ge(x_hi_ready, tiles_before["in2"] + 10)
            dve.tensor_tensor(acts[:, 22:26, 1], proj[:, AU0:AU0 + 4], acts[:, 22:26, 0].bitcast(F32), ALU.subtract)\
                .then_inc(tile_ready, 4)
            dve.wait_ge(x_hi_ready, tiles_before["in2"] + 16)
            dve.tensor_tensor(acts[:, 26:32, 1], proj[:, BB0:BB0 + 6], acts[:, 26:32, 0].bitcast(F32), ALU.subtract)\
                .then_inc(tile_ready, 6)
            stage("out2", None)
            stage("mlp_in0", "out2", norm_hook(8, 6))
            stage("mlp_out0", "mlp_in0")
            stage("mlp_in1", "mlp_out0")
            stage("mlp_out1", "mlp_in1")
            for step in range(2):
                finish(st["mlp_out1"], st["mlp_out1"].iters - 1, 1, step)


def _slots(w):
    k, n = w.shape
    return w.reshape(k // 256, 2, P, n // T, T).transpose(3, 0, 2, 1, 4).reshape(-1, P, 2, T)


def _features(x):
    return x.T.reshape(-1, P, x.shape[0]).transpose(1, 0, 2)


def _per_feature(v):
    return v.reshape(-1, P).T


def lay_out(inputs):
    g = {k: np.asarray(v) for k, v in inputs.items()}
    f = np.float32
    w_in = g["gla_w_in"][0]
    lr = np.zeros((D, T), f)
    lr[:, 0:32] = w_in[:, 6144:6176]
    gate, up = g["ffn_w_in"][0][:, :5632], g["ffn_w_in"][0][:, 5632:]
    parts = [_slots(lr), _slots(w_in[:, 0:6144]), _slots(g["gla_w_out"][0])]
    at = 0
    for k in FFN_HALVES:
        cols = slice(at, at + k * P)
        pair = np.stack([gate[:, cols].reshape(D, k // 2, T), up[:, cols].reshape(D, k // 2, T)], 2)
        parts += [_slots(pair.reshape(D, k * T)), _slots(g["ffn_w_out"][0][cols])]
        at += k * P
    parts += [_slots(g["ple_w_proj"][0]), _slots(g["ple_w_gate"][0])]
    w2 = g["w_in_2"][0]
    e = np.cumsum([0, 512, 512, 768, 768, 768, 768, 768, 768])
    c = [w2[:, e[i]:e[i + 1]] for i in range(8)]
    parts += [_slots(np.concatenate([c[5], c[6], c[7], c[1], c[0], c[3], c[4], c[2]], 1)), _slots(g["w_out_2"][0])]
    for n in range(2):
        cols = slice(n * MLP_HALF * P, (n + 1) * MLP_HALF * P)
        parts += [_slots(g["w_mlp_in_2"][0][:, cols]), _slots(g["w_mlp_out_2"][0][cols])]
    stream = np.concatenate(parts)
    assert len(stream) == N_SLOTS
    stream = np.ascontiguousarray(stream.reshape(N_SLOTS // 2, 2, P, 2, T).transpose(0, 2, 1, 3, 4))
    w_up = np.zeros((32, 2, GLA_U, P), f)
    for z in range(2):
        w_up[16 * z:16 * z + 16, z] = g["gla_w_gate_up"][0, z].reshape(16, GLA_U, P)
    i = np.arange(P)
    masks = np.stack([((i[:, None] // s) ^ (i[None, :] // s)) == 1 for s in LEVELS[:-1]], 1).astype(f)
    t = (np.arange(2)[None, :, None] * P + i[:, None, None])
    key = np.arange(T)[None, None, :]
    back = t - key
    ok = [(back >= 0) & (back <= 128), (back >= 0) & (back % 4 == 0), (back >= 0) & (back % 16 == 0)]
    amask = np.stack([np.where(m, 0.0, NEG) for m in ok], 1).astype(f)
    hp = np.zeros((P, 2), f)
    hp[:HD, 0] = 1
    hp[HD:, 1] = 1
    sgu_b = g["sgu_b_2"][0].reshape(4, 2, P)
    arrays = {
        "stream": stream,
        "x": _features(g["x"][0]),
        "p": _features(g["p"][0, 0]),
        "gains": np.stack([_per_feature(g[n].reshape(-1)) for n in
                           ("mixer_norm", "ffn_norm", "ple_norm", "final_norm", "attn_norm_2", "mlp_norm_2")], 1)[..., None],
        "ones": np.ones((P, P), f), "ident": np.eye(P, dtype=f),
        "b_gate": g["gla_b_gate"][0].reshape(2, GLA_U, P).transpose(2, 0, 1),
        "out_gain": _per_feature(g["gla_out_norm"][0]),
        "masks": masks, "w_up": w_up,
        "causal": (i[:, None] <= i[None, :]).astype(f), "head_pair": hp,
        "qk_gain": np.stack([np.tile(g["q_norm_2"][0], 2), np.tile(g["k_norm_2"][0], 2)], 1),
        "conv_w": g["conv_w_2"][0].reshape(3, 6, P).transpose(2, 1, 0),
        "amask": amask,
        "bias_a": np.repeat(sgu_b.transpose(1, 0, 2), HD, 0),
        "sgu_wt": g["sgu_w_2"][0].transpose(2, 0, 1),
    }
    return {k: np.ascontiguousarray(v) for k, v in arrays.items()}


def kernel(**inputs):
    import concourse.bacc as bacc
    from concourse.bass_utils import run_bass_kernel_spmd

    arrays = lay_out(inputs)
    nc = bacc.Bacc("TRN2", target_bir_lowering=False, num_devices=1)
    aps = {k: nc.dram_tensor(f"in_{k}", v.shape, mybir.dt.from_np(v.dtype), kind="ExternalInput").ap()
           for k, v in arrays.items()}
    out = nc.dram_tensor("out_t", (P, DT, T), F32, kind="ExternalOutput").ap()
    build(nc, aps, out)
    r = run_bass_kernel_spmd(nc, [{f"in_{k}": v for k, v in arrays.items()}], core_ids=[0])
    return r.results[0]["out_t"].transpose(2, 1, 0).reshape(1, T, D)
```

```python
import numpy as np
import concourse.bass as bass
from concourse import mybir
from contextlib import ExitStack

F32 = mybir.dt.float32
F32R = mybir.dt.float32r
U32 = mybir.dt.uint32
ALU = mybir.AluOpType
ACT = mybir.ActivationFunctionType
AX = mybir.AxisListType

P = 128
T = 256
D = 2048
DT = D // P
EPS = 1e-6
RING = 8
KP = DT // 2
GLA_H = 4
GLA_U = 8
DV_T = 4
LEVELS = [1, 2, 4, 8, 16, 32, 64, 128]
FFN_HALVES = [24, 20]
MLP_HALF = 32
HD = 64
C_H = 12
N_IN2 = 44
Q0, K0, V0, AV0, AU0, BC0, BX0, BB0 = 0, 6, 12, 18, 22, 26, 32, 38
NEG = -1.0e38
GAINS = ["mixer", "ffn", "ple", "final", "attn2", "mlp2"]


class Stage:

    def __init__(self, name, k, groups, u, slot0, group0):
        self.name, self.k, self.groups, self.u = name, k, groups, u
        self.kp = k // 2
        self.slot0, self.group0 = slot0, group0
        self.iters = groups // u
        self.body_slots = u * self.kp


def plan():
    order = [("qk", 16, 8, 2), ("v", 16, 8, 2), ("og", 16, 8, 2), ("gla_out", 16, 8, 2)]
    for n, k in enumerate(FFN_HALVES):
        order += [(f"ffn_in{n}", 16, k, 2), (f"ffn_out{n}", k, 8, 2 if k % 8 == 0 else 4)]
    order += [("ple_proj", 2, 8, 8), ("ple_gate", 16, 8, 2), ("in2", 16, N_IN2 // 2, 2), ("out2", 16, 8, 2)]
    for n in range(2):
        order += [(f"mlp_in{n}", 16, MLP_HALF // 2, 2), (f"mlp_out{n}", MLP_HALF, 8, 2)]
    stages, slot, group = {}, RING, 0
    for name, k, groups, u in order:
        stages[name] = s = Stage(name, k, groups, u, slot, group)
        assert s.body_slots % RING == 0
        slot += groups * s.kp
        group += groups
    return stages, slot


STAGES, N_SLOTS = plan()



def build(nc, A, out):
    st = STAGES
    with ExitStack() as ctx:
        def sb(name, shape, dt=F32, where=ctx):
            return where.enter_context(nc.sbuf_tensor(name, shape, dt))

        def sem(name):
            return ctx.enter_context(nc.semaphore(name))

        raw = sb("raw", [P, RING, 2, T])
        w_hi = sb("w_hi", [P, RING, 2, T], F32R)
        w_lo = sb("w_lo", [P, RING, 2, T], F32R)
        h = sb("h", [P, DT, T])
        xs = sb("xs", [P, DT, 2, T], F32R)
        ones = sb("ones", [P, P])
        ident = sb("ident", [P, P])
        gains = sb("gains", [P, len(GAINS), DT, 1])
        gain_fa = sb("gain_fa", [P, DT, 1])
        half = sb("half", [P, 2, T])
        total = sb("total", [P, 2, T])
        scaled = sb("scaled", [P, 2, T])
        sq_sum = sb("sq_sum", [P, 2, T])
        ms = sb("ms", [P, T])
        root = sb("root", [P, T])
        newt = sb("newt", [P, T])
        rs = sb("rs", [P, T])
        rs_final = sb("rs_final", [P, T])
        causal = sb("causal", [P, P])
        head_pair = sb("head_pair", [P, 2])
        qk_gain = sb("qk_gain", [P, 2])
        conv_w = sb("conv_w", [P, 6, 3])
        small = sb("small", [P, 6, 48])

        with ExitStack() as gla:
            cum = sb("cum", [P, 2, GLA_U, T], where=gla)
            dec = sb("dec", [P, 2, GLA_U, T], where=gla)
            qk_dec = sb("qk_dec", [P, 2, GLA_U, T], where=gla)
            qk = sb("qk", [P, 2, GLA_U, T], where=gla)
            v_nat = sb("v_nat", [P, 2, D], where=gla)
            a_t = sb("a_t", [P, GLA_H, 4, P], where=gla)
            masks = sb("masks", [P, len(LEVELS) - 1, P], where=gla)
            b_gate = sb("b_gate", [P, 2, GLA_U], where=gla)
            out_gain = sb("out_gain", [P, DV_T], where=gla)
        with ExitStack() as over:
            rh_wide = sb("rh_wide", [P, 2 * GLA_H, P], where=over)
        with ExitStack() as main:
            acts = sb("acts", [P, MLP_HALF, 2, T], F32R, where=main)
            gate = sb("gate", [P, 2, T], where=main)
            act_gate = sb("act_gate", [P, 2, T], where=main)
            prod = sb("prod", [P, 2, T], where=main)
            sq = sb("sq", [P, 2, 2, T], where=main)
        with ExitStack() as early:
            sb("pad_early", [P, 64 * T], where=early)
            w_up = sb("w_up", [32, 2, GLA_U, P], where=early)
            lr_w_hi = sb("lr_w_hi", [P, DT, P], F32R, where=early)
            lr_t = sb("lr_t", [P, T], where=early)
        with ExitStack() as ple:
            sb("pad_ple", [P, 40 * T], where=ple)
            ple_val = sb("ple_val", [P, DT, T], where=ple)
            p_split = sb("p_split", [P, 2, 2, T], F32R, where=ple)
            p_raw = sb("p_raw", [P, 2, T], where=ple)
        with ExitStack() as att:
            prob = sb("prob", [P, C_H, 2, T], where=att)
            amask = sb("amask", [P, 3, 2, T], where=att)
            bias_a = sb("bias_a", [P, 4, P], where=att)
            proj = sb("proj", [P, N_IN2, T], where=att)
            v2_nat = sb("v2_nat", [P, 2, 1280], where=att)
            prob_t = sb("prob_t", [P, 2, 2, T], where=att)
            sgu_wt = sb("sgu_wt", [P, 8, P], where=att)
        with ExitStack() as over:
            sq_qk = sb("sq_qk", [P, 12, T], where=over)
        with ExitStack() as over:
            r_wide = sb("r_wide", [P, 2, 24, HD], where=over)
        ps = ctx.enter_context(nc.psum_tensor("ps", [P, 8, 512], F32))

        raw_loaded = [sem(f"raw_loaded{i}") for i in range(RING // 2)]
        hi_ready = sem("hi_ready")
        lo_ready = sem("lo_ready")
        slots_used = sem("slots_used")
        half_ready = sem("half_ready")
        sum_done = sem("sum_done")
        evict_done = sem("evict_done")
        x_hi_ready = sem("x_hi_ready")
        tile_ready = sem("tile_ready")
        silu_done = sem("silu_done")
        prod_done = sem("prod_done")
        h_done = sem("h_done")
        sq_ready = sem("sq_ready")
        sq_added = sem("sq_added")
        norm_sum = sem("norm_sum")
        norm_ms = sem("norm_ms")
        norm_root = sem("norm_root")
        norm_done = sem("norm_done")
        sq_step = sem("sq_step")
        x_loaded = sem("x_loaded")
        x_again = sem("x_again")
        consts = sem("consts")
        late_consts = sem("late_consts")
        out_stored = sem("out_stored")
        act_step = sem("act_step")
        dve_step = sem("dve_step")
        x_sq = sem("x_sq")
        lr_done = sem("lr_done")
        lr_half = sem("lr_half")
        lr_ready = sem("lr_ready")
        gk_done = sem("gk_done")
        gk_read = sem("gk_read")
        ls_step = sem("ls_step")
        ls_ready = sem("ls_ready")
        vt_done = sem("vt_done")
        vt_read = sem("vt_read")
        s_done = sem("s_done")
        s_read = sem("s_read")
        dec_arg = sem("dec_arg")
        dec_exp = sem("dec_exp")
        dec_ready = sem("dec_ready")
        o_done = sem("o_done")
        o_read = sem("o_read")
        rh_ready = sem("rh_ready")
        rh_done = sem("rh_done")
        o_sq = sem("o_sq")
        og_silu = sem("og_silu")
        og_used = sem("og_used")
        y_ready = sem("y_ready")
        p_hi = sem("p_hi")
        p_ready = sem("p_ready")
        qk_sq = sem("qk_sq")
        hs_done = sem("hs_done")
        hs_ready = sem("hs_ready")
        rb_done = sem("rb_done")
        qn_ready = sem("qn_ready")
        sc_done = sem("sc_done")
        sc_read = sem("sc_read")
        nm_ready = sem("nm_ready")
        e_ready = sem("e_ready")
        ln_ready = sem("ln_ready")
        lm_ready = sem("lm_ready")
        wexp = sem("wexp")
        pw_ready = sem("pw_ready")
        pt_done = sem("pt_done")
        pt_read = sem("pt_read")
        yc_done = sem("yc_done")
        v2_done = sem("v2_done")
        v2_read = sem("v2_read")
        wm_ready = sem("wm_ready")
        ya_done = sem("ya_done")
        ya_ready = sem("ya_ready")
        yb_ready = sem("yb_ready")

        N_CONST = 11
        block = ctx.enter_context(nc.Block())

        def wait(eng, s, n):
            if not isinstance(n, int) or n > 0:
                eng.wait_ge(s, n)

        def first_time(it):
            return isinstance(it, int) and it == 0

        def iterate(eng, n, body):
            body(0)
            if n > 1:
                with eng.Fori(1, n) as it:
                    body(it)

        tiles_before = {"qk": 16}
        n = 16
        for name in ("v", "og"):
            tiles_before[name] = n
        for name, made_before in (("gla_out", 16), ("ffn_in0", 16), ("ffn_out0", 24), ("ffn_in1", 0), ("ffn_out1", 20),
                                  ("ple_proj", 0), ("ple_gate", 16), ("in2", 16), ("out2", 16), ("mlp_in0", 16),
                                  ("mlp_out0", 32), ("mlp_in1", 0), ("mlp_out1", 32)):
            n += made_before
            tiles_before[name] = n
        prods = {"ffn_in0": 0, "ffn_in1": 24, "mlp_in0": 60, "mlp_in1": 92}
        norm_no = {"ffn_in0": 1, "ple_gate": 2, "in2": 3, "mlp_in0": 4}
        norm_at = {"qk": 0}

        @block.sync
        def _(sp):
            def turn(t):
                for c in range(RING // 2):
                    wait(sp, lo_ready, RING * (t - 1) + 2 * c + 2)
                    sp.dma_start(raw[:, 2 * c:2 * c + 2], A["stream"][RING // 2 * t + c]).then_inc(raw_loaded[c], 16)

            for dst, src in ((gains, "gains"), (ones, "ones"), (ident, "ident")):
                sp.dma_start(dst[:], A[src]).then_inc(consts, 16)
            sp.dma_start(h[:], A["x"]).then_inc(x_loaded, 16)
            iterate(sp, N_SLOTS // RING, turn)
            e0 = 2 * st["mlp_out1"].group0
            for j in range(DT):
                sp.wait_ge(evict_done, e0 + j + 1)
                sp.dma_start(out[:, j], h[:, j]).then_inc(out_stored, 16)
            sp.wait_ge(out_stored, 16 * DT)

        def y_tile(k):
            return 22 + k if k < 10 else 6 + k

        def causal3():
            return causal[:].rearrange("p (a i) -> p a i", a=1).broadcast_to([P, 8, P])

        @block.tensor
        def _(pe):
            def slot(n, r, kp, moving, banks, first, last):
                pe.wait_ge(lo_ready, n + 1)
                for a in range(2):
                    x = moving(2 * kp + a)
                    for b, bank in enumerate(banks):
                        w = slice(b * P, (b + 1) * P)
                        pe.matmul(ps[:, bank, :], w_hi[:, r, a, w], x.rearrange("p a t -> p (a t)"),
                                  start=first and a == 0, stop=last and a == 1, skip_group_check=True)
                        mm = pe.matmul(ps[:, bank, 0:T], w_lo[:, r, a, w], x[:, 0],
                                       start=False, stop=last and a == 1, skip_group_check=True)
                mm.then_inc(slots_used, 1)

            def groups(s, it, moving, needs=(), after_first=None, after=None):
                for u in range(s.u):
                    wait(pe, sum_done, 2 * (s.group0 + it * s.u + u - 1))
                    for kp in range(s.kp):
                        if first_time(it) and u == 0:
                            for at, s_, count in needs:
                                if at == kp:
                                    pe.wait_ge(s_, count)
                        local = u * s.kp + kp
                        slot(s.slot0 + it * s.body_slots + local, local % RING, kp, moving,
                             [2 * (u % 2), 2 * (u % 2) + 1], kp == 0, kp == s.kp - 1)
                    if first_time(it) and u == 0 and after_first is not None:
                        after_first()
                    if after is not None:
                        after(u)

            def stage(name, moving, needs=(), after_first=None):
                iterate(pe, st[name].iters, lambda it: groups(st[name], it, moving, needs, after_first))

            def norm(k, cols):
                def go():
                    pe.wait_ge(sq_added, k)
                    for c in range(cols):
                        mm = pe.matmul(ps[:, 4, c * T:(c + 1) * T], ones[:], sq_sum[:, c], start=True, stop=True,
                                       skip_group_check=True)
                    mm.then_inc(norm_sum, 1)
                return go

            pe.wait_ge(consts, 16 * N_CONST)
            pe.wait_ge(x_sq, 1)
            for j in range(DT):
                mm = pe.matmul(ps[:, 4, 0:T], ones[:], cum[:, j // 8, j % 8], start=j == 0, stop=j == DT - 1,
                               skip_group_check=True)
            mm.then_inc(norm_sum, 1)
            pe.wait_ge(tile_ready, 16)
            for kp in range(KP):
                slot(kp, kp, kp, lambda k: xs[:, k], [5], kp == 0, kp == KP - 1)
            groups(st["qk"], 0, lambda k: xs[:, k])
            pe.wait_ge(lr_ready, 1)
            for n in range(8):
                wait(pe, gk_read, n - 3)
                for c in range(2):
                    z, u = (2 * n + c) // GLA_U, (2 * n + c) % GLA_U
                    mm = pe.matmul(ps[:, 4 + n % 4, c * T:(c + 1) * T], w_up[:, z, u], lr_t[0:32], start=True,
                                   stop=True, skip_group_check=True)
                mm.then_inc(gk_done, 1)
            with pe.Fori(1, st["qk"].iters) as it:
                groups(st["qk"], it, lambda k: xs[:, k])

            def scores(lv):
                src, cross = qk if lv == 0 else qk_dec, lv == len(LEVELS)
                if lv:
                    pe.wait_ge(dec_ready, 2 * lv)
                for hp in range(2):
                    pe.wait_ge(s_read, 2 * lv + hp - 1) if lv else pe.wait_ge(gk_read, 8)
                    for hh in range(2):
                        for jt in range(2):
                            i_t = 1 - jt if cross else jt
                            for d in range(2):
                                u = 2 * (2 * hp + hh) + d
                                mm = pe.matmul(ps[:, 4 + hp, (2 * hh + jt) * P:(2 * hh + jt + 1) * P],
                                               src[:, 1, u, jt * P:(jt + 1) * P], src[:, 0, u, i_t * P:(i_t + 1) * P],
                                               start=d == 0, stop=d == 1, skip_group_check=True)
                    mm.then_inc(s_done, 1)

            def turn_v(g):
                pe.wait_ge(evict_done, 2 * (st["v"].group0 + g) + 2)
                pe.wait_ge(vt_read, g) if g else pe.wait_ge(gk_read, 8)
                for tt in range(2):
                    for b in range(2):
                        mm = pe.transpose(ps[:, 7, (2 * tt + b) * P:(2 * tt + b + 1) * P], scaled[:, b, tt * P:(tt + 1) * P],
                                          ident[:])
                mm.then_inc(vt_done, 1)

            for n in range(len(LEVELS)):
                def after(u, n=n):
                    if 1 <= 2 * n + u <= 8:
                        turn_v(2 * n + u - 1)
                    if n == 0 and u == 0:
                        pe.wait_ge(evict_done, 2 * st["v"].group0)
                        scores(0)
                    if u == 1:
                        scores(n + 1)
                groups(st["v" if n < 4 else "og"], n % 4, lambda k: xs[:, k], after=after)
            pe.wait_ge(vt_read, 8)
            pe.wait_ge(s_read, 18)
            for n in range(8):
                wait(pe, o_read, n - 3)
                for c in range(2):
                    dv = 2 * n + c
                    for jt in range(2):
                        mm = pe.matmul(ps[:, 4 + n % 4, c * T:(c + 1) * T], v_nat[:, jt, dv * P:(dv + 1) * P],
                                       a_t[:, dv // DV_T, 2 * jt:2 * jt + 2].rearrange("p a i -> p (a i)"),
                                       start=jt == 0, stop=jt == 1, skip_group_check=True)
                mm.then_inc(o_done, 1)
            pe.wait_ge(sum_done, 2 * st["gla_out"].group0)
            for hd in range(GLA_H):
                pe.wait_ge(o_sq, 2 * hd + 2)
                for tt in range(2):
                    for d in range(DV_T):
                        n = hd * DV_T + d
                        mm = pe.matmul(ps[:, 0, tt * GLA_H + hd:tt * GLA_H + hd + 1],
                                       qk[:, n // 8, n % 8, tt * P:(tt + 1) * P], ones[:, 0:1], start=d == 0,
                                       stop=d == DV_T - 1, skip_group_check=True)
            mm.then_inc(norm_sum, 1)
            pe.wait_ge(o_read, 8)
            pe.wait_ge(rh_ready, 1)
            for hd in range(GLA_H):
                for tt in range(2):
                    mm = pe.matmul(ps[:, 4 + hd // 2, (hd % 2) * T + tt * P:(hd % 2) * T + (tt + 1) * P],
                                   rh_wide[:, tt * GLA_H + hd], ident[:], start=True, stop=True, skip_group_check=True)
            mm.then_inc(rh_done, 1)
            tb = tiles_before
            stage("gla_out", lambda k: acts[:, k], [(2 * hd, tile_ready, tb["gla_out"] - 12 + 4 * hd) for hd in range(GLA_H)])
            stage("ffn_in0", lambda k: xs[:, k],
                  [(0, tile_ready, tb["ffn_in0"] - 2), (KP - 1, tile_ready, tb["ffn_in0"])], norm(16, 1))
            for n in range(2):
                s = st[f"ffn_out{n}"]
                if n:
                    stage("ffn_in1", lambda k: xs[:, k])
                stage(s.name, lambda k: acts[:, k],
                      [(0, tile_ready, tb[s.name] - 2), (s.kp - 1, tile_ready, tb[s.name])])
            s = st["ple_proj"]
            pe.wait_ge(p_ready, 1)
            for g in range(8):
                pe.wait_ge(sum_done, 2 * (s.group0 + g - 1))
                slot(s.slot0 + g, g, 0, lambda k: p_split[:, k], [2 * (g % 2), 2 * (g % 2) + 1], True, True)
            stage("ple_gate", lambda k: xs[:, k], [(0, tile_ready, tb["ple_gate"])], norm(32, 1))
            stage("in2", lambda k: acts[:, k],
                  [(0, tile_ready, tb["in2"] - 2), (KP - 1, tile_ready, tb["in2"])], norm(48, 2))

            pe.wait_ge(qk_sq, 1)
            for tt in range(2):
                for j in range(12):
                    mm = pe.matmul(ps[:, 4, tt * 24 + 2 * j:tt * 24 + 2 * j + 2], sq_qk[:, j, tt * P:(tt + 1) * P],
                                   head_pair[:], start=True, stop=True, skip_group_check=True)
            mm.then_inc(hs_done, 1)
            for n in range(5):
                wait(pe, v2_read, n - 2)
                for c in range(4):
                    j, tt = (4 * n + c) % 10, (4 * n + c) // 10
                    mm = pe.transpose(ps[:, 5 + n % 3, c * P:(c + 1) * P], proj[:, V0 + j, tt * P:(tt + 1) * P], ident[:])
                mm.then_inc(v2_done, 1)
            pe.wait_ge(hs_ready, 1)
            pe.wait_ge(v2_read, 5)
            for n in range(6):
                wait(pe, qn_ready, 2 * (n - 3))
                for c in range(2):
                    j = 2 * n + c
                    for tt in range(2):
                        r = r_wide[:, tt, 2 * j:2 * j + 2].rearrange("p a b -> p (a b)")
                        mm = pe.matmul(ps[:, 4 + n % 4, c * T + tt * P:c * T + (tt + 1) * P],
                                       r, ident[:],
                                       start=True, stop=True, skip_group_check=True)
                mm.then_inc(rb_done, 1)
            pe.wait_ge(qn_ready, 12)
            for hd in range(C_H):
                wait(pe, sc_read, 2 * (hd - 3))
                j, rows = hd // 2, slice(HD * (hd % 2), HD * (hd % 2) + HD)
                for tt in range(2):
                    mm = pe.matmul(ps[:, 4 + hd % 4, tt * T:(tt + 1) * T], proj[rows, Q0 + j, tt * P:(tt + 1) * P],
                                   proj[rows, K0 + j], start=True, stop=True, skip_group_check=True)
                mm.then_inc(sc_done, 1)
            pe.wait_ge(wm_ready, 1)
            pe.wait_ge(sum_done, 2 * st["out2"].group0)
            for n in range(4):
                for c in range(2):
                    mm = pe.matmul(ps[:, n, c * T:(c + 1) * T], v2_nat[:, c, 768 + n * P:768 + (n + 1) * P],
                                   sgu_wt[:, 2 * n:2 * n + 2].rearrange("p a i -> p (a i)"), start=True, stop=True,
                                   skip_group_check=True)
                mm.then_inc(ya_done, 1)
            pe.wait_ge(sc_read, 24)
            for hd in range(C_H + 1):
                if hd < C_H:
                    pe.wait_ge(pw_ready, 2 * (hd + 1))
                    wait(pe, pt_read, hd - 1)
                    for s_ in range(2):
                        for tt in range(2):
                            mm = pe.transpose(ps[:, 4 + hd % 2, s_ * T + tt * P:s_ * T + (tt + 1) * P],
                                              prob[:, hd, tt, s_ * P:(s_ + 1) * P], ident[:])
                    mm.then_inc(pt_done, 1)
                if hd:
                    g = hd - 1
                    pe.wait_ge(pt_read, g + 1)
                    wait(pe, tile_ready, (tb["in2"] + g // 2 - 1) if g // 2 >= 2 else 0)
                    for s_ in range(2):
                        mm = pe.matmul(ps[HD * (g % 2):HD * (g % 2) + HD, 6 + (g // 2) % 2, 0:T],
                                       v2_nat[:, s_, g * HD:(g + 1) * HD], prob_t[:, g % 2, s_], start=s_ == 0,
                                       stop=s_ == 1, skip_group_check=True)
                    mm.then_inc(yc_done, 1)

            stage("out2", lambda k: acts[:, y_tile(k)], [(0, tile_ready, tb["out2"])])
            stage("mlp_in0", lambda k: xs[:, k],
                  [(0, tile_ready, tb["mlp_in0"] - 2), (KP - 1, tile_ready, tb["mlp_in0"])], norm(64, 1))
            for n in range(2):
                s = st[f"mlp_out{n}"]
                if n:
                    stage("mlp_in1", lambda k: xs[:, k])
                stage(s.name, lambda k: acts[:, k],
                      [(0, tile_ready, tb[s.name] - 2), (s.kp - 1, tile_ready, tb[s.name])])

        hidden = {"ffn_in0": "swiglu", "ffn_in1": "swiglu", "mlp_in0": "relu2", "mlp_in1": "relu2"}
        residual = {"gla_out": (0, 1), "ffn_out1": (16, 2), "out2": (48, 5)}

        def tile_no(s, it, u, b):
            return 2 * (s.group0 + it * s.u + u) + b

        def tile_of(s, it, u, b):
            if hidden.get(s.name) == "swiglu":
                return 2 * (it * (s.u // 2) + u // 2) + b
            return 2 * (it * s.u + u) + b

        def slots_body(s, it, split, finish, before, extra=None):
            for u in range(s.u):
                for kp in range(s.kp):
                    local = u * s.kp + kp
                    split(s.slot0 + it * s.body_slots + local, local % RING,
                          s.slot0 // RING + it * (s.body_slots // RING) + local // RING)
                    if 4 <= kp < 8:
                        if u > 0:
                            finish(s, it, u - 1, kp - 4)
                        elif not first_time(it):
                            finish(s, it - 1, s.u - 1, kp - 4)
                        elif before is not None:
                            finish(before, before.iters - 1, before.u - 1, kp - 4)
                    if extra is not None:
                        extra(u, kp)

        def slots_loop(eng, s, split, finish, before, extra=None):
            iterate(eng, s.iters, lambda it: slots_body(s, it, split, finish, before, extra if first_time(it) else None))

        @block.scalar
        def _(act):
            def split(n, r, turn):
                if r % 2 == 0:
                    act.wait_ge(raw_loaded[r // 2], 16 * (turn + 1))
                wait(act, slots_used, n - RING + 1)
                act.activation(w_hi[:, r], raw[:, r], ACT.Copy).then_inc(hi_ready, 1)

            def second(s, it, u, b):
                e, j = tile_no(s, it, u, b), tile_of(s, it, u, b)
                kind = hidden.get(s.name)
                if kind == "swiglu" and u % 2 == 0:
                    act.wait_ge(evict_done, e + 1)
                    act.activation(act_gate[:, b], scaled[:, b], ACT.Silu).then_inc(silu_done, 1)
                elif kind:
                    act.wait_ge(prod_done, prods[s.name] + j + 1)
                    act.wait_ge(consts, 16 * N_CONST)
                    act.activation(acts[:, j, 0], prod[:, b], ACT.Copy).then_inc(x_hi_ready, 1)
                elif s.name in residual:
                    added, gain = residual[s.name]
                    act.wait_ge(evict_done, e + 1)
                    wait(act, sq_added, added + j - 1)
                    act.wait_ge(consts, 16 * N_CONST)
                    act.activation(sq[:, b, 0], h[:, j], ACT.Square).then_inc(sq_ready, 1)
                    act.activation(xs[:, j, 0], h[:, j], ACT.Copy, scale=gains[:, gain, j]).then_inc(x_hi_ready, 1)
                elif s.name == "ple_gate":
                    act.wait_ge(evict_done, e + 1)
                    act.activation(act_gate[:, b], scaled[:, b], ACT.Sigmoid).then_inc(silu_done, 1)

            def third(s, it, u, b):
                if s.name == "ple_gate":
                    j = tile_of(s, it, u, b)
                    act.wait_ge(h_done, j + 1)
                    wait(act, sq_added, 32 + j - 1)
                    act.wait_ge(consts, 16 * N_CONST)
                    act.activation(sq[:, b, 0], h[:, j], ACT.Square)
                    act.activation(sq[:, b, 1], h[:, j], ACT.Square, scale=gains[:, 3, j]).then_inc(sq_ready, 1)
                    act.activation(acts[:, j, 0], h[:, j], ACT.Copy, scale=gain_fa[:, j]).then_inc(x_hi_ready, 1)

            def halves(s, it, u, b):
                act.wait_ge(slots_used, s.slot0 + (it * s.u + u + 1) * s.kp)
                wait(act, sum_done, tile_no(s, it, u, b) - 1)
                act.activation(half[:, b], ps[:, 2 * (u % 2) + b, T:2 * T], ACT.Copy).then_inc(half_ready, 1)

            def finish(s, it, u, step):
                if step < 2:
                    halves(s, it, u, step)
                if 1 <= step < 3:
                    second(s, it, u, step - 1)
                if step >= 2:
                    third(s, it, u, step - 2)

            def square_root(n):
                act.wait_ge(norm_ms, n)
                act.activation(root[:], ms[:], ACT.Sqrt).then_inc(norm_root, 1)

            def stage(name, before, extra=None):
                slots_loop(act, st[name], split, finish, st[before] if before else None, extra)

            def yc_split(j):
                act.wait_ge(yc_done, 2 * j + 2)
                act.activation(acts[:, 16 + j, 0], ps[:, 6 + j % 2, 0:T], ACT.Copy).then_inc(x_hi_ready, 1)

            for dst, src in ((b_gate, "b_gate"), (out_gain, "out_gain"), (masks, "masks"), (w_up, "w_up"),
                             (causal, "causal"), (head_pair, "head_pair"), (qk_gain, "qk_gain"), (conv_w, "conv_w")):
                act.dma_start(dst[:], A[src]).then_inc(consts, 16)
            act.wait_ge(x_loaded, 16)
            act.wait_ge(consts, 16 * N_CONST)
            act.activation(cum[:], h[:].rearrange("p (a b) t -> p a b t", a=2), ACT.Square).then_inc(x_sq, 1)
            for j in range(DT):
                act.activation(xs[:, j, 0], h[:, j], ACT.Copy, scale=gains[:, 0, j]).then_inc(x_hi_ready, 1)
            square_root(1)
            for r in range(RING):
                split(r, r, 0)

            def during_qk(it, u, kp):
                if (it, u, kp) == (0, 0, 4):
                    act.wait_ge(slots_used, RING)
                    act.activation(half[:, 0], ps[:, 5, T:2 * T], ACT.Copy).then_inc(lr_half, 1)
                if it == 2 and kp == 2:
                    act.wait_ge(ls_step, u + 1)
                    act.activation(dec[:, u], dec[:, u], ACT.Exp, scale=-1.0).then_inc(act_step, 1)
                if it == 2 and kp == 3:
                    act.wait_ge(act_step, u + 1)
                    act.activation(dec[:, u], dec[:, u], ACT.Ln, bias=1.0).then_inc(ls_ready, 1)

            def during_v_og(n, u, kp):
                if u == 0 and kp in (3, 6):
                    part = 0 if kp == 3 else 1
                    act.wait_ge(dec_arg, 2 * n + part + 1)
                    act.activation(dec[:, part], dec[:, part], ACT.Exp, scale=1.0 / 16).then_inc(dec_exp, 1)
                g = 2 * n + u - 2
                if kp == 7 and 0 <= g < 8:
                    act.wait_ge(vt_done, g + 1)
                    act.activation(v_nat[:, :, 2 * g * P:(2 * g + 2) * P],
                                   ps[:, 7].rearrange("p (a c) -> p a c", a=2), ACT.Copy).then_inc(vt_read, 1)

            for it in range(4):
                slots_body(st["qk"], it, split, finish, None, lambda u, kp: during_qk(it, u, kp))
            for n in range(len(LEVELS)):
                name, before = ("v", "qk") if n < 4 else ("og", "v")
                slots_body(st[name], n % 4, split, finish, st[before], lambda u, kp: during_v_og(n, u, kp))
            for step in range(4):
                finish(st["og"], st["og"].iters - 1, 1, step)
            act.wait_ge(evict_done, 2 * st["gla_out"].group0)
            act.activation(h[:], h[:], ACT.Silu).then_inc(og_silu, 1)
            for n in range(8):
                act.wait_ge(o_read, n + 1)
                o2 = qk_dec[:].rearrange("p a b t -> p (a b) t")[:, 2 * n:2 * n + 2]
                act.activation(qk[:].rearrange("p a b t -> p (a b) t")[:, 2 * n:2 * n + 2], o2, ACT.Square).then_inc(o_sq, 1)
            act.wait_ge(norm_ms, 2)
            act.activation(small[:, 2, 0:8], small[:, 1, 0:8], ACT.Sqrt).then_inc(norm_root, 1)
            y = qk_dec[:].rearrange("p a b t -> p (a b) t")
            for hd in range(GLA_H):
                tiles = slice(hd * DV_T, (hd + 1) * DV_T)
                act.wait_ge(y_ready, hd + 1)
                act.activation(acts[:, tiles, 0], y[:, tiles], ACT.Copy).then_inc(x_hi_ready, 4)
            act.wait_ge(og_used, 4)
            act.dma_start(h[:], A["x"]).then_inc(x_again, 16)
            stage("gla_out", None)
            stage("ffn_in0", "gla_out", lambda u, kp: square_root(3) if (u, kp) == (1, 1) else None)
            act.dma_start(p_raw[:], A["p"]).then_inc(late_consts, 16)
            stage("ffn_out0", "ffn_in0")
            act.wait_ge(late_consts, 16)
            act.activation(p_split[:, :, 0], p_raw[:], ACT.Copy).then_inc(p_hi, 1)
            stage("ffn_in1", "ffn_out0")
            stage("ffn_out1", "ffn_in1")
            s, before = st["ple_proj"], st["ffn_out1"]
            for g in range(8):
                split(s.slot0 + g, g, s.slot0 // RING)
                if g == 1:
                    for step in range(4):
                        finish(before, before.iters - 1, before.u - 1, step)
                if g >= 2:
                    halves(s, 0, g - 2, 0)
                    halves(s, 0, g - 2, 1)
            for g in (6, 7):
                halves(s, 0, g, 0)
                halves(s, 0, g, 1)
            stage("ple_gate", None, lambda u, kp: square_root(4) if (u, kp) == (1, 1) else None)
            stage("in2", "ple_gate", lambda u, kp: square_root(4 + kp) if u == 1 and kp in (1, 2) else None)
            for step in range(4):
                finish(st["in2"], st["in2"].iters - 1, 0 + st["in2"].u - 1, step)

            act.wait_ge(slots_used, st["out2"].slot0)
            for dst, src in ((amask, "amask"), (bias_a, "bias_a"), (sgu_wt, "sgu_wt")):
                act.dma_start(dst[:], A[src]).then_inc(late_consts, 16)
            act.wait_ge(evict_done, 2 * (st["in2"].group0 + 6))
            act.activation(sq_qk[:], proj[:, Q0:V0], ACT.Square).then_inc(qk_sq, 1)
            act.wait_ge(norm_ms, 7)
            act.activation(small[:, 2], small[:, 1], ACT.Sqrt).then_inc(norm_root, 1)
            for hd in range(C_H):
                for tt in range(2):
                    i = 2 * hd + tt
                    act.wait_ge(nm_ready, i + 1)
                    act.activation(prob[:, hd, tt], prob[:, hd, tt], ACT.Exp, bias=small[:, 1, i:i + 1],
                                   accum_out=small[:, 2, i:i + 1]).then_inc(e_ready, 1)
            act.wait_ge(e_ready, 24)
            act.activation(small[:, 3, 0:24], small[:, 2, 0:24], ACT.Ln).then_inc(ln_ready, 1)
            act.wait_ge(lm_ready, 1)
            act.activation(small[:, 4, 0:24], small[:, 4, 0:24], ACT.Exp).then_inc(wexp, 1)
            for hd in range(C_H):
                act.wait_ge(pt_done, hd + 1)
                wait(act, yc_done, hd - 1)
                act.activation(prob_t[:, hd % 2], ps[:, 4 + hd % 2].rearrange("p (a t) -> p a t", a=2), ACT.Copy)\
                    .then_inc(pt_read, 1)
                if hd % 2 == 1 and hd >= 3:
                    yc_split(hd // 2 - 1)
            yc_split(5)
            act.wait_ge(ya_ready, 1)
            act.activation(acts[:, 22:26, 0], proj[:, AU0:AU0 + 4], ACT.Copy).then_inc(x_hi_ready, 4)
            act.wait_ge(yb_ready, 1)
            act.wait_ge(tile_ready, tiles_before["in2"] + 10)
            act.activation(acts[:, 26:32, 0], proj[:, BB0:BB0 + 6], ACT.Copy).then_inc(x_hi_ready, 6)
            stage("out2", None)
            stage("mlp_in0", "out2", lambda u, kp: square_root(8) if (u, kp) == (1, 1) else None)
            stage("mlp_out0", "mlp_in0")
            stage("mlp_in1", "mlp_out0")
            stage("mlp_out1", "mlp_in1")
            for step in range(2):
                finish(st["mlp_out1"], st["mlp_out1"].iters - 1, 1, step)

        @block.gpsimd
        def _(pool):
            def add_up(done, cols, norms):
                if norms:
                    pool.wait_ge(norm_sum, norms)
                pool.memset(sq_sum[:, 0:cols], 0.0).then_inc(sq_step, 1)
                pool.wait_ge(sq_step, len(done_norms) + 1)
                done_norms.append(done)

                def two(i):
                    for b in range(2):
                        k = done + i * 2 + b
                        pool.wait_ge(sq_ready, k + 1)
                        wait(pool, sq_added, k)
                        pool.tensor_tensor(sq_sum[:, 0:cols], sq_sum[:, 0:cols], sq[:, b, 0:cols], ALU.add)\
                            .then_inc(sq_added, 1)
                iterate(pool, DT // 2, two)

            done_norms = []
            add_up(0, 1, 2)
            add_up(16, 1, 3)
            add_up(32, 2, 4)
            add_up(48, 1, 5)

        @block.vector
        def _(dve):
            steps = [0]

            def link(ins):
                steps[0] += 1
                ins.then_inc(dve_step, 1)
                dve.wait_ge(dve_step, steps[0])

            def split(n, r, turn):
                dve.wait_ge(hi_ready, n + 1)
                dve.tensor_tensor(w_lo[:, r], raw[:, r], w_hi[:, r].bitcast(F32), ALU.subtract).then_inc(lo_ready, 1)

            def add_halves(s, it, u, b):
                e = tile_no(s, it, u, b)
                dve.wait_ge(half_ready, e + 1)
                wait(dve, evict_done, e - 1)
                dve.tensor_tensor(total[:, b], ps[:, 2 * (u % 2) + b, 0:T], half[:, b], ALU.add).then_inc(sum_done, 1)
                dve.wait_ge(sum_done, e + 1)
                return e

            targets = {"qk": qk, "v": None, "og": h}

            def first(s, it, u, b):
                e, j, name = add_halves(s, it, u, b), tile_of(s, it, u, b), s.name
                if name == "v":
                    wait(dve, vt_done, j // 2)
                    dve.tensor_tensor(scaled[:, b], total[:, b], rs[:], ALU.mult).then_inc(evict_done, 1)
                elif name in targets:
                    t = targets[name]
                    flat = t[:] if name == "og" else t[:].rearrange("p a b t -> p (a b) t")
                    dve.tensor_tensor(flat[:, j], total[:, b], rs[:], ALU.mult).then_inc(evict_done, 1)
                elif name == "in2":
                    dve.tensor_tensor(proj[:, j], total[:, b], rs[:], ALU.mult).then_inc(evict_done, 1)
                elif name == "ple_proj":
                    dve.tensor_copy(ple_val[:, j], total[:, b]).then_inc(evict_done, 1)
                elif hidden.get(name) == "swiglu" and u % 2 == 0:
                    dve.tensor_tensor(scaled[:, b], total[:, b], rs[:], ALU.mult).then_inc(evict_done, 1)
                elif hidden.get(name) == "swiglu":
                    dve.tensor_tensor(gate[:, b], total[:, b], rs[:], ALU.mult).then_inc(evict_done, 1)
                    dve.wait_ge(evict_done, e + 1)
                    dve.wait_ge(silu_done, prods[name] + j + 1)
                    wait(dve, tile_ready, tiles_in(name) + j - 1)
                    dve.tensor_tensor(prod[:, b], gate[:, b], act_gate[:, b], ALU.mult).then_inc(prod_done, 1)
                elif hidden.get(name) == "relu2":
                    dve.tensor_tensor(scaled[:, b], total[:, b], rs[:], ALU.mult).then_inc(evict_done, 1)
                    dve.wait_ge(evict_done, e + 1)
                    wait(dve, tile_ready, tiles_in(name) + j - 1)
                    dve.scalar_tensor_tensor(out=prod[:, b], in0=scaled[:, b], scalar=0.0, in1=scaled[:, b],
                                             op0=ALU.max, op1=ALU.mult).then_inc(prod_done, 1)
                elif name == "ple_gate":
                    dve.tensor_tensor(scaled[:, b], total[:, b], rs[:], ALU.mult).then_inc(evict_done, 1)
                elif name == "out2":
                    dve.scalar_tensor_tensor(out=scaled[:, b], in0=h[:, j], scalar=gains[:, 3, j],
                                             in1=rs_final[:], op0=ALU.mult, op1=ALU.mult).then_inc(h_done, 1)
                    dve.wait_ge(h_done, 16 + j + 1)
                    dve.tensor_tensor(h[:, j], scaled[:, b], total[:, b], ALU.add).then_inc(evict_done, 1)
                else:
                    dve.tensor_tensor(h[:, j], h[:, j], total[:, b], ALU.add).then_inc(evict_done, 1)

            def tiles_in(name):
                return tiles_before[name]

            def then(s, it, u, b):
                e, j = tile_no(s, it, u, b), tile_of(s, it, u, b)
                kind = hidden.get(s.name)
                if kind == "swiglu" and u % 2 == 0:
                    return
                if kind:
                    dve.wait_ge(x_hi_ready, tiles_in(s.name) + j + 1)
                    dve.tensor_tensor(acts[:, j, 1], prod[:, b], acts[:, j, 0].bitcast(F32), ALU.subtract)\
                        .then_inc(tile_ready, 1)
                elif s.name in residual:
                    dve.wait_ge(x_hi_ready, tiles_in(s.name) + j + 1)
                    dve.scalar_tensor_tensor(out=xs[:, j, 1], in0=h[:, j], scalar=gains[:, residual[s.name][1], j],
                                             in1=xs[:, j, 0].bitcast(F32), op0=ALU.mult, op1=ALU.subtract)\
                        .then_inc(tile_ready, 1)
                elif s.name == "ple_gate":
                    dve.wait_ge(silu_done, 44 + j + 1)
                    dve.tensor_tensor(prod[:, b], act_gate[:, b], ple_val[:, j], ALU.mult).then_inc(prod_done, 1)
                    dve.wait_ge(prod_done, 44 + j + 1)
                    dve.tensor_tensor(h[:, j], h[:, j], prod[:, b], ALU.add).then_inc(h_done, 1)

            def last(s, it, u, b):
                if s.name == "ple_gate":
                    j = tile_of(s, it, u, b)
                    dve.wait_ge(x_hi_ready, tiles_in(s.name) + j + 1)
                    dve.scalar_tensor_tensor(out=acts[:, j, 1], in0=h[:, j], scalar=gain_fa[:, j],
                                             in1=acts[:, j, 0].bitcast(F32), op0=ALU.mult, op1=ALU.subtract)\
                        .then_inc(tile_ready, 1)

            def finish(s, it, u, step):
                if step < 2:
                    first(s, it, u, step)
                else:
                    then(s, it, u, step - 2)
                if step == 3:
                    last(s, it, u, 0)
                    last(s, it, u, 1)

            def stage(name, before, extra=None):
                slots_loop(dve, st[name], split, finish, st[before] if before else None, extra)

            def newton(out_, r, x, tmp):
                link(dve.reciprocal(out_, r))
                link(dve.tensor_tensor(tmp, out_, out_, ALU.mult))
                link(dve.tensor_tensor(tmp, tmp, x, ALU.mult))
                link(dve.tensor_scalar(tmp, tmp, -0.5, 1.5, ALU.mult, ALU.add))
                link(dve.tensor_tensor(out_, out_, tmp, ALU.mult))

            def norm_begin(k):
                dve.wait_ge(norm_sum, k)
                dve.tensor_scalar(ms[:], ps[:, 4, 0:T], 1.0 / D, EPS, ALU.mult, ALU.add).then_inc(norm_ms, 1)

            def norm_end(k, dst):
                dve.wait_ge(norm_root, k)
                newton(dst, root[:], ms[:], newt[:])

            def norm_hook(k, sums=None):
                def go(u, kp):
                    if (u, kp) == (1, 0):
                        norm_begin(sums or k)
                    if (u, kp) == (1, 2):
                        norm_end(k, rs[:])
                return go

            dve.wait_ge(consts, 16 * N_CONST)
            link(dve.tensor_tensor(gain_fa[:], gains[:, 3], gains[:, 4], ALU.mult))
            for j in range(DT):
                dve.wait_ge(x_hi_ready, j + 1)
                dve.scalar_tensor_tensor(out=xs[:, j, 1], in0=h[:, j], scalar=gains[:, 0, j],
                                         in1=xs[:, j, 0].bitcast(F32), op0=ALU.mult, op1=ALU.subtract)\
                    .then_inc(tile_ready, 1)
            norm_begin(1)
            norm_end(1, rs[:])
            for r in range(RING):
                split(r, r, 0)

            cumf = cum[:].rearrange("p a b t -> p (a b) t")
            bgf = b_gate[:].rearrange("p a b -> p (a b)")

            def during_qk(it, u, kp):
                if (it, u, kp) == (0, 0, 4):
                    dve.wait_ge(lr_half, 1)
                    link(dve.tensor_tensor(total[:, 0], ps[:, 5, 0:T], half[:, 0], ALU.add))
                    dve.tensor_tensor(lr_t[:], total[:, 0], rs[:], ALU.mult).then_inc(lr_ready, 1)
                    dve.wait_ge(lr_ready, 1)
                if it == 1 and kp < 4:
                    n = 4 * u + kp
                    dve.wait_ge(gk_done, n + 1)
                    for c in range(2):
                        ins = dve.tensor_scalar(cumf[:, 2 * n + c], ps[:, 4 + n % 4, c * T:(c + 1) * T],
                                                bgf[:, 2 * n + c:2 * n + c + 1], None, ALU.add)
                    ins.then_inc(gk_read, 1)
                if it == 2 and kp == 1:
                    dve.wait_ge(gk_read, 8)
                    dve.scalar_tensor_tensor(out=dec[:, u], in0=cum[:, u], scalar=-1.0, in1=cum[:, u], op0=ALU.mult,
                                             op1=ALU.max).then_inc(ls_step, 1)
                if it == 3 and kp == 0:
                    dve.wait_ge(ls_ready, u + 1)
                    link(dve.scalar_tensor_tensor(out=dec[:, u], in0=cum[:, u], scalar=0.0, in1=dec[:, u], op0=ALU.min,
                                                  op1=ALU.subtract))
                    if u == 0:
                        link(dve.memset(qk_dec[:, 0, 0], 1.0))
                    else:
                        link(dve.memset(cum[:, 1, :, 0:1], 0.0))
                if it == 3 and kp in (1, 2, 3, 7):
                    for c in range(2 * (min(kp, 4) - 1), 2 * min(kp, 4)):
                        if u == 0:
                            ins = dve.tensor_tensor_scan(cum[:, 0, c], qk_dec[:, 0, 0], dec[:, 0, c], 0.0, ALU.mult, ALU.add)
                        else:
                            ins = dve.tensor_tensor_scan(cum[:, 1, c, 1:T], qk_dec[:, 0, 0, 1:T], dec[:, 1, c, 0:T - 1],
                                                         0.0, ALU.mult, ALU.add)
                    link(ins)

            def scores_out(lv):
                for hp in range(2):
                    dve.wait_ge(s_done, 2 * lv + hp + 1)
                    wait(dve, s_read, 2 * lv + hp)
                    for hh in range(2):
                        hd = 2 * hp + hh
                        src = ps[:, 4 + hp, hh * T:(hh + 1) * T].rearrange("p (a i) -> p a i", a=2)
                        if lv == 0:
                            ins = dve.tensor_scalar(a_t[:, hd, 0:4:3], src, 2.0, None, ALU.mult)
                        elif lv < len(LEVELS):
                            mask = masks[:, lv - 1:lv].bitcast(U32).broadcast_to([P, 2, P])
                            ins = dve.copy_predicated(a_t[:, hd, 0:4:3], mask, src)
                        else:
                            ins = dve.tensor_copy(a_t[:, hd, 1:3], src)
                    ins.then_inc(s_read, 1)

            def during_v_og(n, u, kp):
                s = LEVELS[n]

                def cut(x):
                    return x.rearrange("p u (n b s) -> p (u n) b s", b=2, s=s)
                pairs = GLA_U * T // (2 * s)
                f, b, dq, dk = cut(cum[:, 0]), cut(cum[:, 1]), cut(dec[:, 0]), cut(dec[:, 1])
                ref_f = f[:, :, 0, s - 1:s].broadcast_to([P, pairs, s])
                ref_b = b[:, :, 1, 0:1].broadcast_to([P, pairs, s])
                if (u, kp) == (0, 0):
                    wait(dve, dec_ready, 2 * n)
                    dve.tensor_tensor(dq[:, :, 1], f[:, :, 1], ref_f, ALU.subtract)
                if (u, kp) == (0, 1):
                    dve.tensor_tensor(dq[:, :, 0], ref_b, b[:, :, 0], ALU.subtract).then_inc(dec_arg, 1)
                if (u, kp) == (0, 2):
                    dve.tensor_tensor(dk[:, :, 0], ref_f, f[:, :, 0], ALU.subtract)
                if (u, kp) == (0, 3):
                    dve.tensor_tensor(dk[:, :, 1], b[:, :, 1], ref_b, ALU.subtract).then_inc(dec_arg, 1)
                if (u, kp) == (0, 7) and n:
                    scores_out(n)
                if u == 1 and kp in (0, 2):
                    part = kp // 2
                    if n == 0:
                        dve.wait_ge(evict_done, 2 * st["v"].group0)
                    dve.wait_ge(dec_exp, 2 * n + part + 1)
                    dve.tensor_tensor(qk_dec[:, part], qk[:, part], dec[:, part], ALU.mult).then_inc(dec_ready, 1)
                if (u, kp) == (1, 3) and n == 0:
                    scores_out(0)

            for it in range(4):
                slots_body(st["qk"], it, split, finish, None, lambda u, kp: during_qk(it, u, kp))
            for n in range(len(LEVELS)):
                name, before = ("v", "qk") if n < 4 else ("og", "v")
                slots_body(st[name], n % 4, split, finish, st[before], lambda u, kp: during_v_og(n, u, kp))
            for step in range(4):
                finish(st["og"], st["og"].iters - 1, 1, step)
            scores_out(len(LEVELS))
            o = qk_dec[:].rearrange("p a b t -> p (a b) t")
            for n in range(8):
                dve.wait_ge(o_done, n + 1)
                dve.tensor_scalar(o[:, 2 * n:2 * n + 2], ps[:, 4 + n % 4].rearrange("p (a t) -> p a t", a=2),
                                  1.0 / 16, None, ALU.mult).then_inc(o_read, 1)
            dve.wait_ge(og_silu, 1)
            dve.wait_ge(o_sq, 8)
            dve.wait_ge(o_read, 8)
            o4 = o.rearrange("p (a b) t -> p a b t", b=DV_T)
            og4 = h[:].rearrange("p (a b) t -> p a b t", b=DV_T)
            for d in range(DV_T):
                dve.scalar_tensor_tensor(out=o4[:, :, d], in0=o4[:, :, d], scalar=out_gain[:, d:d + 1],
                                         in1=og4[:, :, d], op0=ALU.mult, op1=ALU.mult).then_inc(og_used, 1)
                if d == 0:
                    dve.wait_ge(norm_sum, 2)
                    dve.tensor_scalar(small[:, 1, 0:8], ps[:, 0, 0:8], 1.0 / 512, EPS, ALU.mult, ALU.add).then_inc(norm_ms, 1)
                if d == 2:
                    dve.wait_ge(norm_root, 2)
                    newton(small[:, 0, 0:8], small[:, 2, 0:8], small[:, 1, 0:8], small[:, 3, 0:8])
                    rh = small[:, 0, 0:8].rearrange("p (a b) -> p a b", b=1)
                    dve.tensor_copy(rh_wide[:], rh.broadcast_to([P, 8, P])).then_inc(rh_ready, 1)
            dve.wait_ge(og_used, 4)
            dve.wait_ge(rh_done, 1)
            for hd in range(GLA_H):
                tiles = slice(hd * DV_T, (hd + 1) * DV_T)
                r = ps[:, 4 + hd // 2, (hd % 2) * T:(hd % 2 + 1) * T].rearrange("p (a t) -> p a t", a=1)
                dve.tensor_tensor(o[:, tiles], o[:, tiles], r.broadcast_to([P, DV_T, T]), ALU.mult).then_inc(y_ready, 1)
            for hd in range(GLA_H):
                tiles = slice(hd * DV_T, (hd + 1) * DV_T)
                dve.wait_ge(x_hi_ready, 16 + 4 * hd + 4)
                dve.tensor_tensor(acts[:, tiles, 1], o[:, tiles], acts[:, tiles, 0].bitcast(F32), ALU.subtract)\
                    .then_inc(tile_ready, 4)
            dve.wait_ge(x_again, 16)
            stage("gla_out", None)
            stage("ffn_in0", "gla_out", norm_hook(3))
            stage("ffn_out0", "ffn_in0")
            dve.wait_ge(p_hi, 1)
            dve.tensor_tensor(p_split[:, :, 1], p_raw[:], p_split[:, :, 0].bitcast(F32), ALU.subtract).then_inc(p_ready, 1)
            stage("ffn_in1", "ffn_out0")
            stage("ffn_out1", "ffn_in1")
            s, before = st["ple_proj"], st["ffn_out1"]
            for g in range(8):
                split(s.slot0 + g, g, s.slot0 // RING)
                if g == 1:
                    for step in range(4):
                        finish(before, before.iters - 1, before.u - 1, step)
                if g >= 2:
                    first(s, 0, g - 2, 0)
                    first(s, 0, g - 2, 1)
            for g in (6, 7):
                first(s, 0, g, 0)
                first(s, 0, g, 1)
            stage("ple_gate", None, norm_hook(4))

            def two_norms(u, kp):
                if (u, kp) == (1, 0):
                    norm_begin(5)
                if (u, kp) == (1, 2):
                    norm_end(5, rs_final[:])
                    link(dve.tensor_tensor(ms[:], rs_final[:], rs_final[:], ALU.mult))
                    link(dve.tensor_tensor(ms[:], ms[:], ps[:, 4, T:2 * T], ALU.mult))
                    dve.tensor_scalar(ms[:], ms[:], 1.0 / D, EPS, ALU.mult, ALU.add).then_inc(norm_ms, 1)
                if (u, kp) == (1, 3):
                    norm_end(6, rs[:])
                    link(dve.tensor_tensor(rs[:], rs[:], rs_final[:], ALU.mult))

            stage("in2", "ple_gate", two_norms)
            for step in range(4):
                finish(st["in2"], st["in2"].iters - 1, st["in2"].u - 1, step)

            dve.wait_ge(evict_done, 2 * st["out2"].group0)
            dve.wait_ge(hs_done, 1)
            dve.tensor_scalar(small[:, 1], ps[:, 4, 0:48], 1.0 / HD, EPS, ALU.mult, ALU.add).then_inc(norm_ms, 1)
            for n in range(5):
                dve.wait_ge(v2_done, n + 1)
                for c in range(4):
                    j, tt = (4 * n + c) % 10, (4 * n + c) // 10
                    ins = dve.tensor_copy(v2_nat[:, tt, j * P:(j + 1) * P], ps[:, 5 + n % 3, c * P:(c + 1) * P])
                ins.then_inc(v2_read, 1)
            dve.wait_ge(norm_root, 7)
            newton(small[:, 0], small[:, 2], small[:, 1], small[:, 3])
            link(dve.tensor_scalar(qk_gain[:, 0:1], qk_gain[:, 0:1], HD ** -0.5, None, ALU.mult))
            wide = small[:, 0:1].rearrange("p o (a h) -> p (o a) h", a=2).rearrange("p a (h o) -> p a h o", o=1)
            dve.tensor_copy(r_wide[:], wide.broadcast_to([P, 2, 24, HD])).then_inc(hs_ready, 1)
            for j in range(12):
                dve.wait_ge(rb_done, j // 2 + 1)
                dve.scalar_tensor_tensor(out=proj[:, Q0 + j], in0=proj[:, Q0 + j], scalar=qk_gain[:, j // 6:j // 6 + 1],
                                         in1=ps[:, 4 + (j // 2) % 4, (j % 2) * T:(j % 2 + 1) * T], op0=ALU.mult,
                                         op1=ALU.mult).then_inc(qn_ready, 1)
            dve.wait_ge(late_consts, 64)
            dve.tensor_tensor(sgu_wt[:], sgu_wt[:], causal3(), ALU.mult).then_inc(wm_ready, 1)
            dve.wait_ge(qk_sq, 1)
            for hd in range(C_H):
                dve.wait_ge(sc_done, hd + 1)
                for tt in range(2):
                    i = 2 * hd + tt
                    dve.tensor_tensor_reduce(prob[:, hd, tt], ps[:, 4 + hd % 4, tt * T:(tt + 1) * T],
                                             amask[:, hd // 4, tt], 1.0, 2 * NEG, ALU.add, ALU.max,
                                             small[:, 0, i:i + 1]).then_inc(sc_read, 1)
                    dve.wait_ge(sc_read, i + 1)
                    dve.tensor_scalar(small[:, 1, i:i + 1], small[:, 0, i:i + 1], -1.0, None, ALU.mult).then_inc(nm_ready, 1)
            dve.wait_ge(late_consts, 64)
            for n in range(4):
                dve.wait_ge(ya_done, n + 1)
                for hf in range(2):
                    rows = slice(HD * hf, HD * hf + HD)
                    src = ps[rows, n].rearrange("p (c a i) -> p c a i", c=2, a=2)[:, :, hf]
                    ins = dve.tensor_tensor(proj[rows, AV0 + n].rearrange("p (c i) -> p c i", c=2), src,
                                            bias_a[rows, n:n + 1].broadcast_to([HD, 2, P]), ALU.add)
            link(ins)
            dve.tensor_tensor(proj[:, AU0:AU0 + 4], proj[:, AU0:AU0 + 4], proj[:, AV0:AV0 + 4], ALU.mult).then_inc(ya_ready, 1)
            bx, bc, bb = proj[:, BX0:BX0 + 6], proj[:, BC0:BC0 + 6], proj[:, BB0:BB0 + 6]
            link(dve.tensor_tensor(bx, bx, bc, ALU.mult))
            for j in range(6):
                ins = dve.tensor_scalar(bc[:, j], bx[:, j], conv_w[:, j, 2:3], None, ALU.mult)
            link(ins)
            for lag in (1, 2):
                for j in range(6):
                    ins = dve.scalar_tensor_tensor(out=bc[:, j, lag:T], in0=bx[:, j, 0:T - lag],
                                                   scalar=conv_w[:, j, 2 - lag:3 - lag], in1=bc[:, j, lag:T],
                                                   op0=ALU.mult, op1=ALU.add)
                link(ins)
            dve.tensor_tensor(bb, bb, bc, ALU.mult).then_inc(yb_ready, 1)
            dve.wait_ge(ln_ready, 1)
            mx, den, lse, wt, s5 = (small[:, k, 0:24] for k in (0, 2, 3, 4, 5))
            link(dve.tensor_tensor(lse, lse, mx, ALU.add))
            g3 = lse.rearrange("p (g x) -> p g x", g=3)
            w3 = wt.rearrange("p (g x) -> p g x", g=3)
            link(dve.tensor_tensor(s5[:, 0:8], g3[:, 0], g3[:, 1], ALU.max))
            link(dve.tensor_tensor(s5[:, 0:8], s5[:, 0:8], g3[:, 2], ALU.max))
            for g in range(3):
                ins = dve.tensor_tensor(w3[:, g], g3[:, g], s5[:, 0:8], ALU.subtract)
            ins.then_inc(lm_ready, 1)
            dve.wait_ge(wexp, 1)
            link(dve.tensor_tensor(s5[:, 8:16], w3[:, 0], w3[:, 1], ALU.add))
            link(dve.tensor_tensor(s5[:, 8:16], s5[:, 8:16], w3[:, 2], ALU.add))
            for g in range(3):
                ins = dve.tensor_tensor(den.rearrange("p (g x) -> p g x", g=3)[:, g],
                                        den.rearrange("p (g x) -> p g x", g=3)[:, g], s5[:, 8:16], ALU.mult)
            link(ins)
            link(dve.reciprocal(den, den))
            link(dve.tensor_tensor(wt, wt, den, ALU.mult))
            for i in range(24):
                dve.tensor_scalar(prob[:, i // 2, i % 2], prob[:, i // 2, i % 2], wt[:, i:i + 1], None, ALU.mult)\
                    .then_inc(pw_ready, 1)
            for j in range(6):
                dve.wait_ge(x_hi_ready, tiles_before["in2"] + j + 1)
                dve.tensor_tensor(acts[:, 16 + j, 1], ps[:, 6 + j % 2, 0:T], acts[:, 16 + j, 0].bitcast(F32), ALU.subtract)\
                    .then_inc(tile_ready, 1)
            dve.wait_ge(x_hi_ready, tiles_before["in2"] + 10)
            dve.tensor_tensor(acts[:, 22:26, 1], proj[:, AU0:AU0 + 4], acts[:, 22:26, 0].bitcast(F32), ALU.subtract)\
                .then_inc(tile_ready, 4)
            dve.wait_ge(x_hi_ready, tiles_before["in2"] + 16)
            dve.tensor_tensor(acts[:, 26:32, 1], proj[:, BB0:BB0 + 6], acts[:, 26:32, 0].bitcast(F32), ALU.subtract)\
                .then_inc(tile_ready, 6)
            stage("out2", None)
            stage("mlp_in0", "out2", norm_hook(8, 6))
            stage("mlp_out0", "mlp_in0")
            stage("mlp_in1", "mlp_out0")
            stage("mlp_out1", "mlp_in1")
            for step in range(2):
                finish(st["mlp_out1"], st["mlp_out1"].iters - 1, 1, step)


def _slots(w):
    k, n = w.shape
    return w.reshape(k // 256, 2, P, n // T, T).transpose(3, 0, 2, 1, 4).reshape(-1, P, 2, T)


def _features(x):
    return x.T.reshape(-1, P, x.shape[0]).transpose(1, 0, 2)


def _per_feature(v):
    return v.reshape(-1, P).T


def lay_out(inputs):
    g = {k: np.asarray(v) for k, v in inputs.items()}
    f = np.float32
    w_in = g["gla_w_in"][0]
    lr = np.zeros((D, T), f)
    lr[:, 0:32] = w_in[:, 6144:6176]
    gate, up = g["ffn_w_in"][0][:, :5632], g["ffn_w_in"][0][:, 5632:]
    parts = [_slots(lr), _slots(w_in[:, 0:6144]), _slots(g["gla_w_out"][0])]
    at = 0
    for k in FFN_HALVES:
        cols = slice(at, at + k * P)
        pair = np.stack([gate[:, cols].reshape(D, k // 2, T), up[:, cols].reshape(D, k // 2, T)], 2)
        parts += [_slots(pair.reshape(D, k * T)), _slots(g["ffn_w_out"][0][cols])]
        at += k * P
    parts += [_slots(g["ple_w_proj"][0]), _slots(g["ple_w_gate"][0])]
    w2 = g["w_in_2"][0]
    e = np.cumsum([0, 512, 512, 768, 768, 768, 768, 768, 768])
    c = [w2[:, e[i]:e[i + 1]] for i in range(8)]
    parts += [_slots(np.concatenate([c[5], c[6], c[7], c[1], c[0], c[3], c[4], c[2]], 1)), _slots(g["w_out_2"][0])]
    for n in range(2):
        cols = slice(n * MLP_HALF * P, (n + 1) * MLP_HALF * P)
        parts += [_slots(g["w_mlp_in_2"][0][:, cols]), _slots(g["w_mlp_out_2"][0][cols])]
    stream = np.concatenate(parts)
    assert len(stream) == N_SLOTS
    stream = np.ascontiguousarray(stream.reshape(N_SLOTS // 2, 2, P, 2, T).transpose(0, 2, 1, 3, 4))
    w_up = np.zeros((32, 2, GLA_U, P), f)
    for z in range(2):
        w_up[16 * z:16 * z + 16, z] = g["gla_w_gate_up"][0, z].reshape(16, GLA_U, P)
    i = np.arange(P)
    masks = np.stack([((i[:, None] // s) ^ (i[None, :] // s)) == 1 for s in LEVELS[:-1]], 1).astype(f)
    t = (np.arange(2)[None, :, None] * P + i[:, None, None])
    key = np.arange(T)[None, None, :]
    back = t - key
    ok = [(back >= 0) & (back <= 128), (back >= 0) & (back % 4 == 0), (back >= 0) & (back % 16 == 0)]
    amask = np.stack([np.where(m, 0.0, NEG) for m in ok], 1).astype(f)
    hp = np.zeros((P, 2), f)
    hp[:HD, 0] = 1
    hp[HD:, 1] = 1
    sgu_b = g["sgu_b_2"][0].reshape(4, 2, P)
    arrays = {
        "stream": stream,
        "x": _features(g["x"][0]),
        "p": _features(g["p"][0, 0]),
        "gains": np.stack([_per_feature(g[n].reshape(-1)) for n in
                           ("mixer_norm", "ffn_norm", "ple_norm", "final_norm", "attn_norm_2", "mlp_norm_2")], 1)[..., None],
        "ones": np.ones((P, P), f), "ident": np.eye(P, dtype=f),
        "b_gate": g["gla_b_gate"][0].reshape(2, GLA_U, P).transpose(2, 0, 1),
        "out_gain": _per_feature(g["gla_out_norm"][0]),
        "masks": masks, "w_up": w_up,
        "causal": (i[:, None] <= i[None, :]).astype(f), "head_pair": hp,
        "qk_gain": np.stack([np.tile(g["q_norm_2"][0], 2), np.tile(g["k_norm_2"][0], 2)], 1),
        "conv_w": g["conv_w_2"][0].reshape(3, 6, P).transpose(2, 1, 0),
        "amask": amask,
        "bias_a": np.repeat(sgu_b.transpose(1, 0, 2), HD, 0),
        "sgu_wt": g["sgu_w_2"][0].transpose(2, 0, 1),
    }
    return {k: np.ascontiguousarray(v) for k, v in arrays.items()}


def kernel(**inputs):
    import concourse.bacc as bacc
    from concourse.bass_utils import run_bass_kernel_spmd

    arrays = lay_out(inputs)
    nc = bacc.Bacc("TRN2", target_bir_lowering=False, num_devices=1)
    aps = {k: nc.dram_tensor(f"in_{k}", v.shape, mybir.dt.from_np(v.dtype), kind="ExternalInput").ap()
           for k, v in arrays.items()}
    out = nc.dram_tensor("out_t", (P, DT, T), F32, kind="ExternalOutput").ap()
    build(nc, aps, out)
    r = run_bass_kernel_spmd(nc, [{f"in_{k}": v for k, v in arrays.items()}], core_ids=[0])
    return r.results[0]["out_t"].transpose(2, 1, 0).reshape(1, T, D)
```

```python
import numpy as np
import concourse.bass as bass
from concourse import mybir
from contextlib import ExitStack

F32 = mybir.dt.float32
F32R = mybir.dt.float32r
U32 = mybir.dt.uint32
ALU = mybir.AluOpType
ACT = mybir.ActivationFunctionType

P = 128
T = 256
D = 2048
DT = D // P
EPS = 1e-6
RING = 8
KP = DT // 2
GLA_H = 4
GLA_U = 8
DV_T = 4
LEVELS = [1, 2, 4, 8, 16, 32, 64, 128]
FFN_HALVES = [24, 20]
MLP_HALF = 32
HD = 64
C_H = 12
N_IN2 = 44
Q0, K0, V0, AV0, AU0, BC0, BX0, BB0 = 0, 6, 12, 18, 22, 26, 32, 38
NEG = -1.0e38
OUT2_ORDER = [0, 1, 2, 3, 10, 11, 12, 13, 4, 5, 6, 7, 14, 15, 8, 9]
GAINS = ["mixer", "ffn", "ple", "final", "attn2", "mlp2"]


class Stage:

    def __init__(self, name, k, groups, u, slot0, group0):
        self.name, self.k, self.groups, self.u = name, k, groups, u
        self.kp = k // 2
        self.slot0, self.group0 = slot0, group0
        self.iters = groups // u
        self.body_slots = u * self.kp


def plan():
    order = [("qk", 16, 8, 2), ("v", 16, 8, 2), ("og", 16, 8, 2), ("ple_proj", 2, 8, 8), ("gla_out", 16, 8, 2)]
    for n, k in enumerate(FFN_HALVES):
        order += [(f"ffn_in{n}", 16, k, 2), (f"ffn_out{n}", k, 8, 2 if k % 8 == 0 else 4)]
    order += [("ple_gate", 16, 8, 2), ("in2", 16, N_IN2 // 2, 2), ("out2", 16, 8, 2)]
    for n in range(2):
        order += [(f"mlp_in{n}", 16, MLP_HALF // 2, 2), (f"mlp_out{n}", MLP_HALF, 8, 2)]
    stages, slot, group = {}, RING, 0
    for name, k, groups, u in order:
        stages[name] = s = Stage(name, k, groups, u, slot, group)
        assert s.body_slots % RING == 0
        slot += groups * s.kp
        group += groups
    return stages, slot


STAGES, N_SLOTS = plan()


def build(nc, A, out):
    st = STAGES
    with ExitStack() as ctx:
        def sb(name, shape, dt=F32, where=ctx):
            return where.enter_context(nc.sbuf_tensor(name, shape, dt))

        def sem(name):
            return ctx.enter_context(nc.semaphore(name))

        raw = sb("raw", [P, RING, 2, T])
        w_hi = sb("w_hi", [P, RING, 2, T], F32R)
        w_lo = sb("w_lo", [P, RING, 2, T], F32R)
        h = sb("h", [P, DT, T])
        with ExitStack() as place:
            xs = sb("xs", [P, DT, 2, T], F32R, where=place)
        with ExitStack() as place:
            prob = sb("prob", [P, C_H, 2, T], where=place)
            amask = sb("amask", [P, 3, 2, T], where=place)
            bias_a = sb("bias_a", [P, 4, P], where=place)
        with ExitStack() as place:
            sq_qk = sb("sq_qk", [P, 12, T], where=place)
        with ExitStack() as place:
            r_wide = sb("r_wide", [P, 2, 24, HD], where=place)
        sb("xs_place", [P, 2 * DT * T])
        ones = sb("ones", [P, P])
        ident = sb("ident", [P, P])
        gains = sb("gains", [P, len(GAINS), DT, 1])
        gain_fa = sb("gain_fa", [P, DT, 1])
        half = sb("half", [P, 2, T])
        total = sb("total", [P, 2, T])
        scaled = sb("scaled", [P, 2, T])
        sq_sum = sb("sq_sum", [P, 2, T])
        ms = sb("ms", [P, T])
        root = sb("root", [P, T])
        newt = sb("newt", [P, T])
        rs = sb("rs", [P, T])
        rs_final = sb("rs_final", [P, T])
        causal = sb("causal", [P, P])
        head_pair = sb("head_pair", [P, 2])
        qk_gain = sb("qk_gain", [P, 2])
        conv_w = sb("conv_w", [P, 6, 3])
        small = sb("small", [P, 6, 48])
        root_tables = sb("root_tables", [P, 16])

        with ExitStack() as gla:
            cum = sb("cum", [P, 2, GLA_U, T], where=gla)
            dec = sb("dec", [P, 2, GLA_U, T], where=gla)
            qk_dec = sb("qk_dec", [P, 2, GLA_U, T], where=gla)
            qk = sb("qk", [P, 2, GLA_U, T], where=gla)
            v_nat = sb("v_nat", [P, 2, D], where=gla)
            a_t = sb("a_t", [P, GLA_H, 4, P], where=gla)
            masks = sb("masks", [P, len(LEVELS) - 1, P], where=gla)
            b_gate = sb("b_gate", [P, 2, GLA_U], where=gla)
            out_gain = sb("out_gain", [P, DV_T], where=gla)
        with ExitStack() as main:
            acts = sb("acts", [P, MLP_HALF, 2, T], F32R, where=main)
            gate = sb("gate", [P, 2, T], where=main)
            act_gate = sb("act_gate", [P, 2, T], where=main)
            sq = sb("sq", [P, 2, 2, T], where=main)
            prod = sb("prod", [P, 2, T], where=main)
        with ExitStack() as early:
            sb("pad_early", [P, 64 * T], where=early)
            w_up = sb("w_up", [32, 2, GLA_U, P], where=early)
            lr_t = sb("lr_t", [P, T], where=early)
        with ExitStack() as ple:
            sb("pad_p", [P, 16 * T], where=ple)
            p_split = sb("p_split", [P, 2, 2, T], F32R, where=ple)
            p_raw = sb("p_raw", [P, 2, T], where=ple)
            rh_wide = sb("rh_wide", [P, 2 * GLA_H, P], where=ple)
            sb("pad_ple", [P, 22 * T], where=ple)
            ple_val = sb("ple_val", [P, DT, T], where=ple)
        with ExitStack() as att:
            sb("pad_in2", [P, 2 * DT * T], where=att)
            proj = sb("proj", [P, BB0, T], where=att)
            sb("pad_prod", [P, 4 * T], where=att)
            v2_nat = sb("v2_nat", [P, 2, 1280], where=att)
            prob_t = sb("prob_t", [P, 2, 2, T], where=att)
            sgu_wt = sb("sgu_wt", [P, 8, P], where=att)
        ps = ctx.enter_context(nc.psum_tensor("ps", [P, 8, 512], F32))

        raw_loaded = [sem(f"raw_loaded{i}") for i in range(RING // 2)]
        hi_ready = sem("hi_ready")
        lo_ready = sem("lo_ready")
        slots_used = sem("slots_used")
        half_ready = sem("half_ready")
        sum_done = sem("sum_done")
        evict_done = sem("evict_done")
        x_hi_ready = sem("x_hi_ready")
        tile_ready = sem("tile_ready")
        silu_done = sem("silu_done")
        prod_done = sem("prod_done")
        h_done = sem("h_done")
        sq_ready = sem("sq_ready")
        sq_added = sem("sq_added")
        norm_sum = sem("norm_sum")
        norm_ms = sem("norm_ms")
        norm_root = sem("norm_root")
        sq_step = sem("sq_step")
        x_loaded = [sem(f"x_loaded{c}") for c in range(4)]
        gains_loaded = sem("gains_loaded")
        ones_loaded = sem("ones_loaded")
        x_again = sem("x_again")
        consts = sem("consts")
        late_consts = sem("late_consts")
        out_stored = sem("out_stored")
        act_step = sem("act_step")
        dve_step = sem("dve_step")
        x_sq = sem("x_sq")
        x_sq_sum = sem("x_sq_sum")
        place_set = sem("place_set")
        lr_half = sem("lr_half")
        lr_ready = sem("lr_ready")
        gk_done = sem("gk_done")
        gk_read = sem("gk_read")
        ls_step = sem("ls_step")
        ls_ready = sem("ls_ready")
        vt_done = sem("vt_done")
        vt_read = sem("vt_read")
        s_done = sem("s_done")
        s_read = sem("s_read")
        cum_ready = sem("cum_ready")
        q_arg = sem("q_arg")
        k_arg = sem("k_arg")
        dec_exp = sem("dec_exp")
        dec_ready = sem("dec_ready")
        o_done = sem("o_done")
        o_read = sem("o_read")
        rh_ready = sem("rh_ready")
        rh_done = sem("rh_done")
        og_silu = sem("og_silu")
        og_used = sem("og_used")
        o_sq_sum = sem("o_sq_sum")
        y_ready = sem("y_ready")
        y_hi_ready = sem("y_hi_ready")
        y_lo_even = sem("y_lo_even")
        y_lo_odd = sem("y_lo_odd")
        p_hi = sem("p_hi")
        p_ready = sem("p_ready")
        qk_sq = sem("qk_sq")
        hs_done = sem("hs_done")
        hs_ready = sem("hs_ready")
        rb_done = sem("rb_done")
        qn_ready = sem("qn_ready")
        sc_done = sem("sc_done")
        sc_read = sem("sc_read")
        nm_ready = sem("nm_ready")
        e_ready = sem("e_ready")
        ln_ready = sem("ln_ready")
        lm_ready = sem("lm_ready")
        wexp = sem("wexp")
        pw_ready = sem("pw_ready")
        pt_done = sem("pt_done")
        pt_read = sem("pt_read")
        yc_done = sem("yc_done")
        yc_hi = sem("yc_hi")
        yc_lo = sem("yc_lo")
        v2_done = sem("v2_done")
        v2_read = sem("v2_read")
        wm_ready = sem("wm_ready")
        ya_done = sem("ya_done")
        ya_sum = sem("ya_sum")
        ya_ready = sem("ya_ready")
        ya_hi = sem("ya_hi")
        ya_lo = sem("ya_lo")
        conv_step = sem("conv_step")

        N_CONST = 9
        block = ctx.enter_context(nc.Block())

        def wait(eng, s, n):
            if not isinstance(n, int) or n > 0:
                eng.wait_ge(s, n)

        def first_time(it):
            return isinstance(it, int) and it == 0

        def iterate(eng, n, body):
            body(0)
            if n > 1:
                with eng.Fori(1, n) as it:
                    body(it)

        tiles_before = {"qk": 16}
        n = 16
        for name in ("v", "og"):
            tiles_before[name] = n
        for name, made_before in (("gla_out", 0), ("ffn_in0", 16), ("ffn_out0", 24), ("ffn_in1", 0), ("ffn_out1", 20),
                                  ("ple_gate", 16), ("in2", 16), ("out2", 6), ("mlp_in0", 16),
                                  ("mlp_out0", 32), ("mlp_in1", 0), ("mlp_out1", 32)):
            n += made_before
            tiles_before[name] = n
        prods = {"ffn_in0": 0, "ffn_in1": 24, "mlp_in0": 66, "mlp_in1": 98}
        conv_prods = 60

        @block.sync
        def _(sp):
            def turn(t):
                for c in range(RING // 2):
                    wait(sp, lo_ready, RING * (t - 1) + 2 * c + 2)
                    sp.dma_start(raw[:, 2 * c:2 * c + 2], A["stream"][RING // 2 * t + c]).then_inc(raw_loaded[c], 16)

            sp.dma_start(ones[:], A["ones"]).then_inc(ones_loaded, 16)
            turn(0)
            for dst, src in ((ident, "ident"), (w_up, "w_up"), (b_gate, "b_gate"), (out_gain, "out_gain"), (masks, "masks"),
                             (causal, "causal"), (head_pair, "head_pair"), (qk_gain, "qk_gain"), (conv_w, "conv_w")):
                sp.dma_start(dst[:], A[src]).then_inc(consts, 16)
            with sp.Fori(1, N_SLOTS // RING) as t:
                turn(t)
            e0 = 2 * st["mlp_out1"].group0
            for j in range(DT):
                sp.wait_ge(evict_done, e0 + j + 1)
                sp.dma_start(out[:, j], h[:, j]).then_inc(out_stored, 16)
            sp.wait_ge(out_stored, 16 * DT)

        def through_in2(eng, body):
            body(0)
            with eng.Fori(1, 3) as it:
                body(it)
            for it in range(3, st["in2"].iters):
                body(it)

        def in2_group(s, it, u):
            return it * s.u + u if s.name == "in2" and isinstance(it, int) else -1

        def y_tile(k):
            return 22 + k if k < 10 else 6 + k

        def causal3():
            return causal[:].rearrange("p (a i) -> p a i", a=1).broadcast_to([P, 8, P])

        @block.tensor
        def _(pe):
            def slot(n, r, kp, moving, banks, first, last):
                pe.wait_ge(lo_ready, n + 1)
                for a in range(2):
                    x = moving(2 * kp + a)
                    for b, bank in enumerate(banks):
                        w = slice(b * P, (b + 1) * P)
                        pe.matmul(ps[:, bank, :], w_hi[:, r, a, w], x.rearrange("p a t -> p (a t)"),
                                  start=first and a == 0, stop=last and a == 1, skip_group_check=True)
                        mm = pe.matmul(ps[:, bank, 0:T], w_lo[:, r, a, w], x[:, 0],
                                       start=False, stop=last and a == 1, skip_group_check=True)
                mm.then_inc(slots_used, 1)

            def groups(s, it, moving, needs=(), norm_of_input=None, after=None):
                for u in range(s.u):
                    wait(pe, sum_done, 2 * (s.group0 + it * s.u + u - 1))
                    for kp in range(s.kp):
                        if first_time(it) and u == 0:
                            for at, s_, count in needs:
                                if at == kp:
                                    pe.wait_ge(s_, count)
                        local = u * s.kp + kp
                        slot(s.slot0 + it * s.body_slots + local, local % RING, kp, moving,
                             [2 * (u % 2), 2 * (u % 2) + 1], kp == 0, kp == s.kp - 1)
                        if first_time(it) and (u, kp) == (0, 5) and norm_of_input is not None:
                            norm_of_input()
                    if after is not None:
                        after(u)

            def stage(name, moving, needs=(), norm_of_input=None):
                iterate(pe, st[name].iters, lambda it: groups(st[name], it, moving, needs, norm_of_input))

            def norm(k, cols):
                def go():
                    pe.wait_ge(sq_added, k)
                    for c in range(cols):
                        mm = pe.matmul(ps[:, 4, c * T:(c + 1) * T], ones[:], sq_sum[:, c], start=True, stop=True,
                                       skip_group_check=True)
                    mm.then_inc(norm_sum, 1)
                return go

            for kp in range(KP):
                pe.wait_ge(tile_ready, 2 * kp + 2)
                slot(kp, kp, kp, lambda k: xs[:, k], [5], kp == 0, kp == KP - 1)

            def x_norm():
                pe.wait_ge(ones_loaded, 16)
                pe.wait_ge(x_sq_sum, 4)
                pe.matmul(ps[:, 4, 0:T], ones[:], cum[:, 0, 0], start=True, stop=True, skip_group_check=True)\
                    .then_inc(norm_sum, 1)

            groups(st["qk"], 0, lambda k: xs[:, k], norm_of_input=x_norm)
            pe.wait_ge(consts, 16 * N_CONST)
            pe.wait_ge(lr_ready, 1)
            for n in range(8):
                wait(pe, gk_read, n - 3)
                for c in range(2):
                    z, u = (2 * n + c) // GLA_U, (2 * n + c) % GLA_U
                    mm = pe.matmul(ps[:, 4 + n % 4, c * T:(c + 1) * T], w_up[:, z, u], lr_t[0:32], start=True,
                                   stop=True, skip_group_check=True)
                mm.then_inc(gk_done, 1)
            with pe.Fori(1, st["qk"].iters) as it:
                groups(st["qk"], it, lambda k: xs[:, k])

            def scores(lv):
                src, cross = qk if lv == 0 else qk_dec, lv == len(LEVELS)
                if lv:
                    pe.wait_ge(dec_ready, 2 * lv)
                for hp in range(2):
                    pe.wait_ge(s_read, 2 * lv + hp - 1) if lv else pe.wait_ge(gk_read, 8)
                    for hh in range(2):
                        for jt in range(2):
                            i_t = 1 - jt if cross else jt
                            for d in range(2):
                                u = 2 * (2 * hp + hh) + d
                                mm = pe.matmul(ps[:, 4 + hp, (2 * hh + jt) * P:(2 * hh + jt + 1) * P],
                                               src[:, 1, u, jt * P:(jt + 1) * P], src[:, 0, u, i_t * P:(i_t + 1) * P],
                                               start=d == 0, stop=d == 1, skip_group_check=True)
                    mm.then_inc(s_done, 1)

            def turn_v(g):
                pe.wait_ge(evict_done, 2 * (st["v"].group0 + g) + 2)
                pe.wait_ge(vt_read, g) if g else pe.wait_ge(gk_read, 8)
                for tt in range(2):
                    for b in range(2):
                        mm = pe.transpose(ps[:, 7, (2 * tt + b) * P:(2 * tt + b + 1) * P], scaled[:, b, tt * P:(tt + 1) * P],
                                          ident[:])
                mm.then_inc(vt_done, 1)

            for n in range(len(LEVELS)):
                def after(u, n=n):
                    if 1 <= 2 * n + u <= 8:
                        turn_v(2 * n + u - 1)
                    if n == 0 and u == 0:
                        pe.wait_ge(evict_done, 2 * st["v"].group0)
                        scores(0)
                    if u == 1:
                        scores(n + 1)
                groups(st["v" if n < 4 else "og"], n % 4, lambda k: xs[:, k], after=after)
            def ple_groups(first_g, last_g):
                s = st["ple_proj"]
                for g in range(first_g, last_g):
                    pe.wait_ge(sum_done, 2 * (s.group0 + g - 1))
                    slot(s.slot0 + g, g, 0, lambda k: p_split[:, k], [2 * (g % 2), 2 * (g % 2) + 1], True, True)

            pe.wait_ge(p_ready, 1)
            ple_groups(0, 4)
            pe.wait_ge(vt_read, 8)
            pe.wait_ge(s_read, 18)
            for n in range(8):
                wait(pe, o_read, n - 3)
                for c in range(2):
                    dv = 2 * n + c
                    for jt in range(2):
                        mm = pe.matmul(ps[:, 4 + n % 4, c * T:(c + 1) * T], v_nat[:, jt, dv * P:(dv + 1) * P],
                                       a_t[:, dv // DV_T, 2 * jt:2 * jt + 2].rearrange("p a i -> p (a i)"),
                                       start=jt == 0, stop=jt == 1, skip_group_check=True)
                mm.then_inc(o_done, 1)
            ple_groups(4, 5)
            pe.wait_ge(o_read, 8)
            pe.wait_ge(o_sq_sum, 3 * GLA_H)
            for hd in range(GLA_H):
                n = hd * DV_T
                for tt in range(2):
                    mm = pe.matmul(ps[:, 6, tt * GLA_H + hd:tt * GLA_H + hd + 1],
                                   cum[:, n // 8, n % 8, tt * P:(tt + 1) * P], ones[:, 0:1], start=True, stop=True,
                                   skip_group_check=True)
            mm.then_inc(norm_sum, 1)
            ple_groups(5, 7)
            pe.wait_ge(rh_ready, 1)
            for hd in range(GLA_H):
                for tt in range(2):
                    mm = pe.matmul(ps[:, 4 + hd // 2, (hd % 2) * T + tt * P:(hd % 2) * T + (tt + 1) * P],
                                   rh_wide[:, tt * GLA_H + hd], ident[:], start=True, stop=True, skip_group_check=True)
            mm.then_inc(rh_done, 1)
            ple_groups(7, 8)
            tb = tiles_before
            stage("gla_out", lambda k: acts[:, k],
                  [(2 * hd, y_lo_odd if hd % 2 else y_lo_even, hd // 2 + 1) for hd in range(GLA_H)])
            stage("ffn_in0", lambda k: xs[:, k],
                  [(0, tile_ready, tb["ffn_in0"] - 2), (KP - 1, tile_ready, tb["ffn_in0"])], norm(16, 1))
            for n in range(2):
                s = st[f"ffn_out{n}"]
                if n:
                    stage("ffn_in1", lambda k: xs[:, k])
                stage(s.name, lambda k: acts[:, k],
                      [(0, tile_ready, tb[s.name] - 2), (s.kp - 1, tile_ready, tb[s.name])])
            stage("ple_gate", lambda k: xs[:, k],
                  [(0, tile_ready, tb["ple_gate"] - 2), (KP - 1, tile_ready, tb["ple_gate"])], norm(32, 1))

            def head_squares():
                pe.wait_ge(qk_sq, 2)
                for tt in range(2):
                    for j in range(12):
                        mm = pe.matmul(ps[:, 4, tt * 24 + 2 * j:tt * 24 + 2 * j + 2], sq_qk[:, j, tt * P:(tt + 1) * P],
                                       head_pair[:], start=True, stop=True, skip_group_check=True)
                mm.then_inc(hs_done, 1)

            def head_rstd(n):
                wait(pe, qn_ready, 2 * (n - 2))
                for c in range(2):
                    for tt in range(2):
                        r = r_wide[:, tt, 4 * n + 2 * c:4 * n + 2 * c + 2].rearrange("p a b -> p (a b)")
                        mm = pe.matmul(ps[:, 4 + n % 3, c * T + tt * P:c * T + (tt + 1) * P], r, ident[:],
                                       start=True, stop=True, skip_group_check=True)
                mm.then_inc(rb_done, 1)

            def turn_v2(n):
                pe.wait_ge(evict_done, 2 * st["in2"].group0 + V0 + 2 * n + 2)
                wait(pe, v2_read, n)
                for tt in range(2):
                    for b in range(2):
                        mm = pe.transpose(ps[:, 7, (2 * tt + b) * P:(2 * tt + b + 1) * P],
                                          proj[:, V0 + 2 * n + b, tt * P:(tt + 1) * P], ident[:])
                mm.then_inc(v2_done, 1)

            def head_scores(hd):
                pe.wait_ge(qn_ready, 12)
                wait(pe, sc_read, 2 * (hd - 2))
                j, rows = hd // 2, slice(HD * (hd % 2), HD * (hd % 2) + HD)
                for tt in range(2):
                    mm = pe.matmul(ps[:, 4 + hd % 3, tt * T:(tt + 1) * T], proj[rows, Q0 + j, tt * P:(tt + 1) * P],
                                   proj[rows, K0 + j], start=True, stop=True, skip_group_check=True)
                mm.then_inc(sc_done, 1)

            def gating(n):
                pe.wait_ge(wm_ready, 1)
                pe.wait_ge(v2_read, 5)
                wait(pe, ya_sum, n)
                for c in range(2):
                    mm = pe.matmul(ps[:, 7, c * T:(c + 1) * T], v2_nat[:, c, 768 + n * P:768 + (n + 1) * P],
                                   sgu_wt[:, 2 * n:2 * n + 2].rearrange("p a i -> p (a i)"), start=True, stop=True,
                                   skip_group_check=True)
                mm.then_inc(ya_done, 1)

            def turn_weights(hd):
                pe.wait_ge(sc_read, 2 * C_H)
                pe.wait_ge(pw_ready, 2 * (hd + 1))
                wait(pe, pt_read, hd - 1)
                for s_ in range(2):
                    for tt in range(2):
                        mm = pe.transpose(ps[:, 4 + hd % 2, s_ * T + tt * P:s_ * T + (tt + 1) * P],
                                          prob[:, hd, tt, s_ * P:(s_ + 1) * P], ident[:])
                mm.then_inc(pt_done, 1)

            def weighted_v(j):
                pe.wait_ge(pt_read, 2 * j + 2)
                wait(pe, yc_lo, j)
                for g in (2 * j, 2 * j + 1):
                    for s_ in range(2):
                        mm = pe.matmul(ps[HD * (g % 2):HD * (g % 2) + HD, 6, 0:T], v2_nat[:, s_, g * HD:(g + 1) * HD],
                                       prob_t[:, g % 2, s_], start=s_ == 0, stop=s_ == 1, skip_group_check=True)
                mm.then_inc(yc_done, 1)

            def after_in2(g):
                if g == 6:
                    head_squares()
                if g in (7, 8):
                    pe.wait_ge(hs_ready, 1)
                    for n in range(3 * (g - 7), 3 * (g - 6)):
                        head_rstd(n)
                if 7 <= g <= 11:
                    turn_v2(g - 7)
                if 9 <= g <= 12:
                    for hd in range(3 * (g - 9), 3 * (g - 8)):
                        head_scores(hd)
                if 13 <= g <= 16:
                    gating(g - 13)
                if 16 <= g <= 21:
                    weighted_v(g - 16)
                if 15 <= g <= 20:
                    turn_weights(2 * (g - 15))
                    turn_weights(2 * (g - 15) + 1)

            through_in2(pe, lambda it: groups(
                st["in2"], it, lambda k: acts[:, k], [(0, tile_ready, tb["in2"] - 2), (KP - 1, tile_ready, tb["in2"])],
                norm(48, 2), (lambda u: after_in2(2 * it + u)) if isinstance(it, int) else None))
            stage("out2", lambda k: acts[:, y_tile(OUT2_ORDER[k])],
                  [(0, ya_lo, 4), (2, yc_lo, 4), (4, tile_ready, tb["out2"] - 2), (6, yc_lo, 6), (7, tile_ready, tb["out2"])])
            stage("mlp_in0", lambda k: xs[:, k],
                  [(0, tile_ready, tb["mlp_in0"] - 2), (KP - 1, tile_ready, tb["mlp_in0"])], norm(64, 1))
            for n in range(2):
                s = st[f"mlp_out{n}"]
                if n:
                    stage("mlp_in1", lambda k: xs[:, k])
                stage(s.name, lambda k: acts[:, k],
                      [(0, tile_ready, tb[s.name] - 2), (s.kp - 1, tile_ready, tb[s.name])])

        hidden = {"ffn_in0": "swiglu", "ffn_in1": "swiglu", "mlp_in0": "relu2", "mlp_in1": "relu2"}
        residual = {"gla_out": (0, 1), "ffn_out1": (16, 2), "out2": (48, 5)}

        def tile_no(s, it, u, b):
            return 2 * (s.group0 + it * s.u + u) + b

        def tile_of(s, it, u, b):
            if hidden.get(s.name) == "swiglu":
                return 2 * (it * (s.u // 2) + u // 2) + b
            return 2 * (it * s.u + u) + b

        def slots_body(s, it, split, finish, before, extra=None):
            for u in range(s.u):
                for kp in range(s.kp):
                    local = u * s.kp + kp
                    split(s.slot0 + it * s.body_slots + local, local % RING,
                          s.slot0 // RING + it * (s.body_slots // RING) + local // RING)
                    if 4 <= kp < 8:
                        if u > 0:
                            finish(s, it, u - 1, kp - 4)
                        elif not first_time(it):
                            finish(s, it - 1, s.u - 1, kp - 4)
                        elif before is not None:
                            finish(before, before.iters - 1, before.u - 1, kp - 4)
                    if extra is not None:
                        extra(u, kp)

        def slots_loop(eng, s, split, finish, before, extra=None):
            iterate(eng, s.iters, lambda it: slots_body(s, it, split, finish, before, extra if first_time(it) else None))

        @block.scalar
        def _(act):
            def split(n, r, turn):
                if r % 2 == 0:
                    act.wait_ge(raw_loaded[r // 2], 16 * (turn + 1))
                wait(act, slots_used, n - RING + 1)
                act.activation(w_hi[:, r], raw[:, r], ACT.Copy).then_inc(hi_ready, 1)

            def second(s, it, u, b):
                e, j = tile_no(s, it, u, b), tile_of(s, it, u, b)
                kind = hidden.get(s.name)
                if kind == "swiglu" and u % 2 == 0:
                    act.wait_ge(evict_done, e + 1)
                    act.activation(act_gate[:, b], scaled[:, b], ACT.Silu).then_inc(silu_done, 1)
                elif kind:
                    act.wait_ge(prod_done, prods[s.name] + j + 1)
                    act.wait_ge(consts, 16 * N_CONST)
                    act.activation(acts[:, j, 0], prod[:, b], ACT.Copy).then_inc(x_hi_ready, 1)
                elif s.name in residual:
                    added, gain = residual[s.name]
                    act.wait_ge(evict_done, e + 1)
                    wait(act, sq_added, added + j - 1)
                    act.wait_ge(consts, 16 * N_CONST)
                    act.activation(xs[:, j, 0], h[:, j], ACT.Copy, scale=gains[:, gain, j]).then_inc(x_hi_ready, 1)
                    act.activation(sq[:, b, 0], h[:, j], ACT.Square).then_inc(sq_ready, 1)
                elif in2_group(s, it, u) >= BB0 // 2:
                    act.wait_ge(prod_done, conv_prods + j - BB0 + 1)
                    act.activation(acts[:, y_tile(4 + j - BB0), 0], prod[:, b], ACT.Copy).then_inc(x_hi_ready, 1)
                elif s.name == "ple_gate":
                    act.wait_ge(evict_done, e + 1)
                    act.activation(act_gate[:, b], scaled[:, b], ACT.Sigmoid).then_inc(silu_done, 1)

            def third(s, it, u, b):
                if s.name == "ple_gate":
                    j = tile_of(s, it, u, b)
                    act.wait_ge(h_done, j + 1)
                    wait(act, sq_added, 32 + j - 1)
                    act.wait_ge(consts, 16 * N_CONST)
                    act.activation(acts[:, j, 0], h[:, j], ACT.Copy, scale=gain_fa[:, j]).then_inc(x_hi_ready, 1)
                    act.activation(sq[:, b, 0], h[:, j], ACT.Square)
                    act.activation(sq[:, b, 1], h[:, j], ACT.Square, scale=gains[:, 3, j]).then_inc(sq_ready, 1)

            def halves(s, it, u, b):
                act.wait_ge(slots_used, s.slot0 + (it * s.u + u + 1) * s.kp)
                wait(act, sum_done, tile_no(s, it, u, b) - 1)
                act.activation(half[:, b], ps[:, 2 * (u % 2) + b, T:2 * T], ACT.Copy).then_inc(half_ready, 1)

            def finish(s, it, u, step):
                if step < 2:
                    halves(s, it, u, step)
                if 1 <= step < 3:
                    second(s, it, u, step - 1)
                if step == 3:
                    third(s, it, u, 0)
                    third(s, it, u, 1)

            def square_root(n):
                act.wait_ge(norm_ms, n)
                act.activation(root[:], ms[:], ACT.Sqrt).then_inc(norm_root, 1)

            def norm_root_at(n, u, kp):
                if (u, kp) == (1, 0):
                    act.activation(root_tables[:, n:n + 1], ones[:, 0:1], ACT.Sqrt)
                if (u, kp) == (1, 2):
                    square_root(n)

            def stage(name, before, extra=None):
                slots_loop(act, st[name], split, finish, st[before] if before else None, extra)

            def yc_split(j):
                act.wait_ge(yc_done, j + 1)
                act.activation(acts[:, y_tile(10 + j), 0], ps[:, 6, 0:T], ACT.Copy).then_inc(yc_hi, 1)

            act.dma_start(gains[:], A["gains"]).then_inc(gains_loaded, 16)
            for c in range(4):
                act.dma_start(h[:, 4 * c:4 * c + 4], A["x"][:, 4 * c:4 * c + 4]).then_inc(x_loaded[c], 16)
            act.wait_ge(place_set, 1)
            act.activation(root_tables[:, 1:2], root_tables[:, 0:1], ACT.Copy)
            act.wait_ge(gains_loaded, 16)
            for c in range(4):
                act.wait_ge(x_loaded[c], 16)
                for j in range(4 * c, 4 * c + 4):
                    act.activation(xs[:, j, 0], h[:, j], ACT.Copy, scale=gains[:, 0, j]).then_inc(x_hi_ready, 1)
                for r in (2 * c, 2 * c + 1):
                    split(r, r, 0)

            def during_qk(it, u, kp):
                if (it, u, kp) == (0, 1, 0):
                    act.activation(root_tables[:, 2:3], root_tables[:, 0:1], ACT.Sqrt)
                if (it, u, kp) == (0, 1, 2):
                    square_root(1)
                    act.wait_ge(slots_used, RING)
                    act.activation(scaled[:, 0], ps[:, 5, T:2 * T], ACT.Copy).then_inc(lr_half, 1)
                if it == 2 and kp == 2:
                    act.wait_ge(ls_step, u + 1)
                    act.activation(dec[:, u], dec[:, u], ACT.Exp, scale=-1.0).then_inc(act_step, 1)
                if it == 2 and kp == 3:
                    act.wait_ge(act_step, u + 1)
                    act.activation(dec[:, u], dec[:, u], ACT.Ln, bias=1.0).then_inc(ls_ready, 1)

            def during_v_og(n, u, kp):
                if u == 0 and kp in (3, 6):
                    part = 0 if kp == 3 else 1
                    act.wait_ge(k_arg if part else q_arg, n + 1)
                    act.activation(dec[:, part], dec[:, part], ACT.Exp, scale=1.0 / 16).then_inc(dec_exp, 1)
                if (n, u, kp) == (len(LEVELS) - 1, 1, 5):
                    act.wait_ge(dec_ready, 2 * len(LEVELS))
                    act.dma_start(p_raw[:], A["p"]).then_inc(late_consts, 16)
                g = 2 * n + u - 2
                if kp == 7 and 0 <= g < 8:
                    act.wait_ge(vt_done, g + 1)
                    act.activation(v_nat[:, :, 2 * g * P:(2 * g + 2) * P],
                                   ps[:, 7].rearrange("p (a c) -> p a c", a=2), ACT.Copy).then_inc(vt_read, 1)

            for it in range(4):
                slots_body(st["qk"], it, split, finish, None, lambda u, kp: during_qk(it, u, kp))
            for n in range(len(LEVELS)):
                name, before = ("v", "qk") if n < 4 else ("og", "v")
                slots_body(st[name], n % 4, split, finish, st[before], lambda u, kp: during_v_og(n, u, kp))
            s = st["ple_proj"]
            for r in range(RING):
                split(s.slot0 + r, r, s.slot0 // RING)
                if r == 0:
                    act.wait_ge(late_consts, 16)
                    act.activation(p_split[:, :, 0], p_raw[:], ACT.Copy).then_inc(p_hi, 1)
                if r >= 4:
                    finish(st["og"], st["og"].iters - 1, 1, r - 4)

            def ple_halves(g):
                act.wait_ge(slots_used, s.slot0 + g + 1)
                act.wait_ge(sum_done, 2 * (s.group0 + g))
                act.activation(half[:], ps[:, 2 * (g % 2):2 * (g % 2) + 2, T:2 * T], ACT.Copy).then_inc(half_ready, 2)

            for g in range(4):
                ple_halves(g)
            act.wait_ge(evict_done, 2 * s.group0)
            act.activation(h[:], h[:], ACT.Silu).then_inc(og_silu, 1)
            y = qk_dec[:].rearrange("p a b t -> p (a b) t")
            o_sq = cum[:].rearrange("p a b t -> p (a b) t")
            for n in range(8):
                act.wait_ge(o_done, n + 1)
                o_ps = ps[:, 4 + n % 4].rearrange("p (a t) -> p a t", a=2)
                act.activation(y[:, 2 * n:2 * n + 2], o_ps, ACT.Copy, scale=1.0 / 16)
                act.activation(o_sq[:, 2 * n:2 * n + 2], o_ps, ACT.Square, scale=1.0 / 16).then_inc(o_read, 1)
            ple_halves(4)
            act.wait_ge(og_used, DT)
            act.dma_start(h[:], A["x"]).then_inc(x_again, 16)
            act.wait_ge(norm_ms, 2)
            act.activation(small[:, 2, 0:8], small[:, 1, 0:8], ACT.Sqrt).then_inc(norm_root, 1)
            for g in (5, 6):
                ple_halves(g)

            def y_hi(u, kp):
                if u == 0 and kp < GLA_H:
                    tiles = slice(kp * DV_T, (kp + 1) * DV_T)
                    if kp == 2:
                        act.wait_ge(slots_used, s.slot0 + RING)
                    act.wait_ge(y_ready, kp + 1)
                    act.activation(acts[:, tiles, 0], y[:, tiles], ACT.Copy).then_inc(y_hi_ready, 1)
                if (u, kp) == (0, 0):
                    ple_halves(7)

            stage("gla_out", None, y_hi)
            stage("ffn_in0", "gla_out", lambda u, kp: norm_root_at(3, u, kp))
            stage("ffn_out0", "ffn_in0")
            stage("ffn_in1", "ffn_out0")
            stage("ffn_out1", "ffn_in1")
            stage("ple_gate", "ffn_out1", lambda u, kp: norm_root_at(4, u, kp))

            def during_in2(w, kp):
                if w < 2:
                    norm_root_at(5, w, kp)
                if (w, kp) == (6, 2):
                    square_root(6)
                if (w, kp) == (1, 7):
                    for dst, src in ((amask, "amask"), (bias_a, "bias_a"), (sgu_wt, "sgu_wt")):
                        act.dma_start(dst[:], A[src]).then_inc(late_consts, 16)
                if (w, kp) in ((6, 7), (7, 0)):
                    part = w - 6
                    act.wait_ge(evict_done, 2 * st["in2"].group0 + 6 * part + 6)
                    act.activation(sq_qk[:, 6 * part:6 * part + 6], proj[:, 6 * part:6 * part + 6], ACT.Square)\
                        .then_inc(qk_sq, 1)
                if (w, kp) == (8, 0):
                    act.wait_ge(norm_ms, 7)
                    act.activation(small[:, 2], small[:, 1], ACT.Sqrt).then_inc(norm_root, 1)
                if 8 <= w <= 12 and kp == 7:
                    n = w - 8
                    act.wait_ge(v2_done, n + 1)
                    act.activation(v2_nat[:, :, 2 * n * P:(2 * n + 2) * P], ps[:, 7].rearrange("p (a c) -> p a c", a=2),
                                   ACT.Copy).then_inc(v2_read, 1)
                if 11 <= w <= 14 and kp < 3:
                    hd = 3 * (w - 11) + kp
                    for tt in range(2):
                        i = 2 * hd + tt
                        act.wait_ge(nm_ready, i + 1)
                        act.activation(prob[:, hd, tt], prob[:, hd, tt], ACT.Exp, bias=small[:, 1, i:i + 1],
                                       accum_out=small[:, 2, i:i + 1]).then_inc(e_ready, 1)
                if (w, kp) == (14, 3):
                    act.wait_ge(e_ready, 24)
                    act.activation(small[:, 3, 0:24], small[:, 2, 0:24], ACT.Ln).then_inc(ln_ready, 1)
                if (w, kp) == (15, 0):
                    act.wait_ge(lm_ready, 1)
                    act.activation(small[:, 4, 0:24], small[:, 4, 0:24], ACT.Exp).then_inc(wexp, 1)
                if 15 <= w <= 18 and kp == 1:
                    n = w - 15
                    act.wait_ge(ya_ready, n + 1)
                    act.activation(acts[:, y_tile(n), 0], proj[:, AU0 + n], ACT.Copy).then_inc(ya_hi, 1)
                if 16 <= w <= 21 and kp == 7:
                    for hd in (2 * (w - 16), 2 * (w - 16) + 1):
                        act.wait_ge(pt_done, hd + 1)
                        wait(act, yc_done, w - 16)
                        act.activation(prob_t[:, hd % 2], ps[:, 4 + hd % 2].rearrange("p (a t) -> p a t", a=2), ACT.Copy)\
                            .then_inc(pt_read, 1)
                if 17 <= w <= 21 and kp == 7:
                    yc_split(w - 17)

            s = st["in2"]
            through_in2(act, lambda it: slots_body(s, it, split, finish, st["ple_gate"],
                        (lambda u, kp: during_in2(2 * it + u, kp)) if isinstance(it, int) else None))
            stage("out2", "in2", lambda u, kp: yc_split(5) if (u, kp) == (0, 6) else None)
            stage("mlp_in0", "out2", lambda u, kp: norm_root_at(8, u, kp))
            stage("mlp_out0", "mlp_in0")
            stage("mlp_in1", "mlp_out0")
            stage("mlp_out1", "mlp_in1")
            for step in range(2):
                finish(st["mlp_out1"], st["mlp_out1"].iters - 1, 1, step)

        def cut(x, size):
            return x.rearrange("p u (n b s) -> p (u n) b s", b=2, s=size)

        def references(f, b, size):
            pairs = GLA_U * T // (2 * size)
            return (f[:, :, 0, size - 1:size].broadcast_to([P, pairs, size]),
                    b[:, :, 1, 0:1].broadcast_to([P, pairs, size]))

        @block.gpsimd
        def _(pool):
            def add_up(done, cols, norms):
                if norms:
                    pool.wait_ge(norm_sum, norms)
                pool.memset(sq_sum[:, 0:cols], 0.0).then_inc(sq_step, 1)
                pool.wait_ge(sq_step, len(done_norms) + 1)
                done_norms.append(done)

                def two(i):
                    for b in range(2):
                        k = done + i * 2 + b
                        pool.wait_ge(sq_ready, k + 1)
                        wait(pool, sq_added, k)
                        pool.tensor_tensor(sq_sum[:, 0:cols], sq_sum[:, 0:cols], sq[:, b, 0:cols], ALU.add)\
                            .then_inc(sq_added, 1)
                iterate(pool, DT // 2, two)

            for j in range(DT):
                if j % 4 == 0:
                    pool.wait_ge(x_loaded[j // 4], 16)
                pool.tensor_tensor(cum[:, j // 8, j % 8], h[:, j], h[:, j], ALU.mult).then_inc(x_sq, 1)
            for n, size in enumerate(LEVELS):
                pool.wait_ge(cum_ready, 1)
                if n:
                    pool.wait_ge(dec_ready, 2 * n)
                f, b, dk = cut(cum[:, 0], size), cut(cum[:, 1], size), cut(dec[:, 1], size)
                ref_f, ref_b = references(f, b, size)
                pool.tensor_tensor(dk[:, :, 0], ref_f, f[:, :, 0], ALU.subtract)
                pool.tensor_tensor(dk[:, :, 1], b[:, :, 1], ref_b, ALU.subtract).then_inc(k_arg, 1)
            o_sq = cum[:].rearrange("p a b t -> p (a b) t")
            for hd in range(GLA_H):
                k = hd * DV_T
                for step, (to, other, read) in enumerate(((k, k + 1, 2 * hd + 1), (k + 2, k + 3, 2 * hd + 2), (k, k + 2, 0))):
                    wait(pool, o_read, read)
                    wait(pool, o_sq_sum, 3 * hd + step)
                    pool.tensor_tensor(o_sq[:, to], o_sq[:, to], o_sq[:, other], ALU.add).then_inc(o_sq_sum, 1)
            y = qk_dec[:].rearrange("p a b t -> p (a b) t")
            for hd in (1, 3):
                tiles = slice(hd * DV_T, (hd + 1) * DV_T)
                pool.wait_ge(y_hi_ready, hd + 1)
                pool.tensor_tensor(acts[:, tiles, 1], y[:, tiles], acts[:, tiles, 0].bitcast(F32), ALU.subtract)\
                    .then_inc(y_lo_odd, 1)
            done_norms = []
            add_up(0, 1, 2)
            add_up(16, 1, 3)
            add_up(32, 2, 4)
            add_up(48, 1, 5)

        @block.vector
        def _(dve):
            steps = [0]

            def link(ins):
                steps[0] += 1
                ins.then_inc(dve_step, 1)
                dve.wait_ge(dve_step, steps[0])

            def split(n, r, turn):
                dve.wait_ge(hi_ready, n + 1)
                dve.tensor_tensor(w_lo[:, r], raw[:, r], w_hi[:, r].bitcast(F32), ALU.subtract).then_inc(lo_ready, 1)

            def add_halves(s, it, u, b):
                e = tile_no(s, it, u, b)
                dve.wait_ge(half_ready, e + 1)
                wait(dve, evict_done, e - 1)
                dve.tensor_tensor(total[:, b], ps[:, 2 * (u % 2) + b, 0:T], half[:, b], ALU.add).then_inc(sum_done, 1)
                dve.wait_ge(sum_done, e + 1)
                return e

            targets = {"qk": qk, "v": None, "og": h}

            def first(s, it, u, b):
                e, j, name = add_halves(s, it, u, b), tile_of(s, it, u, b), s.name
                if name == "v":
                    wait(dve, vt_done, j // 2)
                    dve.tensor_tensor(scaled[:, b], total[:, b], rs[:], ALU.mult).then_inc(evict_done, 1)
                elif name in targets:
                    t = targets[name]
                    flat = t[:] if name == "og" else t[:].rearrange("p a b t -> p (a b) t")
                    dve.tensor_tensor(flat[:, j], total[:, b], rs[:], ALU.mult).then_inc(evict_done, 1)
                elif in2_group(s, it, u) >= BB0 // 2:
                    c = j - BB0
                    dve.tensor_tensor(scaled[:, b], total[:, b], rs[:], ALU.mult).then_inc(evict_done, 1)
                    dve.wait_ge(evict_done, e + 1)
                    wait(dve, tile_ready, tiles_in("in2") + c - 1)
                    dve.wait_ge(conv_step, 4 * (c // 2) + 4)
                    dve.tensor_tensor(prod[:, b], scaled[:, b], proj[:, BC0 + c], ALU.mult).then_inc(prod_done, 1)
                elif name == "in2":
                    dve.tensor_tensor(proj[:, j], total[:, b], rs[:], ALU.mult).then_inc(evict_done, 1)
                elif hidden.get(name) == "swiglu" and u % 2 == 0:
                    dve.tensor_tensor(scaled[:, b], total[:, b], rs[:], ALU.mult).then_inc(evict_done, 1)
                elif hidden.get(name) == "swiglu":
                    dve.tensor_tensor(gate[:, b], total[:, b], rs[:], ALU.mult).then_inc(evict_done, 1)
                    dve.wait_ge(evict_done, e + 1)
                    dve.wait_ge(silu_done, prods[name] + j + 1)
                    wait(dve, tile_ready, tiles_in(name) + j - 1)
                    dve.tensor_tensor(prod[:, b], gate[:, b], act_gate[:, b], ALU.mult).then_inc(prod_done, 1)
                elif hidden.get(name) == "relu2":
                    dve.tensor_tensor(scaled[:, b], total[:, b], rs[:], ALU.mult).then_inc(evict_done, 1)
                    dve.wait_ge(evict_done, e + 1)
                    wait(dve, tile_ready, tiles_in(name) + j - 1)
                    dve.scalar_tensor_tensor(out=prod[:, b], in0=scaled[:, b], scalar=0.0, in1=scaled[:, b],
                                             op0=ALU.max, op1=ALU.mult).then_inc(prod_done, 1)
                elif name == "ple_gate":
                    dve.tensor_tensor(scaled[:, b], total[:, b], rs[:], ALU.mult).then_inc(evict_done, 1)
                elif name == "out2":
                    dve.scalar_tensor_tensor(out=scaled[:, b], in0=h[:, j], scalar=gains[:, 3, j],
                                             in1=rs_final[:], op0=ALU.mult, op1=ALU.mult).then_inc(h_done, 1)
                    dve.wait_ge(h_done, 16 + j + 1)
                    dve.tensor_tensor(h[:, j], scaled[:, b], total[:, b], ALU.add).then_inc(evict_done, 1)
                else:
                    dve.tensor_tensor(h[:, j], h[:, j], total[:, b], ALU.add).then_inc(evict_done, 1)

            def tiles_in(name):
                return tiles_before[name]

            def then(s, it, u, b):
                e, j = tile_no(s, it, u, b), tile_of(s, it, u, b)
                kind = hidden.get(s.name)
                if kind == "swiglu" and u % 2 == 0:
                    return
                if kind:
                    dve.wait_ge(x_hi_ready, tiles_in(s.name) + j + 1)
                    dve.tensor_tensor(acts[:, j, 1], prod[:, b], acts[:, j, 0].bitcast(F32), ALU.subtract)\
                        .then_inc(tile_ready, 1)
                elif s.name in residual:
                    dve.wait_ge(x_hi_ready, tiles_in(s.name) + j + 1)
                    dve.scalar_tensor_tensor(out=xs[:, j, 1], in0=h[:, j], scalar=gains[:, residual[s.name][1], j],
                                             in1=xs[:, j, 0].bitcast(F32), op0=ALU.mult, op1=ALU.subtract)\
                        .then_inc(tile_ready, 1)
                elif in2_group(s, it, u) >= BB0 // 2:
                    dve.wait_ge(x_hi_ready, tiles_in("in2") + j - BB0 + 1)
                    y = y_tile(4 + j - BB0)
                    dve.tensor_tensor(acts[:, y, 1], prod[:, b], acts[:, y, 0].bitcast(F32), ALU.subtract)\
                        .then_inc(tile_ready, 1)
                elif s.name == "ple_gate":
                    dve.wait_ge(silu_done, 44 + j + 1)
                    dve.tensor_tensor(prod[:, b], act_gate[:, b], ple_val[:, j], ALU.mult).then_inc(prod_done, 1)
                    dve.wait_ge(prod_done, 44 + j + 1)
                    dve.tensor_tensor(h[:, j], h[:, j], prod[:, b], ALU.add).then_inc(h_done, 1)

            def last(s, it, u, b):
                if s.name == "ple_gate":
                    j = tile_of(s, it, u, b)
                    dve.wait_ge(x_hi_ready, tiles_in(s.name) + j + 1)
                    dve.scalar_tensor_tensor(out=acts[:, j, 1], in0=h[:, j], scalar=gain_fa[:, j],
                                             in1=acts[:, j, 0].bitcast(F32), op0=ALU.mult, op1=ALU.subtract)\
                        .then_inc(tile_ready, 1)

            def finish(s, it, u, step):
                if step < 2:
                    first(s, it, u, step)
                else:
                    then(s, it, u, step - 2)
                if step == 3:
                    last(s, it, u, 0)
                    last(s, it, u, 1)

            def stage(name, before, extra=None):
                slots_loop(dve, st[name], split, finish, st[before] if before else None, extra)

            def newton(out_, r, x, tmp):
                link(dve.reciprocal(out_, r))
                link(dve.tensor_tensor(tmp, out_, out_, ALU.mult))
                link(dve.scalar_tensor_tensor(out=tmp, in0=tmp, scalar=-0.5, in1=x, op0=ALU.mult, op1=ALU.mult))
                link(dve.scalar_tensor_tensor(out=out_, in0=tmp, scalar=1.5, in1=out_, op0=ALU.add, op1=ALU.mult))

            def norm_begin(k):
                dve.wait_ge(norm_sum, k)
                dve.tensor_scalar(ms[:], ps[:, 4, 0:T], 1.0 / D, EPS, ALU.mult, ALU.add).then_inc(norm_ms, 1)

            def norm_end(k, dst):
                dve.wait_ge(norm_root, k)
                newton(dst, root[:], ms[:], newt[:])

            def norm_hook(k, sums=None):
                def go(u, kp):
                    if (u, kp) == (1, 1):
                        norm_begin(sums or k)
                    if (u, kp) == (1, 3):
                        norm_end(k, rs[:])
                return go

            dve.memset(root_tables[:, 0:1], 1.0).then_inc(place_set, 1)
            dve.wait_ge(gains_loaded, 16)
            link(dve.tensor_tensor(gain_fa[:], gains[:, 3], gains[:, 4], ALU.mult))
            for c in range(4):
                for j in range(4 * c, 4 * c + 4):
                    dve.wait_ge(x_hi_ready, j + 1)
                    dve.scalar_tensor_tensor(out=xs[:, j, 1], in0=h[:, j], scalar=gains[:, 0, j],
                                             in1=xs[:, j, 0].bitcast(F32), op0=ALU.mult, op1=ALU.subtract)\
                        .then_inc(tile_ready, 1)
                for r in (2 * c, 2 * c + 1):
                    split(r, r, 0)

            cumf = cum[:].rearrange("p a b t -> p (a b) t")
            bgf = b_gate[:].rearrange("p a b -> p (a b)")

            def during_qk(it, u, kp):
                if (it, u) == (0, 0) and kp < 4:
                    dve.wait_ge(x_sq, DT)
                    wait(dve, x_sq_sum, kp)
                    rest = DT >> (kp + 1)
                    dve.tensor_tensor(cumf[:, 0:rest], cumf[:, 0:rest], cumf[:, rest:2 * rest], ALU.add).then_inc(x_sq_sum, 1)
                if (it, u, kp) == (0, 1, 1):
                    norm_begin(1)
                if (it, u, kp) == (0, 1, 3):
                    norm_end(1, rs[:])
                if (it, u, kp) == (1, 0, 0):
                    dve.wait_ge(consts, 16 * N_CONST)
                if (it, u, kp) == (0, 1, 3):
                    dve.wait_ge(lr_half, 1)
                    link(dve.tensor_tensor(total[:, 0], ps[:, 5, 0:T], scaled[:, 0], ALU.add))
                    dve.tensor_tensor(lr_t[:], total[:, 0], rs[:], ALU.mult).then_inc(lr_ready, 1)
                    dve.wait_ge(lr_ready, 1)
                if it == 1 and kp < 4:
                    n = 4 * u + kp
                    dve.wait_ge(gk_done, n + 1)
                    for c in range(2):
                        ins = dve.tensor_scalar(cumf[:, 2 * n + c], ps[:, 4 + n % 4, c * T:(c + 1) * T],
                                                bgf[:, 2 * n + c:2 * n + c + 1], None, ALU.add)
                    ins.then_inc(gk_read, 1)
                if it == 2 and kp == 1:
                    dve.wait_ge(gk_read, 8)
                    dve.scalar_tensor_tensor(out=dec[:, u], in0=cum[:, u], scalar=-1.0, in1=cum[:, u], op0=ALU.mult,
                                             op1=ALU.max).then_inc(ls_step, 1)
                if it == 3 and kp == 0:
                    dve.wait_ge(ls_ready, u + 1)
                    link(dve.scalar_tensor_tensor(out=dec[:, u], in0=cum[:, u], scalar=0.0, in1=dec[:, u], op0=ALU.min,
                                                  op1=ALU.subtract))
                    if u == 0:
                        link(dve.memset(qk_dec[:, 0, 0], 1.0))
                    else:
                        link(dve.memset(cum[:, 1, :, 0:1], 0.0))
                if it == 3 and kp in (1, 2, 3, 7):
                    for c in range(2 * (min(kp, 4) - 1), 2 * min(kp, 4)):
                        if u == 0:
                            ins = dve.tensor_tensor_scan(cum[:, 0, c], qk_dec[:, 0, 0], dec[:, 0, c], 0.0, ALU.mult, ALU.add)
                        else:
                            ins = dve.tensor_tensor_scan(cum[:, 1, c, 1:T], qk_dec[:, 0, 0, 1:T], dec[:, 1, c, 0:T - 1],
                                                         0.0, ALU.mult, ALU.add)
                    if (u, kp) == (1, 7):
                        ins.then_inc(cum_ready, 1)
                        dve.wait_ge(cum_ready, 1)
                    else:
                        link(ins)

            def scores_out(lv):
                for hp in range(2):
                    dve.wait_ge(s_done, 2 * lv + hp + 1)
                    wait(dve, s_read, 2 * lv + hp)
                    for hh in range(2):
                        hd = 2 * hp + hh
                        src = ps[:, 4 + hp, hh * T:(hh + 1) * T].rearrange("p (a i) -> p a i", a=2)
                        if lv == 0:
                            ins = dve.tensor_scalar(a_t[:, hd, 0:4:3], src, 2.0, None, ALU.mult)
                        elif lv < len(LEVELS):
                            mask = masks[:, lv - 1:lv].bitcast(U32).broadcast_to([P, 2, P])
                            ins = dve.copy_predicated(a_t[:, hd, 0:4:3], mask, src)
                        else:
                            ins = dve.tensor_copy(a_t[:, hd, 1:3], src)
                    ins.then_inc(s_read, 1)

            def during_v_og(n, u, kp):
                size = LEVELS[n]
                f, b, dq = cut(cum[:, 0], size), cut(cum[:, 1], size), cut(dec[:, 0], size)
                ref_f, ref_b = references(f, b, size)
                if (u, kp) == (0, 0):
                    wait(dve, dec_ready, 2 * n)
                    dve.tensor_tensor(dq[:, :, 1], f[:, :, 1], ref_f, ALU.subtract)
                if (u, kp) == (0, 1):
                    dve.tensor_tensor(dq[:, :, 0], ref_b, b[:, :, 0], ALU.subtract).then_inc(q_arg, 1)
                if (u, kp) == (0, 7) and n:
                    scores_out(n)
                if u == 1 and kp in (0, 2):
                    part = kp // 2
                    if n == 0:
                        dve.wait_ge(evict_done, 2 * st["v"].group0)
                    dve.wait_ge(dec_exp, 2 * n + part + 1)
                    dve.tensor_tensor(qk_dec[:, part], qk[:, part], dec[:, part], ALU.mult).then_inc(dec_ready, 1)
                if (u, kp) == (1, 3) and n == 0:
                    scores_out(0)

            for it in range(4):
                slots_body(st["qk"], it, split, finish, None, lambda u, kp: during_qk(it, u, kp))
            for n in range(len(LEVELS)):
                name, before = ("v", "qk") if n < 4 else ("og", "v")
                slots_body(st[name], n % 4, split, finish, st[before], lambda u, kp: during_v_og(n, u, kp))
            s = st["ple_proj"]
            for r in range(RING):
                split(s.slot0 + r, r, s.slot0 // RING)
                if r == 0:
                    dve.wait_ge(p_hi, 1)
                    dve.tensor_tensor(p_split[:, :, 1], p_raw[:], p_split[:, :, 0].bitcast(F32), ALU.subtract)\
                        .then_inc(p_ready, 1)
                if r >= 4:
                    finish(st["og"], st["og"].iters - 1, 1, r - 4)
            scores_out(len(LEVELS))

            def ple_add(g):
                dve.wait_ge(half_ready, 2 * (s.group0 + g + 1))
                dve.tensor_tensor(ple_val[:, 2 * g:2 * g + 2], ps[:, 2 * (g % 2):2 * (g % 2) + 2, 0:T], half[:], ALU.add)\
                    .then_inc(sum_done, 2)

            for g in range(4):
                ple_add(g)
            o = qk_dec[:].rearrange("p a b t -> p (a b) t")
            dve.wait_ge(og_silu, 1)
            for n in range(8):
                dve.wait_ge(o_read, n + 1)
                for k in (2 * n, 2 * n + 1):
                    dve.scalar_tensor_tensor(out=o[:, k], in0=o[:, k], scalar=out_gain[:, k % DV_T:k % DV_T + 1],
                                             in1=h[:, k], op0=ALU.mult, op1=ALU.mult).then_inc(og_used, 1)
            ple_add(4)
            dve.wait_ge(norm_sum, 2)
            dve.tensor_scalar(small[:, 1, 0:8], ps[:, 6, 0:8], 1.0 / 512, EPS, ALU.mult, ALU.add).then_inc(norm_ms, 1)
            dve.wait_ge(norm_root, 2)
            newton(small[:, 0, 0:8], small[:, 2, 0:8], small[:, 1, 0:8], small[:, 3, 0:8])
            rh = small[:, 0, 0:8].rearrange("p (a b) -> p a b", b=1)
            dve.tensor_copy(rh_wide[:], rh.broadcast_to([P, 8, P])).then_inc(rh_ready, 1)

            def y_scaled(hd):
                tiles = slice(hd * DV_T, (hd + 1) * DV_T)
                r = ps[:, 4 + hd // 2, (hd % 2) * T:(hd % 2 + 1) * T].rearrange("p (a t) -> p a t", a=1)
                dve.tensor_tensor(o[:, tiles], o[:, tiles], r.broadcast_to([P, DV_T, T]), ALU.mult).then_inc(y_ready, 1)

            for g in (5, 6):
                ple_add(g)
            dve.wait_ge(og_used, DT)
            dve.wait_ge(rh_done, 1)
            y_scaled(0)

            def y_lo(u, kp):
                if u == 0 and kp < GLA_H:
                    tiles = slice(kp * DV_T, (kp + 1) * DV_T)
                    if kp % 2 == 0:
                        dve.wait_ge(y_hi_ready, kp + 1)
                        dve.tensor_tensor(acts[:, tiles, 1], o[:, tiles], acts[:, tiles, 0].bitcast(F32), ALU.subtract)\
                            .then_inc(y_lo_even, 1)
                    if kp + 1 < GLA_H:
                        y_scaled(kp + 1)
                if (u, kp) == (0, 0):
                    ple_add(7)
                    dve.wait_ge(sum_done, 2 * st["gla_out"].group0)
                    dve.memset(small[:, 5, 0:1], 0.0).then_inc(evict_done, DT)
                if (u, kp) == (1, 3):
                    dve.wait_ge(x_again, 16)

            stage("gla_out", None, y_lo)
            stage("ffn_in0", "gla_out", norm_hook(3))
            stage("ffn_out0", "ffn_in0")
            stage("ffn_in1", "ffn_out0")
            stage("ffn_out1", "ffn_in1")
            stage("ple_gate", "ffn_out1", norm_hook(4))

            def two_norms(w, kp):
                if (w, kp) == (1, 1):
                    dve.wait_ge(norm_sum, 5)
                    link(dve.tensor_scalar(rs_final[:], ps[:, 4, 0:T], 1.0 / D, EPS, ALU.mult, ALU.add))
                    link(dve.tensor_scalar(ms[:], rs_final[:], EPS, None, ALU.mult))
                    dve.scalar_tensor_tensor(out=ms[:], in0=ps[:, 4, T:2 * T], scalar=1.0 / D, in1=ms[:], op0=ALU.mult,
                                             op1=ALU.add).then_inc(norm_ms, 1)
                if (w, kp) == (1, 3):
                    norm_end(5, rs[:])
                if (w, kp) == (6, 1):
                    dve.tensor_copy(ms[:], rs_final[:]).then_inc(norm_ms, 1)
                if (w, kp) == (6, 3):
                    norm_end(6, rs_final[:])

            def score_out(hd):
                dve.wait_ge(sc_done, hd + 1)
                for tt in range(2):
                    i = 2 * hd + tt
                    dve.tensor_tensor_reduce(prob[:, hd, tt], ps[:, 4 + hd % 3, tt * T:(tt + 1) * T],
                                             amask[:, hd // 4, tt], 1.0, 2 * NEG, ALU.add, ALU.max,
                                             small[:, 0, i:i + 1]).then_inc(sc_read, 1)
                    dve.wait_ge(sc_read, i + 1)
                    dve.tensor_scalar(small[:, 1, i:i + 1], small[:, 0, i:i + 1], -1.0, None, ALU.mult).then_inc(nm_ready, 1)

            def qk_scaled(n):
                dve.wait_ge(rb_done, n + 1)
                for j in (2 * n, 2 * n + 1):
                    dve.scalar_tensor_tensor(out=proj[:, Q0 + j], in0=proj[:, Q0 + j], scalar=qk_gain[:, j // 6:j // 6 + 1],
                                             in1=ps[:, 4 + n % 3, (j % 2) * T:(j % 2 + 1) * T], op0=ALU.mult,
                                             op1=ALU.mult).then_inc(qn_ready, 1)

            mx, den, lse, wt, s5 = (small[:, k, 0:24] for k in (0, 2, 3, 4, 5))
            g3 = lse.rearrange("p (g x) -> p g x", g=3)
            w3 = wt.rearrange("p (g x) -> p g x", g=3)
            d3 = den.rearrange("p (g x) -> p g x", g=3)

            def pattern_logits():
                dve.wait_ge(ln_ready, 1)
                link(dve.tensor_tensor(lse, lse, mx, ALU.add))
                link(dve.tensor_tensor(s5[:, 0:8], g3[:, 0], g3[:, 1], ALU.max))
                link(dve.tensor_tensor(s5[:, 0:8], s5[:, 0:8], g3[:, 2], ALU.max))
                for g in range(3):
                    ins = dve.tensor_tensor(w3[:, g], g3[:, g], s5[:, 0:8], ALU.subtract)
                ins.then_inc(lm_ready, 1)

            def pattern_shares():
                dve.wait_ge(wexp, 1)
                link(dve.tensor_tensor(s5[:, 8:16], w3[:, 0], w3[:, 1], ALU.add))
                link(dve.tensor_tensor(s5[:, 8:16], s5[:, 8:16], w3[:, 2], ALU.add))
                for g in range(3):
                    ins = dve.tensor_tensor(d3[:, g], d3[:, g], s5[:, 8:16], ALU.mult)
                link(ins)
                link(dve.reciprocal(den, den))
                link(dve.tensor_tensor(wt, wt, den, ALU.mult))

            def weights(first_i, last_i):
                for i in range(first_i, last_i):
                    dve.tensor_scalar(prob[:, i // 2, i % 2], prob[:, i // 2, i % 2], wt[:, i:i + 1], None, ALU.mult)\
                        .then_inc(pw_ready, 1)

            def gated(n):
                dve.wait_ge(ya_done, n + 1)
                for hf in range(2):
                    rows = slice(HD * hf, HD * hf + HD)
                    src = ps[rows, 7].rearrange("p (c a i) -> p c a i", c=2, a=2)[:, :, hf]
                    ins = dve.tensor_tensor(proj[rows, AV0 + n].rearrange("p (c i) -> p c i", c=2), src,
                                            bias_a[rows, n:n + 1].broadcast_to([HD, 2, P]), ALU.add)
                ins.then_inc(ya_sum, 1)
                dve.wait_ge(ya_sum, n + 1)
                dve.tensor_tensor(proj[:, AU0 + n], proj[:, AU0 + n], proj[:, AV0 + n], ALU.mult).then_inc(ya_ready, 1)

            def convolution(m, step):
                for j in (2 * m, 2 * m + 1):
                    z, c = proj[:, BX0 + j], proj[:, BC0 + j]
                    if step == 0:
                        ins = dve.tensor_tensor(z, z, c, ALU.mult)
                    elif step == 1:
                        ins = dve.tensor_scalar(c, z, conv_w[:, j, 2:3], None, ALU.mult)
                    else:
                        lag = step - 1
                        ins = dve.scalar_tensor_tensor(out=c[:, lag:T], in0=z[:, 0:T - lag],
                                                       scalar=conv_w[:, j, 2 - lag:3 - lag],
                                                       in1=c[:, lag:T], op0=ALU.mult, op1=ALU.add)
                ins.then_inc(conv_step, 1)

            def yc_lo_part(j):
                dve.wait_ge(yc_hi, j + 1)
                y = y_tile(10 + j)
                dve.tensor_tensor(acts[:, y, 1], ps[:, 6, 0:T], acts[:, y, 0].bitcast(F32), ALU.subtract).then_inc(yc_lo, 1)

            def during_in2(w, kp):
                two_norms(w, kp)
                if (w, kp) == (6, 0):
                    dve.wait_ge(late_consts, 64)
                    dve.tensor_tensor(sgu_wt[:], sgu_wt[:], causal3(), ALU.mult).then_inc(wm_ready, 1)
                if (w, kp) == (7, 7):
                    dve.wait_ge(hs_done, 1)
                    dve.tensor_scalar(small[:, 1], ps[:, 4, 0:48], 1.0 / HD, EPS, ALU.mult, ALU.add).then_inc(norm_ms, 1)
                if (w, kp) == (8, 1):
                    dve.wait_ge(norm_root, 7)
                    newton(small[:, 0], small[:, 2], small[:, 1], small[:, 3])
                    link(dve.tensor_scalar(qk_gain[:, 0:1], qk_gain[:, 0:1], HD ** -0.5, None, ALU.mult))
                if w == 8 and kp in (1, 2):
                    rstd = small[:, 0, 24 * (kp - 1):24 * kp].rearrange("p (h o) -> p h o", o=1)
                    ins = dve.tensor_copy(r_wide[:, kp - 1], rstd.broadcast_to([P, 24, HD]))
                    if kp == 2:
                        ins.then_inc(hs_ready, 1)
                if w in (8, 9) and kp == 7:
                    qk_scaled(3 * (w - 8))
                if w in (9, 10) and kp < 2:
                    qk_scaled(3 * (w - 9) + 1 + kp)
                if 10 <= w <= 13 and kp == 7:
                    score_out(3 * (w - 10))
                if 11 <= w <= 14 and kp < 2:
                    score_out(3 * (w - 11) + 1 + kp)
                if (w, kp) == (14, 6):
                    pattern_logits()
                if (w, kp) == (15, 1):
                    pattern_shares()
                if w == 15 and kp in (2, 3):
                    weights(4 * (kp - 2), 4 * (kp - 1))
                if w in (16, 17) and kp < 4:
                    weights(8 * (w - 15) + 2 * kp, 8 * (w - 15) + 2 * kp + 2)
                if 14 <= w <= 17 and kp == 7:
                    gated(w - 14)
                if 15 <= w <= 18 and kp == 3:
                    n = w - 15
                    dve.wait_ge(ya_hi, n + 1)
                    dve.tensor_tensor(acts[:, y_tile(n), 1], proj[:, AU0 + n], acts[:, y_tile(n), 0].bitcast(F32),
                                      ALU.subtract).then_inc(ya_lo, 1)
                if 18 <= w <= 20 and kp < 4:
                    if kp:
                        dve.wait_ge(conv_step, 4 * (w - 18) + kp)
                    else:
                        dve.wait_ge(evict_done, 2 * st["in2"].group0 + BX0 + 2 * (w - 18) + 2)
                    convolution(w - 18, kp)
                if 18 <= w <= 21 and kp == 0:
                    yc_lo_part(w - 18)

            def last_yc(u, kp):
                if (u, kp) == (0, 0):
                    yc_lo_part(4)
                if (u, kp) == (0, 7):
                    yc_lo_part(5)

            s = st["in2"]
            through_in2(dve, lambda it: slots_body(s, it, split, finish, st["ple_gate"],
                        (lambda u, kp: during_in2(2 * it + u, kp)) if isinstance(it, int) else None))
            stage("out2", "in2", last_yc)
            stage("mlp_in0", "out2", norm_hook(8, 6))
            stage("mlp_out0", "mlp_in0")
            stage("mlp_in1", "mlp_out0")
            stage("mlp_out1", "mlp_in1")
            for step in range(2):
                finish(st["mlp_out1"], st["mlp_out1"].iters - 1, 1, step)


def _slots(w):
    k, n = w.shape
    return w.reshape(k // 256, 2, P, n // T, T).transpose(3, 0, 2, 1, 4).reshape(-1, P, 2, T)


def _features(x):
    return x.T.reshape(-1, P, x.shape[0]).transpose(1, 0, 2)


def _per_feature(v):
    return v.reshape(-1, P).T


def lay_out(inputs):
    g = {k: np.asarray(v) for k, v in inputs.items()}
    f = np.float32
    w_in = g["gla_w_in"][0]
    lr = np.zeros((D, T), f)
    lr[:, 0:32] = w_in[:, 6144:6176]
    gate, up = g["ffn_w_in"][0][:, :5632], g["ffn_w_in"][0][:, 5632:]
    parts = [_slots(lr), _slots(w_in[:, 0:6144]), _slots(g["ple_w_proj"][0]), _slots(g["gla_w_out"][0])]
    at = 0
    for k in FFN_HALVES:
        cols = slice(at, at + k * P)
        pair = np.stack([gate[:, cols].reshape(D, k // 2, T), up[:, cols].reshape(D, k // 2, T)], 2)
        parts += [_slots(pair.reshape(D, k * T)), _slots(g["ffn_w_out"][0][cols])]
        at += k * P
    parts += [_slots(g["ple_w_gate"][0])]
    w2 = g["w_in_2"][0]
    e = np.cumsum([0, 512, 512, 768, 768, 768, 768, 768, 768])
    c = [w2[:, e[i]:e[i + 1]] for i in range(8)]
    parts += [_slots(np.concatenate([c[5], c[6], c[7], c[1], c[0], c[3], c[4], c[2]], 1)), 
              _slots(g["w_out_2"][0].reshape(DT, P, D)[OUT2_ORDER].reshape(D, D))]
    for n in range(2):
        cols = slice(n * MLP_HALF * P, (n + 1) * MLP_HALF * P)
        parts += [_slots(g["w_mlp_in_2"][0][:, cols]), _slots(g["w_mlp_out_2"][0][cols])]
    stream = np.concatenate(parts)
    assert len(stream) == N_SLOTS
    stream = np.ascontiguousarray(stream.reshape(N_SLOTS // 2, 2, P, 2, T).transpose(0, 2, 1, 3, 4))
    w_up = np.zeros((32, 2, GLA_U, P), f)
    for z in range(2):
        w_up[16 * z:16 * z + 16, z] = g["gla_w_gate_up"][0, z].reshape(16, GLA_U, P)
    i = np.arange(P)
    masks = np.stack([((i[:, None] // s) ^ (i[None, :] // s)) == 1 for s in LEVELS[:-1]], 1).astype(f)
    t = (np.arange(2)[None, :, None] * P + i[:, None, None])
    key = np.arange(T)[None, None, :]
    back = t - key
    ok = [(back >= 0) & (back <= 128), (back >= 0) & (back % 4 == 0), (back >= 0) & (back % 16 == 0)]
    amask = np.stack([np.where(m, 0.0, NEG) for m in ok], 1).astype(f)
    hp = np.zeros((P, 2), f)
    hp[:HD, 0] = 1
    hp[HD:, 1] = 1
    sgu_b = g["sgu_b_2"][0].reshape(4, 2, P)
    arrays = {
        "stream": stream,
        "x": _features(g["x"][0]),
        "p": _features(g["p"][0, 0]),
        "gains": np.stack([_per_feature(g[n].reshape(-1)) for n in
                           ("mixer_norm", "ffn_norm", "ple_norm", "final_norm", "attn_norm_2", "mlp_norm_2")], 1)[..., None],
        "ones": np.ones((P, P), f), "ident": np.eye(P, dtype=f),
        "b_gate": g["gla_b_gate"][0].reshape(2, GLA_U, P).transpose(2, 0, 1),
        "out_gain": _per_feature(g["gla_out_norm"][0]),
        "masks": masks, "w_up": w_up,
        "causal": (i[:, None] <= i[None, :]).astype(f), "head_pair": hp,
        "qk_gain": np.stack([np.tile(g["q_norm_2"][0], 2), np.tile(g["k_norm_2"][0], 2)], 1),
        "conv_w": g["conv_w_2"][0].reshape(3, 6, P).transpose(2, 1, 0),
        "amask": amask,
        "bias_a": np.repeat(sgu_b.transpose(1, 0, 2), HD, 0),
        "sgu_wt": g["sgu_w_2"][0].transpose(2, 0, 1),
    }
    return {k: np.ascontiguousarray(v) for k, v in arrays.items()}


def kernel(**inputs):
    import concourse.bacc as bacc
    from concourse.bass_utils import run_bass_kernel_spmd

    arrays = lay_out(inputs)
    nc = bacc.Bacc("TRN2", target_bir_lowering=False, num_devices=1)
    aps = {k: nc.dram_tensor(f"in_{k}", v.shape, mybir.dt.from_np(v.dtype), kind="ExternalInput").ap()
           for k, v in arrays.items()}
    out = nc.dram_tensor("out_t", (P, DT, T), F32, kind="ExternalOutput").ap()
    build(nc, aps, out)
    r = run_bass_kernel_spmd(nc, [{f"in_{k}": v for k, v in arrays.items()}], core_ids=[0])
    return r.results[0]["out_t"].transpose(2, 1, 0).reshape(1, T, D)
```
